# Optimizing a Trainium2 kernel written in Bass

```python
import jax, jax.numpy as jnp
from jax import lax
import numpy as np

D_MODEL = 1024
BATCH = 1
SEQ = 512
DEPTH = 1
DEC_BATCH = 1
DEC_SEQ = 64
PAST_LEN = 256

CHUNK = 64
HEAD_DIM = 64
A_HEADS = 8
A_KV_HEADS = 2
A_GROUP = A_HEADS // A_KV_HEADS
WINDOW = 128
WIN_CHUNKS = WINDOW // CHUNK
B_HEADS = 8
FOX_BLOCK = 128
ROPE_THETA = 10000.0
ATTN_SCALE = HEAD_DIM ** -0.5
A_Q = A_HEADS * HEAD_DIM
A_KV = A_KV_HEADS * HEAD_DIM
B_W = B_HEADS * HEAD_DIM
IN_COLS = A_Q + 2 * A_KV + 3 * B_W + B_HEADS + 2 * D_MODEL
PEER_HEADS = 8
N_SUBKEYS = 128
N_EXPERTS = N_SUBKEYS * N_SUBKEYS
PEER_TOPK = 16
PEER_KEY_DIM = 256
PEER_HALF = PEER_KEY_DIM // 2
PEER_BLOCK = 128
RMS_EPS = 1e-6
FGATE_BIAS_INIT = 3.0

kernel_name = 'hybrid_swa_fox_peer_stream_step'

def rms_norm(x, g):
    xf = x.astype(jnp.float32)
    y = xf * lax.rsqrt(jnp.mean(xf * xf, axis=-1, keepdims=True) + RMS_EPS)
    return (y * g.astype(jnp.float32)).astype(x.dtype)

def rope(x, pos):
    half = HEAD_DIM // 2
    inv_freq = ROPE_THETA ** (-jnp.arange(half, dtype=jnp.float32) / half)
    ang = pos.astype(jnp.float32)[:, None] * inv_freq[None, :]
    cos = jnp.cos(ang)[None, :, None, :]
    sin = jnp.sin(ang)[None, :, None, :]
    xf = x.astype(jnp.float32)
    x1, x2 = xf[..., :half], xf[..., half:]
    return jnp.concatenate([x1 * cos - x2 * sin, x2 * cos + x1 * sin], axis=-1).astype(x.dtype)

def project_in(h, w_in, b_fgate):
    B, T, _ = h.shape
    p = jnp.einsum('btd,dc->btc', h, w_in)
    o1 = A_Q
    o2 = o1 + A_KV
    o3 = o2 + A_KV
    o4 = o3 + B_W
    o5 = o4 + B_W
    o6 = o5 + B_W
    o7 = o6 + B_HEADS
    o8 = o7 + D_MODEL
    qa, ka, va, qb, kb, vb, fraw, ga, gb = jnp.split(p, [o1, o2, o3, o4, o5, o6, o7, o8], axis=-1)
    qa = qa.reshape(B, T, A_HEADS, HEAD_DIM)
    ka = ka.reshape(B, T, A_KV_HEADS, HEAD_DIM)
    va = va.reshape(B, T, A_KV_HEADS, HEAD_DIM)
    qb = qb.reshape(B, T, B_HEADS, HEAD_DIM)
    kb = kb.reshape(B, T, B_HEADS, HEAD_DIM)
    vb = vb.reshape(B, T, B_HEADS, HEAD_DIM)
    logf = jax.nn.log_sigmoid(fraw.astype(jnp.float32) + b_fgate.astype(jnp.float32))
    return qa, ka, va, qb, kb, vb, logf, ga, gb

def with_sink(logits, sink):
    sink = jnp.broadcast_to(sink.astype(jnp.float32), logits.shape[:-1] + (1,))
    p = jax.nn.softmax(jnp.concatenate([logits, sink], axis=-1), axis=-1)
    return p[..., :-1]

def swa_prompt(q, k, v, sinks):
    B, S = q.shape[0], q.shape[1]
    nc = S // CHUNK
    padw = ((0, 0), (WINDOW, 0), (0, 0), (0, 0))
    kp = jnp.pad(k, padw).reshape(B, nc + WIN_CHUNKS, CHUNK, A_KV_HEADS, HEAD_DIM)
    vp = jnp.pad(v, padw).reshape(B, nc + WIN_CHUNKS, CHUNK, A_KV_HEADS, HEAD_DIM)
    kband = jnp.concatenate([kp[:, i:i + nc] for i in range(WIN_CHUNKS + 1)], axis=2)
    vband = jnp.concatenate([vp[:, i:i + nc] for i in range(WIN_CHUNKS + 1)], axis=2)
    key_pos = jnp.arange(nc)[:, None] * CHUNK - WINDOW + jnp.arange((WIN_CHUNKS + 1) * CHUNK)[None, :]
    valid = (key_pos >= 0)[None, :, None, None, None, :]
    qg = q.reshape(B, nc, CHUNK, A_KV_HEADS, A_GROUP, HEAD_DIM)
    s = jnp.einsum('bcqkgd,bcskd->bckgqs', qg, kband, preferred_element_type=jnp.float32) * ATTN_SCALE
    s = jnp.where(valid, s, -jnp.inf)
    p = with_sink(s, sinks.reshape(1, 1, A_KV_HEADS, A_GROUP, 1, 1))
    o = jnp.einsum('bckgqs,bcskd->bcqkgd', p.astype(v.dtype), vband)
    return o.reshape(B, S, A_Q)

def swa_step(q, k_new, v_new, cache_k, cache_v, sinks):
    Bd, T = q.shape[0], q.shape[1]
    k = jnp.concatenate([cache_k.astype(k_new.dtype), k_new], axis=1)
    v = jnp.concatenate([cache_v.astype(v_new.dtype), v_new], axis=1)
    qg = q.reshape(Bd, T, A_KV_HEADS, A_GROUP, HEAD_DIM)
    s = jnp.einsum('btkgd,bskd->bkgts', qg, k, preferred_element_type=jnp.float32) * ATTN_SCALE
    p = with_sink(s, sinks.reshape(1, A_KV_HEADS, A_GROUP, 1, 1))
    o = jnp.einsum('bkgts,bskd->btkgd', p.astype(v.dtype), v).reshape(Bd, T, A_Q)
    return o, k[:, -WINDOW:], v[:, -WINDOW:]

def fox_prompt(q, k, v, logf):
    B, S = q.shape[0], q.shape[1]
    nb = S // FOX_BLOCK
    Ft = jnp.cumsum(logf, axis=1).transpose(0, 2, 1)
    qb = q.reshape(B, nb, FOX_BLOCK, B_HEADS, HEAD_DIM).transpose(1, 0, 2, 3, 4)
    Fqb = Ft.reshape(B, B_HEADS, nb, FOX_BLOCK).transpose(2, 0, 1, 3)
    kpos = jnp.arange(S)

    def block(args):
        i, qi, Fi = args
        s = jnp.einsum('bqhd,bshd->bhqs', qi, k, preferred_element_type=jnp.float32) * ATTN_SCALE
        s = s + Fi[..., None] - Ft[:, :, None, :]
        qpos = i * FOX_BLOCK + jnp.arange(FOX_BLOCK)
        s = jnp.where(kpos[None, :] <= qpos[:, None], s, -jnp.inf)
        p = jax.nn.softmax(s, axis=-1)
        return jnp.einsum('bhqs,bshd->bqhd', p.astype(v.dtype), v)

    o = lax.map(block, (jnp.arange(nb), qb, Fqb))
    return o.transpose(1, 0, 2, 3, 4).reshape(B, S, B_W)

def fox_step(q, k_new, v_new, logf_new, cache_k, cache_v, cache_logf):
    Bd, T = q.shape[0], q.shape[1]
    P = cache_k.shape[1]
    k = jnp.concatenate([cache_k.astype(k_new.dtype), k_new], axis=1)
    v = jnp.concatenate([cache_v.astype(v_new.dtype), v_new], axis=1)
    lf = jnp.concatenate([cache_logf.astype(jnp.float32), logf_new], axis=1)
    Ft = jnp.cumsum(lf, axis=1).transpose(0, 2, 1)
    Fq = Ft[:, :, P:]
    s = jnp.einsum('bthd,bshd->bhts', q, k, preferred_element_type=jnp.float32) * ATTN_SCALE
    s = s + Fq[..., None] - Ft[:, :, None, :]
    mask = jnp.arange(P + T)[None, :] <= (P + jnp.arange(T))[:, None]
    s = jnp.where(mask, s, -jnp.inf)
    p = jax.nn.softmax(s, axis=-1)
    o = jnp.einsum('bhts,bshd->bthd', p.astype(v.dtype), v)
    return o.reshape(Bd, T, B_W)

def merge_out(ya, yb, ga, gb, w_a_out, w_b_out, w_out):
    za = jnp.einsum('btc,cd->btd', ya, w_a_out)
    zb = jnp.einsum('btc,cd->btd', yb, w_b_out)
    mixed = jax.nn.sigmoid(ga) * za + jax.nn.sigmoid(gb) * zb
    return jnp.einsum('btd,de->bte', mixed, w_out)

def peer_ffn(h, w_pq, sub_keys, u, v):
    B, T, D = h.shape
    n = B * T
    x = h.reshape(n, D)
    q = jnp.einsum('nd,dk->nk', x, w_pq).reshape(n, PEER_HEADS, 2, PEER_HALF)
    s = jnp.einsum('nhpd,hpkd->nhpk', q, sub_keys, preferred_element_type=jnp.float32)
    s_top, i_top = lax.top_k(s, PEER_TOPK)
    cand = s_top[:, :, 0, :, None] + s_top[:, :, 1, None, :]
    cand_idx = i_top[:, :, 0, :, None] * N_SUBKEYS + i_top[:, :, 1, None, :]
    best, sel = lax.top_k(cand.reshape(n, PEER_HEADS, PEER_TOPK * PEER_TOPK), PEER_TOPK)
    expert = jnp.take_along_axis(cand_idx.reshape(n, PEER_HEADS, -1), sel, axis=-1)
    gate = jax.nn.softmax(best, axis=-1)
    expert = expert.reshape(n, PEER_HEADS * PEER_TOPK)
    gate = gate.reshape(n, PEER_HEADS * PEER_TOPK).astype(h.dtype)
    npad = (-n) % PEER_BLOCK
    xp = jnp.pad(x, ((0, npad), (0, 0))).reshape(-1, PEER_BLOCK, D)
    ep = jnp.pad(expert, ((0, npad), (0, 0))).reshape(-1, PEER_BLOCK, PEER_HEADS * PEER_TOPK)
    gp = jnp.pad(gate, ((0, npad), (0, 0))).reshape(-1, PEER_BLOCK, PEER_HEADS * PEER_TOPK)

    def block(args):
        xb, eb, gb = args
        a = jnp.einsum('nd,ned->ne', xb, jnp.take(u, eb, axis=0))
        act = jax.nn.gelu(a, approximate=False) * gb
        return jnp.einsum('ne,ned->nd', act, jnp.take(v, eb, axis=0))

    out = lax.map(block, (xp, ep, gp)).reshape(-1, D)[:n]
    return out.reshape(B, T, D)

def layer_prompt(x, g_mix, w_in, b_fgate, sinks, w_a_out, w_b_out, w_out, g_ffn, w_pq, sub_keys, u, v):
    S = x.shape[1]
    pos = jnp.arange(S, dtype=jnp.int32)
    h = rms_norm(x, g_mix)
    qa, ka, va, qb, kb, vb, logf, ga, gb = project_in(h, w_in, b_fgate)
    qa = rope(qa, pos)
    ka = rope(ka, pos)
    ya = swa_prompt(qa, ka, va, sinks)
    yb = fox_prompt(qb, kb, vb, logf)
    x = x + merge_out(ya, yb, ga, gb, w_a_out, w_b_out, w_out)
    x = x + peer_ffn(rms_norm(x, g_ffn), w_pq, sub_keys, u, v)
    return x, ka[:, -WINDOW:], va[:, -WINDOW:], kb, vb, logf

def layer_step(x, c_swa_k, c_swa_v, c_fox_k, c_fox_v, c_fox_logf, g_mix, w_in, b_fgate, sinks,
               w_a_out, w_b_out, w_out, g_ffn, w_pq, sub_keys, u, v):
    T = x.shape[1]
    P = c_fox_k.shape[1]
    pos = P + jnp.arange(T, dtype=jnp.int32)
    h = rms_norm(x, g_mix)
    qa, ka, va, qb, kb, vb, logf, ga, gb = project_in(h, w_in, b_fgate)
    qa = rope(qa, pos)
    ka = rope(ka, pos)
    ya, nk, nv = swa_step(qa, ka, va, c_swa_k, c_swa_v, sinks)
    yb = fox_step(qb, kb, vb, logf, c_fox_k, c_fox_v, c_fox_logf)
    x = x + merge_out(ya, yb, ga, gb, w_a_out, w_b_out, w_out)
    x = x + peer_ffn(rms_norm(x, g_ffn), w_pq, sub_keys, u, v)
    return x, nk, nv, kb, vb, logf

def setup_inputs(seed: int = 0) -> dict:
    key = jax.random.key(seed)
    ks = jax.random.split(key, 20)
    f32 = jnp.float32

    def nrm(k, shape, scale):
        return jax.random.normal(k, shape, f32) * scale

    swa_rows = min(WINDOW, PAST_LEN)
    return {
        'x_prompt': nrm(ks[0], (BATCH, SEQ, D_MODEL), 1.0),
        'x_sample': nrm(ks[1], (DEC_BATCH, DEC_SEQ, D_MODEL), 1.0),
        'cache_swa_k': nrm(ks[2], (DEPTH, DEC_BATCH, swa_rows, A_KV_HEADS, HEAD_DIM), 1.0),
        'cache_swa_v': nrm(ks[3], (DEPTH, DEC_BATCH, swa_rows, A_KV_HEADS, HEAD_DIM), 1.0),
        'cache_fox_k': nrm(ks[4], (DEPTH, DEC_BATCH, PAST_LEN, B_HEADS, HEAD_DIM), 1.0),
        'cache_fox_v': nrm(ks[5], (DEPTH, DEC_BATCH, PAST_LEN, B_HEADS, HEAD_DIM), 1.0),
        'cache_fox_logf': jax.nn.log_sigmoid(FGATE_BIAS_INIT + nrm(ks[6], (DEPTH, DEC_BATCH, PAST_LEN, B_HEADS), 0.5)),
        'g_mix': 1.0 + nrm(ks[7], (DEPTH, D_MODEL), 0.02),
        'w_in': nrm(ks[8], (DEPTH, D_MODEL, IN_COLS), D_MODEL ** -0.5),
        'b_fgate': FGATE_BIAS_INIT + nrm(ks[9], (DEPTH, B_HEADS), 0.1),
        'sinks': nrm(ks[10], (DEPTH, A_HEADS), 0.5),
        'w_a_out': nrm(ks[11], (DEPTH, A_Q, D_MODEL), A_Q ** -0.5),
        'w_b_out': nrm(ks[12], (DEPTH, B_W, D_MODEL), B_W ** -0.5),
        'w_out': nrm(ks[13], (DEPTH, D_MODEL, D_MODEL), D_MODEL ** -0.5),
        'g_ffn': 1.0 + nrm(ks[14], (DEPTH, D_MODEL), 0.02),
        'w_pq': nrm(ks[15], (DEPTH, D_MODEL, PEER_HEADS * PEER_KEY_DIM), D_MODEL ** -0.5),
        'peer_sub_keys': nrm(ks[16], (DEPTH, PEER_HEADS, 2, N_SUBKEYS, PEER_HALF), PEER_HALF ** -0.5),
        'peer_u': nrm(ks[17], (DEPTH, N_EXPERTS, D_MODEL), D_MODEL ** -0.5),
        'peer_v': nrm(ks[18], (DEPTH, N_EXPERTS, D_MODEL), 0.2),
        'g_final': 1.0 + nrm(ks[19], (D_MODEL,), 0.02),
    }

def reference(x_prompt, x_sample, cache_swa_k, cache_swa_v, cache_fox_k, cache_fox_v, cache_fox_logf,
              g_mix, w_in, b_fgate, sinks, w_a_out, w_b_out, w_out, g_ffn, w_pq, peer_sub_keys,
              peer_u, peer_v, g_final):
    xp, xs = x_prompt, x_sample
    p_swa_k, p_swa_v, p_fox_k, p_fox_v, p_fox_lf = [], [], [], [], []
    s_swa_k, s_swa_v, s_fox_k, s_fox_v, s_fox_lf = [], [], [], [], []
    for l in range(DEPTH):
        xp, a, b, c, d, e = layer_prompt(xp, g_mix[l], w_in[l], b_fgate[l], sinks[l], w_a_out[l], w_b_out[l],
                                         w_out[l], g_ffn[l], w_pq[l], peer_sub_keys[l], peer_u[l], peer_v[l])
        p_swa_k.append(a); p_swa_v.append(b); p_fox_k.append(c); p_fox_v.append(d); p_fox_lf.append(e)
        xs, a, b, c, d, e = layer_step(xs, cache_swa_k[l], cache_swa_v[l], cache_fox_k[l], cache_fox_v[l],
                                       cache_fox_logf[l], g_mix[l], w_in[l], b_fgate[l], sinks[l], w_a_out[l],
                                       w_b_out[l], w_out[l], g_ffn[l], w_pq[l], peer_sub_keys[l], peer_u[l], peer_v[l])
        s_swa_k.append(a); s_swa_v.append(b); s_fox_k.append(c); s_fox_v.append(d); s_fox_lf.append(e)
    y_prompt = rms_norm(xp, g_final)
    y_sample = rms_norm(xs, g_final)
    return (y_prompt, y_sample,
            jnp.stack(p_swa_k), jnp.stack(p_swa_v), jnp.stack(p_fox_k), jnp.stack(p_fox_v), jnp.stack(p_fox_lf),
            jnp.stack(s_swa_k), jnp.stack(s_swa_v), jnp.stack(s_fox_k), jnp.stack(s_fox_v), jnp.stack(s_fox_lf))


_drawn_inputs = setup_inputs


def setup_inputs(seed=0):
    import zlib

    import numpy as np

    out = dict(_drawn_inputs(seed))
    spreads = {}
    factors = {'cache_fox_logf': 44.352, 'g_mix': 2.846, 'sinks': 64.0, 'g_ffn': 11.28, 'g_final': 7.998}
    for name, (base, spread) in spreads.items():
        noise = np.random.default_rng([zlib.crc32(name.encode()), seed]).standard_normal(out[name].shape)
        drawn = base * np.exp(spread * noise) if base else spread * noise
        out[name] = __import__('jax').numpy.asarray(drawn.astype(out[name].dtype))
    for name, factor in factors.items():
        out[name] = (out[name] * factor).astype(out[name].dtype)
    return out
```

```python
from contextlib import ExitStack

import numpy as np

import concourse.bass as bass
from concourse import mybir

ALU = mybir.AluOpType
ACT = mybir.ActivationFunctionType
AX_X = mybir.AxisListType.X
F32 = mybir.dt.float32
U32 = mybir.dt.uint32

P = 128
D = 1024
KC = D // P
SEQ, DEC, PAST = 512, 64, 256
HD = 64
HEADS = 8
KV = 2
GRP = HEADS // KV
WINDOW = 128
SCALE = HD ** -0.5
EPS = 1e-6
MASKED = -1e30
REPLACED = -3e38
TILES = 5
ROWS = [P, P, P, P, DEC]
PART = {"A": (0, 1), "B": (2, 3, 4)}
TOKENS = {"A": 256, "B": 320}
TOPK = 16
NSUB = 128
GROUP = TOPK
RING = 8
DIAGS = 4
GROUPS_A = 2 * HEADS
GROUPS = GROUPS_A + 2 * HEADS + HEADS // 2
UNROLLED = 22
PROJ = ("qa", "kvf", "qb", "kb", "vb")
PROJ_COLS = {"qa": 512, "kvf": 264, "qb": 512, "kb": 512, "vb": 512}
STAGED = ("qa", "kvf", "qb", "kb")
STAGES = 4
BANKS = 4
TRI = 896
C_IDENT, C_CAUSAL, C_FOLD, C_COS, C_SIN, C_IOTA, C_END = 0, 128, 256, 512, 672, 832, 848


def part_of(t):
    return "A" if t in PART["A"] else "B"


def column_of(t):
    return P * (t - PART[part_of(t)][0])


def group_place(g):
    if g < GROUPS_A:
        return g % 2, g // 2
    n = g - GROUPS_A
    return (2 + n // HEADS, n % HEADS) if n < 2 * HEADS else (4, 2 * (n - 2 * HEADS))


def branches(part):
    return [(t, br) for t in PART[part] for br in ("swa", "fox")]


def units(part):
    return [(t, br, h) for t, br in branches(part) for h in range(HEADS)]


def branch_number(t, br):
    return 2 * t + (br == "fox")


def unit_number(t, br, h):
    return branch_number(t, br) * HEADS + h


def attention_items(part):
    n = len(units(part))
    out = []
    for v in range(n + 2):
        out.append((("att", part, v), 1.0))
        if v >= 9 and (v - 9) % 8 == 0:
            out.append((("ytr",) + branches(part)[(v - 9) // 8], 1.0))
    return out


def merge_items(part):
    n = TOKENS[part]
    us = n * 4 / 2400
    out = [(("gate", part, m, w), us * (KC if w < 2 else KC // 2)) for m in range(KC) for w in range(4)]
    for q in range(4):
        for t in PART[part]:
            out.append((("wout", part, q, t), KC * 256 * 4 / 2400))
            if q == 3:
                out.append((("norm", 5 + t), 2.0))
    return out


def plan():
    before = [("norm", 0), ("norm", 1)]
    waiting = None
    for c in PROJ:
        for t in range(TILES):
            before.append(("proj", c, t))
            if waiting:
                before.append(("tr",) + waiting)
            waiting = (c, t) if c in STAGED else None
            if c == "qa" and t < 3:
                before.append(("norm", t + 2))
            if (c, t) == ("qb", 0):
                before.append(("logf",))
    before.append(("cumulate",))
    before += [i for i, _ in attention_items("A")]
    before += [i for i, _ in merge_items("A")]
    before += [("query", "A", 0, 0), ("query", "A", 0, 1), ("select", 0)]

    rest = attention_items("B") + merge_items("B")
    for h in range(HEADS):
        rest += [(("query", "B", h, p), KC * TOKENS["B"] * 4 / 2400) for p in range(2)]
        rest += [(("select", GROUPS_A + h), 1.5), (("select", GROUPS_A + HEADS + h), 1.5)]
        rest += [(("even", h // 2), 0.5)] if h % 2 == 0 else [(("select", GROUPS_A + 2 * HEADS + h // 2), 1.5)]
    slots = {}
    budget = 0.0
    for s in range(UNROLLED):
        front = []
        if s % 2 == 0 and s // 2 + 1 < HEADS:
            front = [(("query", "A", s // 2 + 1, p), KC * TOKENS["A"] * 4 / 2400) for p in range(2)]
        for j in range(2, GROUP):
            here = slots.setdefault((s, j), [])
            if j == 5 and s + 1 < GROUPS_A:
                here.append(("select", s + 1))
            if s in (18, 19) and j == 4:
                here.append(("norm", 10 + s - 18))
            budget = min(budget + 1.26, 3.0)
            while budget > 0 and (front or rest):
                item, cost = (front or rest).pop(0)
                here.append(item)
                budget -= cost
    slots.setdefault((UNROLLED - 1, GROUP - 1), []).extend(i for i, _ in rest)
    return before, slots


def jobs_of(item):
    kind = item[0]
    if kind == "norm" and item[1] < 10:
        return [("nt", item[1], 0), ("nt", item[1], 1)]
    if kind in ("proj", "tr", "gate", "wout", "query", "even", "select"):
        return [item]
    if kind == "cumulate":
        return [("cumulate", 0), ("cumulate", 1)]
    if kind == "ytr":
        return [item]
    if kind == "att":
        _, part, v = item
        us = units(part)
        out = []
        if v < len(us):
            out.append(("scores",) + us[v])
        if 0 <= v - 1 < len(us):
            out.append(("pt",) + us[v - 1])
        if 0 <= v - 2 < len(us):
            out.append(("values",) + us[v - 2])
        return out
    return []


def weight_piece(item):
    if item[0] == "gate":
        return ("gates", item[1], item[2]) if item[3] < 2 else ("branches", item[1], item[2])
    if item[0] == "wout":
        return ("wout", item[1], item[2])
    if item[0] == "query":
        return ("query", item[1], item[2])
    return None


def layer(nc, x_prompt, x_sample, w_qa, w_kvf, w_qb, w_kb, w_vb, w_gates, w_branches, w_out, w_pq, sub_keys,
          g_mix, g_ffn, g_final, b_fgate, sinks, swa_kT, swa_k, swa_v, fox_kT, fox_v, fox_logf, consts, tri_d,
          peer_u, peer_v, y_prompt, y_sample, p_swa_k, p_swa_v, p_fox_k, p_fox_v, p_logf,
          s_swa_k, s_swa_v, s_fox_k, s_fox_v, s_logf):
    before, slots = plan()
    order = list(before)
    for s in range(UNROLLED):
        for j in range(GROUP):
            order += slots.get((s, j), [])
    finals = [("norm", 10 + t) for t in PART["B"]]
    jobs = {}
    for item in order:
        for job in jobs_of(item):
            jobs[job] = len(jobs)
    pieces, last_job = {}, {}
    for item in order:
        w = weight_piece(item)
        if w:
            pieces.setdefault(w, len(pieces))
            last_job[w] = jobs_of(item)[-1]
    selects = [i[1] for i in order if i[0] == "select"]
    select_number = {g: n for n, g in enumerate(selects)}
    plain = [g for g in selects if group_place(g)[0] != 4]
    paired = [g for g in selects if group_place(g)[0] == 4]
    staged_number = {(c, t): TILES * n + t for n, c in enumerate(STAGED) for t in range(TILES)}

    with ExitStack() as ctx:
        def sb(name, shape, dt=F32):
            return ctx.enter_context(nc.sbuf_tensor(name, shape, dt))

        def sem(name):
            return ctx.enter_context(nc.semaphore(name))

        qx = sb("qx", [P, 5120])
        qT = {"A": qx[:, 0:2048].rearrange("p (b n) -> p b n", b=8),
              "B": qx[:, 2048:4608].rearrange("p (b n) -> p b n", b=8)}
        x_part = {"A": qx[:, 0:2048].rearrange("p (t d) -> p t d", d=D),
                  "B": qx[:, 2048:5120].rearrange("p (t d) -> p t d", d=D)}
        hT = {"A": sb("hT_A", [P, KC, 256]), "B": sb("hT_B", [P, KC, 320])}
        kk = sb("kk", [P, 4032])
        kaT = kk[:, 0:512]
        kbT = kk[:, 512:2560].rearrange("p (b n) -> p b n", b=4)
        kaT_s = kk[:, 2560:2752]
        kbT_s = kk[:, 2752:4032].rearrange("p (b n) -> p b n", b=4)
        h2 = {"A": sb("h2_A", [P, 2, D]), "B": kk[:, 0:3072].rearrange("p (t d) -> p t d", d=D)}
        va = sb("va", [P, TILES, KV * HD])
        vb = sb("vb", [P, TILES, HEADS * HD])
        cache_va = sb("cache_va", [P, KV * HD])
        cache_vb = sb("cache_vb", [P, 2, HEADS * HD])
        mixed = sb("mixed", [P, KC, 384])
        u_ring = sb("u_ring", [P, RING, D])
        v_ring = sb("v_ring", [P, RING, D])
        w_ring = sb("w_ring", [P, 2, 2048])
        keysT = sb("keysT", [P, 2 * HEADS, NSUB])
        qp = sb("qp", [P, 2, 2, 256])
        q_even = sb("q_even", [P, 2, DEC])
        q_odd = sb("q_odd", [P, 2, P])
        s_ring = sb("s_ring", [P, 2, 2 * NSUB])
        s_pair = sb("s_pair", [P, 2 * NSUB])
        cand = sb("cand", [P, TOPK, TOPK])
        onehot = sb("onehot", [P, TOPK, TOPK])
        top = sb("top", [P, 2, TOPK])
        top_u = sb("top_u", [P, 2, TOPK], U32)
        top_f = sb("top_f", [P, 2, TOPK])
        best = sb("best", [P, TOPK])
        best_e = sb("best_e", [P, TOPK])
        place_u = sb("place_u", [P, 3, TOPK], U32)
        place_f = sb("place_f", [P, 2, TOPK])
        picked = sb("picked", [P, 2, TOPK])
        small = sb("small", [P, 4])
        experts = sb("experts", [P, GROUPS * GROUP], U32)
        gates = sb("gates", [P, GROUPS * GROUP])
        work = sb("work", [P, 1536])
        probs, probsT, y_rows = work[:, 0:512], work[:, 512:1024], work[:, 1024:1536]
        gate_sig = work[:, 0:640].rearrange("p (w n) -> p w n", w=2)
        gate_tmp = work[:, 640:1280].rearrange("p (w n) -> p w n", w=2)
        const = sb("const", [P, C_END])
        ident = const[:, C_IDENT:C_IDENT + P]
        causal = const[:, C_CAUSAL:C_CAUSAL + P]
        fold = const[:, C_FOLD:C_FOLD + 2 * P].rearrange("p (w n) -> p w n", w=2)
        cos = const[:, C_COS:C_COS + 160].rearrange("p (t n) -> p t n", t=TILES)
        sin = const[:, C_SIN:C_SIN + 160].rearrange("p (t n) -> p t n", t=TILES)
        iota = const[:, C_IOTA:C_IOTA + TOPK]
        g_row = sb("g_row", [P, D])
        negF = sb("negF", [HEADS, SEQ])
        negF_s = sb("negF_s", [HEADS, PAST + DEC])
        bias_f = sb("bias_f", [P, HEADS])
        sink = sb("sink", [P, HEADS])
        neg_sink = sb("neg_sink", [P, HEADS])
        raw_f = sb("raw_f", [P, TILES, HEADS])
        f_tmp = sb("f_tmp", [P, 6, TILES * HEADS])
        logf = sb("logf", [P, TILES, HEADS])
        cache_f = sb("cache_f", [P, 2, HEADS])
        negm = sb("negm", [P, 2, HEADS])
        lsum = sb("lsum", [P, 2, HEADS])
        sink_e = sb("sink_e", [P, 2, HEADS])
        rinv = sb("rinv", [P, HEADS])
        stat = sb("stat", [P, 4, 15])
        diag = sb("diag", [P, DIAGS, P])
        dots_sb = sb("dots_sb", [P, 2, GROUP])
        gelu_sb = sb("gelu_sb", [P, 2, GROUP])
        weights_sb = sb("weights_sb", [P, 2, GROUP])
        idx_u = sb("idx_u", [P, 2, GROUP], U32)
        idx_v = sb("idx_v", [P, 2, GROUP], U32)
        proj_w = [u_ring[:, 4 * n:4 * n + 4, :].rearrange("p a d -> p (a d)") for n in range(2)]
        scratch = v_ring[:].rearrange("p a d -> p (a d)")
        x_tmp = scratch[:, 0:2048].rearrange("p (t d) -> p t d", d=D)
        h_tmp = scratch[:, 2048:4096].rearrange("p (t d) -> p t d", d=D)
        stage = scratch[:, 4096:6144].rearrange("p (t d) -> p t d", d=512)
        rope_c, rope_s = scratch[:, 6144:6656], scratch[:, 6656:7168]
        tri = scratch[:, 7168:7168 + TRI]

        bank = [ctx.enter_context(nc.psum_tensor(f"bank{i}", [P, 512], F32)) for i in range(BANKS)]
        summed = [[ctx.enter_context(nc.psum_tensor(f"summed{a}{b}", [P, 512], F32)) for b in range(2)]
                  for a in range(2)]

        bank_full = [sem(f"bank_full{i}") for i in range(BANKS)]
        bank_used = [sem(f"bank_used{i}") for i in range(BANKS)]
        const_loaded = sem("const_loaded")
        x_tmp_loaded = [sem(f"x_tmp_loaded{i}") for i in range(2)]
        proj_w_loaded = [sem(f"proj_w_loaded{i}") for i in range(2)]
        cache_loaded = sem("cache_loaded")
        keys_loaded = sem("keys_loaded")
        g_loaded = sem("g_loaded")
        w_loaded = [sem(f"w_loaded{i}") for i in range(2)]
        x_loaded = sem("x_loaded")
        squares_summed = sem("squares_summed")
        mean_ready = sem("mean_ready")
        root_ready = sem("root_ready")
        normed = sem("normed")
        roped = sem("roped")
        stage_stored = [sem(f"stage_stored{i}") for i in range(STAGES)]
        logf_step = sem("logf_step")
        rowmax_ready = sem("rowmax_ready")
        y_ready = sem("y_ready")
        mixed_ready = sem("mixed_ready")
        best_ready = sem("best_ready")
        exp_ready = sem("exp_ready")
        selected = sem("selected")
        vector_chain = sem("vector_chain")
        outputs_stored = sem("outputs_stored")
        y_stored = sem("y_stored")
        idx_copied = sem("idx_copied")
        paced = sem("paced")
        paced_scalar = sem("paced_scalar")
        u_landed = [sem(f"u_landed{i}") for i in range(RING)]
        v_landed = [sem(f"v_landed{i}") for i in range(RING)]
        u_free = sem("u_free")
        v_free = sem("v_free")
        gelu_ready = sem("gelu_ready")
        weights_ready = sem("weights_ready")
        diag_ready = sem("diag_ready")
        collected = sem("collected")

        def bank_of(job):
            return bank[jobs[job] % BANKS]

        def full(eng, job):
            n = jobs[job]
            eng.wait_ge(bank_full[n % BANKS], n // BANKS + 1)

        def used(eng, job):
            n = jobs[job]
            eng.wait_ge(bank_used[n % BANKS], n // BANKS + 1)

        def release(job):
            return bank_used[jobs[job] % BANKS]

        def piece_ap(w):
            return w_ring[:, pieces[w] % 2, :]

        def x_of(t):
            return x_part[part_of(t)][:, t - PART[part_of(t)][0], :]

        def h2_of(t):
            return h2[part_of(t)][:, t - PART[part_of(t)][0], :]

        def key_span(t, br):
            if br == "swa":
                if t == 4:
                    return kaT_s, 0, [(P, cache_va[:, :]), (DEC, va[0:DEC, 4, :])]
                first = max(t - 1, 0)
                return kaT, P * first, [(P, va[:, i, :]) for i in range(first, t + 1)]
            if t == 4:
                return kbT_s, 0, [(P, cache_vb[:, 0, :]), (P, cache_vb[:, 1, :]), (DEC, vb[0:DEC, 4, :])]
            return kbT, 0, [(P, vb[:, i, :]) for i in range(t + 1)]

        def group_x(g, offset=None):
            return x_part["B"][:, offset, :] if offset is not None else x_of(group_place(g)[0])

        def group_h(g, offset=None):
            return h2["B"][:, offset, :] if offset is not None else h2_of(group_place(g)[0])

        def stage_stores(c, t):
            return int(c == "kb" or (c == "kvf" and t >= 3))

        def stores_of_stage(b, upto=None):
            keys = [k for k, n in staged_number.items() if n % STAGES == b and (upto is None or n < upto)]
            return 16 * sum(stage_stores(*k) for k in keys)

        block = ctx.enter_context(nc.Block())

        @block.sync
        def _(sp):
            def load_x_tmp(t):
                if t >= 2:
                    sp.wait_ge(normed, t - 1)
                src = x_prompt[P * t:P * t + P, :] if t < 4 else x_sample
                sp.dma_start(x_tmp[0:ROWS[t], t % 2, :], src).then_inc(x_tmp_loaded[t % 2], 16)

            def load_proj(n):
                src = (w_qa, w_kvf, w_qb, w_kb, w_vb)[n]
                if n >= 2:
                    full(sp, ("proj", PROJ[n - 2], TILES - 1))
                sp.dma_start(proj_w[n % 2][:, 0:KC * PROJ_COLS[PROJ[n]]], src).then_inc(proj_w_loaded[n % 2], 16)

            load_x_tmp(0)
            sp.dma_start(g_row[:], g_mix.partition_broadcast(P)).then_inc(g_loaded, 16)
            sp.dma_start(const[:], consts).then_inc(const_loaded, 16)
            load_x_tmp(1)
            load_proj(0)
            load_x_tmp(2)
            load_proj(1)
            load_x_tmp(3)
            load_x_tmp(4)
            for dst, src in ((bias_f[:], b_fgate.partition_broadcast(P)), (sink[:], sinks.partition_broadcast(P)),
                             (tri, tri_d), (cache_f[:], fox_logf), (kaT_s[:, 0:WINDOW], swa_kT),
                             (kbT_s[:, :, 0:PAST], fox_kT), (cache_va[:], swa_v), (cache_vb[:], fox_v)):
                sp.dma_start(dst, src).then_inc(cache_loaded, 16)
            for dst, src in ((s_swa_k, swa_k), (s_swa_v, swa_v)):
                sp.dma_start(dst[0:WINDOW - DEC, :], src[DEC:WINDOW, :]).then_inc(outputs_stored, 16)
            for n in range(2, 5):
                load_proj(n)
            sp.dma_start(keysT[:], sub_keys).then_inc(keys_loaded, 16)
            sp.wait_ge(normed, 5)
            sp.dma_start(g_row[:], g_ffn.partition_broadcast(P)).then_inc(g_loaded, 16)

            by_number = sorted(pieces, key=pieces.get)
            for n, w in enumerate(by_number):
                kind, part, i = w
                if n >= 2:
                    full(sp, last_job[by_number[n - 2]])
                src = {"gates": w_gates, "branches": w_branches, "wout": w_out, "query": w_pq}[kind][i]
                sp.dma_start(w_ring[:, n % 2, 0:src.shape[1]], src).then_inc(w_loaded[n % 2], 16)
                if kind == "branches" and i == KC - 1:
                    full(sp, ("gate", part, i, 3))
                    for t in PART[part]:
                        if t < 4:
                            sp.dma_start(x_of(t), x_prompt[P * t:P * t + P, :]).then_inc(x_loaded, 16)
                        else:
                            for half in range(2):
                                sp.dma_start(x_of(t)[DEC * half:DEC * half + DEC, :], x_sample).then_inc(x_loaded, 16)
                if w == ("query", "B", 0):
                    sp.wait_ge(normed, 10)
                    sp.dma_start(g_row[:], g_final.partition_broadcast(P)).then_inc(g_loaded, 16)

            for t in range(TILES):
                sp.wait_ge(normed, 11 + t)
                dst = y_prompt[P * t:P * t + P, :] if t < 4 else y_sample
                sp.dma_start(dst, h2_of(t)[0:ROWS[t], :]).then_inc(y_stored, 16)
            sp.wait_ge(y_stored, 16 * TILES)

        @block.gpsimd
        def _(pool):
            def copy_indices(g, dst, number, looped=False):
                nc.gpsimd.tensor_copy(dst, experts[:, bass.ds(g * GROUP, GROUP)]).then_inc(idx_copied, 1)
                pool.wait_ge(idx_copied, number)
                if looped:
                    pool.sem_inc(paced, 1)

            def gather(table, ring, landed, free, idx, g, j, looped):
                pool.wait_ge(free, g * GROUP + (j + 1))
                if looped:
                    pool.sem_inc(paced, 1)
                nc.gpsimd.indirect_dma_start(
                    ring[:, j % RING, :], None, table,
                    bass.IndirectOffsetOnAxis(idx[:, j:j + 1], 0)).then_inc(landed[j % RING], 16)

            def gather_u(g, par, j, looped=False):
                gather(peer_u, u_ring, u_landed, u_free, idx_u[:, par, :], g, j, looped)

            def gather_v(g, par, j, looped=False):
                gather(peer_v, v_ring, v_landed, v_free, idx_v[:, par, :], g, j, looped)

            for b in range(STAGES):
                pool.wait_ge(stage_stored[b], stores_of_stage(b))
            for g in range(UNROLLED):
                pool.wait_ge(selected, select_number[g] + 1)
                copy_indices(g, idx_u[:, g % 2, :], max(2 * g, 1))
                if g:
                    copy_indices(g - 1, idx_v[:, (g - 1) % 2, :], 2 * g + 1)
                for j in range(GROUP):
                    gather_u(g, g % 2, j)
                    if g:
                        gather_v(g - 1, (g - 1) % 2, j)
            pool.wait_ge(selected, GROUPS)
            with pool.Fori(0, (GROUPS - UNROLLED) // 2) as p:
                for par in range(2):
                    g = p * 2 + (UNROLLED + par)
                    copy_indices(g, idx_u[:, par, :], g * 2, True)
                    copy_indices(g - 1, idx_v[:, 1 - par, :], g * 2 + 1, True)
                    for j in range(GROUP):
                        gather_u(g, par, j, True)
                        gather_v(g - 1, 1 - par, j, True)
            g = GROUPS - 1
            copy_indices(g, idx_v[:, 1, :], 2 * GROUPS)
            for j in range(GROUP):
                gather_v(g, 1, j)

        @block.tensor
        def _(pe):
            def take_bank(job):
                n = jobs[job]
                if n >= BANKS:
                    pe.wait_ge(bank_used[n % BANKS], n // BANKS)
                return bank_of(job)

            def done(ins, job):
                ins.then_inc(bank_full[jobs[job] % BANKS], 1)

            def front(item):
                kind = item[0]
                w = weight_piece(item)
                if w:
                    pe.wait_ge(w_loaded[pieces[w] % 2], 16 * (pieces[w] // 2 + 1))
                if kind == "norm" and item[1] < 10:
                    n = item[1]
                    t = n % 5
                    src = h_tmp[:, t % 2, :] if n < 5 else h2_of(t)
                    pe.wait_ge(normed, n + 1)
                    for half in range(2):
                        job = ("nt", n, half)
                        ps = take_bank(job)
                        for b in range(4):
                            k = 4 * half + b
                            mm = nc.tensor.transpose(ps[:, P * b:P * b + ROWS[t]], src[0:ROWS[t], P * k:P * k + P],
                                                     ident[0:ROWS[t], 0:ROWS[t]])
                        done(mm, job)
                elif kind == "proj":
                    _, c, t = item
                    n = PROJ.index(c)
                    cols = PROJ_COLS[c]
                    pe.wait_ge(proj_w_loaded[n % 2], 16 * (n // 2 + 1))
                    if c == "qa":
                        used(pe, ("nt", t, 1))
                    ps = take_bank(item)
                    wv = proj_w[n % 2][:, 0:KC * cols].rearrange("p (k n) -> p k n", k=KC)
                    for k in range(KC):
                        mm = nc.tensor.matmul(ps[0:ROWS[t], 0:cols],
                                              hT[part_of(t)][:, k, column_of(t):column_of(t) + ROWS[t]],
                                              wv[:, k, :], start=(k == 0), stop=(k == KC - 1))
                    done(mm, item)
                elif kind == "tr":
                    _, c, t = item
                    if c in ("qa", "kvf"):
                        pe.wait_ge(roped, staged_number[(c, t)] + 1)
                    else:
                        used(pe, ("proj", c, t))
                    ps = take_bank(item)
                    src = stage[:, staged_number[(c, t)] % STAGES, :]
                    for b in range(1 if c == "kvf" else 4):
                        mm = nc.tensor.transpose(ps[:, P * b:P * b + ROWS[t]], src[0:ROWS[t], P * b:P * b + P],
                                                 ident[0:ROWS[t], 0:ROWS[t]])
                    done(mm, item)
                elif kind == "cumulate":
                    pe.wait_ge(logf_step, 5)
                    pe.wait_ge(cache_loaded, 16 * 8)
                    ps = take_bank(("cumulate", 0))
                    for i in range(4):
                        mm = nc.tensor.matmul(ps[0:HEADS, 0:SEQ], logf[:, i, :], tri[:, 384 - P * i:384 - P * i + SEQ],
                                              start=(i == 0), stop=(i == 3))
                    done(mm, ("cumulate", 0))
                    ps = take_bank(("cumulate", 1))
                    n = PAST + DEC
                    for i in range(3):
                        r = P if i < 2 else DEC
                        src = cache_f[:, i, :] if i < 2 else logf[0:DEC, 4, :]
                        mm = nc.tensor.matmul(ps[0:HEADS, 0:n], src, tri[0:r, 384 - P * i:384 - P * i + n],
                                              start=(i == 0), stop=(i == 2))
                    done(mm, ("cumulate", 1))
                elif kind == "att":
                    attention(item)
                elif kind == "ytr":
                    _, t, br = item
                    pe.wait_ge(y_ready, branch_number(t, br) + 1)
                    ps = take_bank(item)
                    for b in range(4):
                        mm = nc.tensor.transpose(ps[:, P * b:P * b + ROWS[t]], y_rows[0:ROWS[t], P * b:P * b + P],
                                                 ident[0:ROWS[t], 0:ROWS[t]])
                    done(mm, item)
                elif kind == "gate":
                    _, part, m, w4 = item
                    n = TOKENS[part]
                    if m == 0 and w4 == 0:
                        for t, br in branches(part):
                            used(pe, ("ytr", t, br))
                    ps = take_bank(item)
                    piece = piece_ap(w)
                    if w4 < 2:
                        wv = piece.rearrange("p (w k n) -> p w k n", w=2, k=KC)
                        for k in range(KC):
                            mm = nc.tensor.matmul(ps[:, 0:n], wv[:, w4, k, :], hT[part][:, k, :],
                                                  start=(k == 0), stop=(k == KC - 1))
                    else:
                        wv = piece[:, 0:1024].rearrange("p (w k n) -> p w k n", w=2, k=4)
                        for k in range(4):
                            mm = nc.tensor.matmul(ps[:, 0:n], wv[:, w4 - 2, k, :], qT[part][:, 4 * (w4 - 2) + k, :],
                                                  start=(k == 0), stop=(k == 3))
                    done(mm, item)
                elif kind == "wout":
                    _, part, q, t = item
                    pe.wait_ge(mixed_ready, KC if part == "A" else 3 * KC)
                    ps = take_bank(item)
                    wv = piece_ap(w).rearrange("p (k n) -> p k n", k=KC)
                    for k in range(KC):
                        mm = nc.tensor.matmul(ps[:, 0:256], mixed[:, k, column_of(t):column_of(t) + P], wv[:, k, :],
                                              start=(k == 0), stop=(k == KC - 1))
                    done(mm, item)
                elif kind == "query":
                    _, part, h, p2 = item
                    n = TOKENS[part]
                    if h == 0 and p2 == 0:
                        for t in PART[part]:
                            used(pe, ("nt", 5 + t, 1))
                    ps = take_bank(item)
                    wv = piece_ap(w).rearrange("p (k n) -> p k n", k=KC)
                    for k in range(KC):
                        mm = nc.tensor.matmul(ps[:, 0:n], wv[:, k, P * p2:P * p2 + P], hT[part][:, k, :],
                                              start=(k == 0), stop=(k == KC - 1))
                    done(mm, item)
                elif kind == "even":
                    h = 2 * item[1]
                    used(pe, ("query", "B", h, 1))
                    ps = take_bank(item)
                    for p2 in range(2):
                        mm = nc.tensor.matmul(ps[0:DEC, P * p2:P * p2 + P], q_even[:, p2, :], keysT[:, 2 * h + p2, :],
                                              start=True, stop=True)
                    done(mm, item)
                elif kind == "select":
                    t, h = group_place(item[1])
                    h += t == 4
                    if item[1] == 0:
                        pe.wait_ge(keys_loaded, 16)
                    used(pe, ("query", part_of(t), h, 1))
                    ps = take_bank(item)
                    for p2 in range(2):
                        q = q_odd[:, p2, :] if t == 4 else qp[:, h % 2, p2, column_of(t):column_of(t) + P]
                        mm = nc.tensor.matmul(ps[:, P * p2:P * p2 + P], q, keysT[:, 2 * h + p2, :],
                                              start=True, stop=True)
                    done(mm, item)

            def attention(item):
                _, part, v = item
                us = units(part)
                if v < len(us):
                    t, br, h = us[v]
                    r, c = ROWS[t], column_of(t)
                    kT, first, blocks = key_span(t, br)
                    n = sum(b[0] for b in blocks)
                    if v == 0:
                        for pt in PART[part]:
                            for cc in STAGED:
                                used(pe, ("tr", cc, pt))
                            used(pe, ("proj", "vb", pt))
                        used(pe, ("cumulate", 1))
                    job = ("scores", t, br, h)
                    ps = take_bank(job)
                    if br == "swa":
                        lo = HD * (h // GRP)
                        mm = nc.tensor.matmul(ps[0:r, 0:n], qT[part][lo:lo + HD, h % GRP, c:c + r],
                                              kT[lo:lo + HD, first:first + n], start=True, stop=True)
                    else:
                        lo = HD * (h % 2)
                        nc.tensor.matmul(ps[0:r, 0:n], qT[part][lo:lo + HD, 4 + h // 2, c:c + r],
                                         kT[lo:lo + HD, h // 2, 0:n], start=True, stop=False)
                        fs = negF_s if t == 4 else negF
                        mm = nc.tensor.matmul(ps[0:r, 0:n], ident[0:HEADS, h:h + 1].broadcast_to([HEADS, r]),
                                              fs[:, 0:n], start=False, stop=True)
                    done(mm, job)
                if 0 <= v - 1 < len(us):
                    t, br, h = us[v - 1]
                    r = ROWS[t]
                    job = ("pt", t, br, h)
                    used(pe, ("scores", t, br, h))
                    ps = take_bank(job)
                    for b, (kn, _v) in enumerate(key_span(t, br)[2]):
                        mm = nc.tensor.transpose(ps[0:kn, P * b:P * b + r], probs[0:r, P * b:P * b + kn],
                                                 ident[0:r, 0:r])
                    done(mm, job)
                if 0 <= v - 2 < len(us):
                    t, br, h = us[v - 2]
                    r = ROWS[t]
                    job = ("values", t, br, h)
                    used(pe, ("pt", t, br, h))
                    ps = take_bank(job)
                    blocks = key_span(t, br)[2]
                    col = HD * (h // GRP if br == "swa" else h)
                    for b, (kn, values) in enumerate(blocks):
                        mm = nc.tensor.matmul(ps[0:r, 0:HD], probsT[0:kn, P * b:P * b + r],
                                              values[:, col:col + HD], start=(b == 0), stop=(b == len(blocks) - 1))
                    done(mm, job)

            def expert_sum(g, par, j):
                if j == 0:
                    pe.wait_ge(collected, g + 1)
                pe.wait_ge(diag_ready, g * GROUP + (j + 1))
                pe.wait_ge(v_landed[j % RING], g * (2 * 16) + 16 * (j // RING + 1))
                for c in range(2):
                    mm = nc.tensor.matmul(summed[par][c][:], diag[:, j % DIAGS, :],
                                          v_ring[:, j % RING, 512 * c:512 * c + 512],
                                          start=(j == 0), stop=(j == GROUP - 1))
                mm.then_inc(v_free, 1)

            pe.wait_ge(const_loaded, 16)
            for item in before:
                front(item)
            for s in range(UNROLLED):
                for j in range(GROUP):
                    if s:
                        expert_sum(s - 1, (s - 1) % 2, j)
                    for item in slots.get((s, j), ()):
                        front(item)
            with pe.Fori(0, (GROUPS - UNROLLED) // 2) as p:
                for par in range(2):
                    for j in range(GROUP):
                        expert_sum(p * 2 + (UNROLLED - 1 + par), 1 - par, j)
            for j in range(GROUP):
                expert_sum(GROUPS - 1, 1, j)

        @block.scalar
        def _(act):
            def copy_out(job, dst, src, scale=1.0):
                nc.scalar.activation(dst, src, ACT.Copy, scale=scale).then_inc(release(job), 1)

            def front(item):
                kind = item[0]
                if kind == "norm":
                    n = item[1]
                    t = n % 5
                    r = ROWS[t] if n < 5 else P
                    if n < 5:
                        act.wait_ge(x_tmp_loaded[t % 2], 16 * (t // 2 + 1))
                        if n >= 2:
                            full(act, ("nt", n - 2, 1))
                        src, dst = x_tmp[0:r, t % 2, :], h_tmp[0:r, t % 2, :]
                    else:
                        if n < 10:
                            used(act, ("wout", part_of(t), 3, t))
                        else:
                            last = [g for g in range(GROUPS) if group_place(g)[0] == t][-1]
                            act.wait_ge(collected, 2 + last + 1)
                        src, dst = x_of(t), h2_of(t)
                    nc.scalar.activation(dst, src, ACT.Square, accum_out=stat[0:r, 0, n:n + 1]).then_inc(
                        squares_summed, 1)
                    act.wait_ge(mean_ready, n + 1)
                    nc.scalar.activation(stat[0:r, 2, n:n + 1], stat[0:r, 1, n:n + 1], ACT.Sqrt).then_inc(
                        root_ready, 1)
                    if n < 10:
                        c = column_of(t)
                        for half in range(2):
                            job = ("nt", n, half)
                            full(act, job)
                            src = bank_of(job)[:].rearrange("p (b n) -> p b n", b=4)[:, :, 0:ROWS[t]]
                            copy_out(job, hT[part_of(t)][:, 4 * half:4 * half + 4, c:c + ROWS[t]], src)
                elif kind == "proj":
                    _, c, t = item
                    if c == "vb":
                        full(act, item)
                        copy_out(item, vb[0:ROWS[t], t, :], bank_of(item)[0:ROWS[t], 0:512])
                        used(act, item)
                        dst = p_fox_v[P * t:P * t + P, :] if t < 4 else s_fox_v
                        act.dma_start(dst, vb[0:ROWS[t], t, :]).then_inc(outputs_stored, 16)
                    if c == "kvf" and t >= 3:
                        used(act, item)
                        dst = p_swa_v if t == 3 else s_swa_v[WINDOW - DEC:WINDOW, :]
                        act.dma_start(dst, va[0:ROWS[t], t, :]).then_inc(outputs_stored, 16)
                elif kind == "tr":
                    _, c, t = item
                    r = ROWS[t]
                    b = staged_number[(c, t)] % STAGES
                    full(act, item)
                    if c == "kb":
                        dst = p_fox_k[P * t:P * t + P, :] if t < 4 else s_fox_k
                        act.dma_start(dst, stage[0:r, b, :]).then_inc(stage_stored[b], 16)
                    if c == "kvf" and t >= 3:
                        dst = p_swa_k if t == 3 else s_swa_k[WINDOW - DEC:WINDOW, :]
                        act.dma_start(dst, stage[0:r, b, 0:P]).then_inc(stage_stored[b], 16)
                    src = bank_of(item)[:].rearrange("p (b n) -> p b n", b=4)[:, :, 0:r]
                    if c in ("qa", "qb"):
                        first = 4 * (c == "qb")
                        copy_out(item, qT[part_of(t)][:, first:first + 4, column_of(t):column_of(t) + r], src, SCALE)
                    elif c == "kvf":
                        dst = kaT[:, P * t:P * t + P] if t < 4 else kaT_s[:, WINDOW:WINDOW + DEC]
                        copy_out(item, dst, bank_of(item)[:, 0:r])
                    else:
                        dst = kbT[:, :, P * t:P * t + P] if t < 4 else kbT_s[:, :, PAST:PAST + DEC]
                        copy_out(item, dst, src)
                elif kind == "logf":
                    act.wait_ge(logf_step, 1)
                    nc.scalar.activation(f_tmp[:, 2, :], f_tmp[:, 1, :], ACT.Exp).then_inc(logf_step, 1)
                    act.wait_ge(logf_step, 3)
                    nc.scalar.activation(f_tmp[:, 4, :], f_tmp[:, 3, :], ACT.Ln).then_inc(logf_step, 1)
                    act.wait_ge(logf_step, 5)
                    act.dma_start(p_logf.rearrange("(t p) h -> p t h", p=P), logf[:, 0:4, :]).then_inc(
                        outputs_stored, 16)
                    act.dma_start(s_logf, logf[0:DEC, 4, :]).then_inc(outputs_stored, 16)
                elif kind == "att":
                    _, part, v = item
                    us = units(part)
                    if v < len(us):
                        t, br, h = us[v]
                        r = ROWS[t]
                        b = branch_number(t, br)
                        n = sum(x[0] for x in key_span(t, br)[2])
                        job = ("scores", t, br, h)
                        act.wait_ge(rowmax_ready, unit_number(t, br, h) + 1)
                        bias = negm[0:r, b % 2, h:h + 1]
                        if br == "swa":
                            nc.scalar.activation(sink_e[0:r, b % 2, h:h + 1], sink[0:r, h:h + 1], ACT.Exp, bias=bias)
                        if v > 0:
                            full(act, ("pt",) + us[v - 1])
                        nc.scalar.activation(probs[0:r, 0:n], bank_of(job)[0:r, 0:n], ACT.Exp, bias=bias,
                                             accum_out=lsum[0:r, b % 2, h:h + 1]).then_inc(release(job), 1)
                    if 0 <= v - 1 < len(us):
                        t, br, h = us[v - 1]
                        job = ("pt", t, br, h)
                        full(act, job)
                        if v - 2 >= 0:
                            full(act, ("values",) + us[v - 2])
                        blocks = key_span(t, br)[2]
                        whole = [b for b in blocks if b[0] == P]
                        src = bank_of(job)
                        if ROWS[t] == P:
                            copy_out(job, probsT[:, 0:P * len(blocks)], src[:, 0:P * len(blocks)])
                        else:
                            nw = len(whole)
                            nc.scalar.activation(
                                probsT[:, 0:P * nw].rearrange("p (b n) -> p b n", b=nw)[:, :, 0:DEC],
                                src[:, 0:P * nw].rearrange("p (b n) -> p b n", b=nw)[:, :, 0:DEC], ACT.Copy)
                            copy_out(job, probsT[0:DEC, P * nw:P * nw + DEC], src[0:DEC, P * nw:P * nw + DEC])
                elif kind == "ytr":
                    _, t, br = item
                    first = 4 * (br == "fox")
                    full(act, item)
                    src = bank_of(item)[:].rearrange("p (b n) -> p b n", b=4)[:, :, 0:ROWS[t]]
                    copy_out(item, qT[part_of(t)][:, first:first + 4, column_of(t):column_of(t) + ROWS[t]], src)
                elif kind == "gate" and item[3] < 2:
                    _, part, m, w4 = item
                    n = TOKENS[part]
                    full(act, item)
                    if m > 0:
                        used(act, ("gate", part, m - 1, w4 + 2))
                    nc.scalar.activation(gate_sig[:, w4, 0:n], bank_of(item)[:, 0:n], ACT.Sigmoid).then_inc(
                        release(item), 1)
                elif kind == "query":
                    _, part, h, p2 = item
                    full(act, item)
                    if part == "B":
                        dst = q_even[:, p2, :] if h % 2 == 0 else q_odd[:, p2, DEC:P]
                        nc.scalar.activation(dst, bank_of(item)[:, 256:320], ACT.Copy)
                    copy_out(item, qp[:, h % 2, p2, :], bank_of(item)[:, 0:256])
                elif kind == "even":
                    n = paired.index(GROUPS_A + 2 * HEADS + item[1])
                    if n:
                        act.wait_ge(selected, select_number[paired[n - 1]] + 1)
                    full(act, item)
                    copy_out(item, s_pair[0:DEC, :], bank_of(item)[0:DEC, 0:2 * NSUB])
                elif kind == "select":
                    g = item[1]
                    n = select_number[g]
                    full(act, item)
                    if group_place(g)[0] == 4:
                        copy_out(item, s_pair[DEC:P, :], bank_of(item)[DEC:P, 0:2 * NSUB])
                    else:
                        i = plain.index(g)
                        if i >= 2:
                            act.wait_ge(selected, select_number[plain[i - 2]] + 1)
                        copy_out(item, s_ring[:, i % 2, :], bank_of(item)[:, 0:2 * NSUB])
                    act.wait_ge(best_ready, n + 1)
                    nc.scalar.activation(best_e[:], best[:], ACT.Exp, bias=small[:, 0:1],
                                         accum_out=small[:, 1:2]).then_inc(exp_ready, 1)

            def gelu(g, par):
                act.wait_ge(u_free, g * GROUP + (RING + GROUP))
                nc.scalar.activation(gelu_sb[:, par, :], dots_sb[:, par, :], ACT.Gelu).then_inc(gelu_ready, 1)

            def diagonal(g, par, j, fold_of):
                if j == 0:
                    act.wait_ge(weights_ready, g + 1)
                act.wait_ge(v_free, g * GROUP + (j + 1 + RING - DIAGS))
                if not isinstance(fold_of, int):
                    act.sem_inc(paced_scalar, 1)
                nc.scalar.activation(diag[:, j % DIAGS, :], fold[:, fold_of, :], ACT.Copy,
                                     scale=weights_sb[:, par, j:j + 1]).then_inc(diag_ready, 1)

            act.wait_ge(const_loaded, 16)
            for item in before:
                front(item)
            for s in range(UNROLLED):
                if s:
                    gelu(s - 1, (s - 1) % 2)
                for j in range(GROUP):
                    if s:
                        diagonal(s - 1, (s - 1) % 2, j, 0)
                    for item in slots.get((s, j), ()):
                        front(item)
            with act.Fori(0, (GROUPS - UNROLLED) // 2) as p:
                for par in range(2):
                    g = p * 2 + (UNROLLED - 1 + par)
                    gelu(g, 1 - par)
                    for j in range(GROUP):
                        diagonal(g, 1 - par, j, g // 32)
            gelu(GROUPS - 1, 1)
            for j in range(GROUP):
                diagonal(GROUPS - 1, 1, j, 1)
            for item in finals:
                front(item)
            act.wait_ge(outputs_stored, 16 * (2 + 5 + 2 + 2))

        @block.vector
        def _(dve):
            chain = [0]

            def step(ins):
                chain[0] += 1
                ins.then_inc(vector_chain, 1)
                return chain[0]

            def behind(n):
                dve.wait_ge(vector_chain, n)

            def front(item):
                kind = item[0]
                if kind == "norm":
                    n = item[1]
                    t = n % 5
                    r = ROWS[t] if n < 5 else P
                    src, dst = (x_tmp[0:r, t % 2, :], h_tmp[0:r, t % 2, :]) if n < 5 else (x_of(t), h2_of(t))
                    dve.wait_ge(squares_summed, n + 1)
                    nc.vector.tensor_scalar(stat[0:r, 1, n:n + 1], stat[0:r, 0, n:n + 1], 1.0 / D, EPS,
                                            ALU.mult, ALU.add).then_inc(mean_ready, 1)
                    dve.wait_ge(root_ready, n + 1)
                    behind(step(nc.vector.reciprocal(stat[0:r, 3, n:n + 1], stat[0:r, 2, n:n + 1])))
                    dve.wait_ge(g_loaded, 16 * (n // 5 + 1))
                    nc.vector.scalar_tensor_tensor(dst, src, stat[0:r, 3, n:n + 1], g_row[0:r, :],
                                                   ALU.mult, ALU.mult).then_inc(normed, 1)
                elif kind == "proj":
                    project(item)
                elif kind == "logf":
                    z, na, e, u, ln, w = (f_tmp[:, i, :] for i in range(6))
                    z3 = z.rearrange("p (t h) -> p t h", t=TILES)
                    dve.wait_ge(cache_loaded, 16 * 8)
                    used(dve, ("proj", "kvf", 4))
                    behind(step(nc.vector.tensor_tensor(z3, raw_f[:], bias_f[:].unsqueeze(1).broadcast_to(
                        [P, TILES, HEADS]), ALU.add)))
                    nc.vector.scalar_tensor_tensor(na, z, -1.0, z, ALU.mult, ALU.min).then_inc(logf_step, 1)
                    dve.wait_ge(logf_step, 2)
                    nc.vector.tensor_scalar(u, e, 1.0, None, ALU.add).then_inc(logf_step, 1)
                    dve.wait_ge(logf_step, 4)
                    behind(step(nc.vector.tensor_scalar(w, u, 1.0, None, ALU.is_equal)))
                    step(nc.vector.tensor_tensor(ln, ln, w, ALU.add))
                    behind(step(nc.vector.scalar_tensor_tensor(w, u, -1.0, w, ALU.add, ALU.add)))
                    behind(step(nc.vector.reciprocal(u, w)))
                    behind(step(nc.vector.tensor_tensor(ln, ln, u, ALU.mult)))
                    behind(step(nc.vector.tensor_tensor(ln, ln, e, ALU.mult)))
                    nc.vector.scalar_tensor_tensor(logf[:].rearrange("p t h -> p (t h)"), z, 0.0, ln,
                                                   ALU.min, ALU.subtract).then_inc(logf_step, 1)
                    behind(step(nc.vector.tensor_scalar(neg_sink[:], sink[:], -1.0, None, ALU.mult)))
                elif kind == "cumulate":
                    for i, dst in ((0, negF), (1, negF_s)):
                        job = ("cumulate", i)
                        full(dve, job)
                        nc.vector.tensor_scalar(dst[:], bank_of(job)[0:HEADS, 0:dst.shape[1]], -1.0, None,
                                                ALU.mult).then_inc(release(job), 1)
                elif kind == "att":
                    attention(item)
                elif kind == "ytr":
                    _, t, br = item
                    r = ROWS[t]
                    b = branch_number(t, br) % 2
                    used(dve, ("values", t, br, HEADS - 1))
                    if br == "swa":
                        behind(step(nc.vector.tensor_tensor(lsum[0:r, b, :], lsum[0:r, b, :], sink_e[0:r, b, :],
                                                            ALU.add)))
                    behind(step(nc.vector.reciprocal(rinv[0:r, :], lsum[0:r, b, :])))
                    yv = y_rows[0:r, :].rearrange("p (h d) -> p h d", h=HEADS)
                    nc.vector.tensor_tensor(yv, yv, rinv[0:r, :].unsqueeze(2).broadcast_to([r, HEADS, HD]),
                                            ALU.mult).then_inc(y_ready, 1)
                elif kind == "gate" and item[3] >= 2:
                    _, part, m, w4 = item
                    n = TOKENS[part]
                    ready = m if part == "A" else KC + 2 * m
                    full(dve, item)
                    used(dve, ("gate", part, m, w4 - 2))
                    if w4 == 2 and ready:
                        dve.wait_ge(mixed_ready, ready)
                    nc.vector.tensor_tensor(gate_tmp[:, w4 - 2, 0:n], bank_of(item)[:, 0:n],
                                            gate_sig[:, w4 - 2, 0:n], ALU.mult).then_inc(release(item), 1)
                    if w4 == 3:
                        used(dve, item)
                        nc.vector.tensor_tensor(mixed[:, m, 0:n], gate_tmp[:, 0, 0:n], gate_tmp[:, 1, 0:n],
                                                ALU.add).then_inc(mixed_ready, 1)
                        if part == "B":
                            nc.vector.tensor_tensor(mixed[:, m, 320:384], gate_tmp[:, 0, 256:320],
                                                    gate_tmp[:, 1, 256:320], ALU.add).then_inc(mixed_ready, 1)
                elif kind == "wout":
                    _, part, q, t = item
                    full(dve, item)
                    dve.wait_ge(x_loaded, 16 * (2 if part == "A" else 6))
                    xv = x_of(t)[:, 256 * q:256 * q + 256]
                    nc.vector.tensor_tensor(xv, xv, bank_of(item)[:, 0:256], ALU.add).then_inc(release(item), 1)
                elif kind == "select":
                    select(item)

            def project(item):
                _, c, t = item
                r = ROWS[t]
                ps = bank_of(item)
                if c == "vb":
                    return
                n = staged_number[(c, t)]
                full(dve, item)
                if n >= STAGES:
                    former = [k for k, m in staged_number.items() if m == n - STAGES][0]
                    full(dve, ("tr",) + former)
                    if stores_of_stage(n % STAGES, n):
                        dve.wait_ge(stage_stored[n % STAGES], stores_of_stage(n % STAGES, n))
                dst = stage[0:r, n % STAGES, :]
                if c in ("qb", "kb"):
                    nc.vector.tensor_copy(dst, ps[0:r, 0:512]).then_inc(release(item), 1)
                    return
                heads = HEADS if c == "qa" else KV
                w = heads * HD
                if n:
                    dve.wait_ge(roped, n)
                if c == "kvf":
                    nc.vector.tensor_copy(va[0:r, t, :], ps[0:r, w:2 * w])
                    nc.vector.tensor_copy(raw_f[0:r, t, :], ps[0:r, 2 * w:2 * w + HEADS])

                def table(a):
                    return a[0:r, t, :].unsqueeze(1).broadcast_to([r, 2 * heads, HD // 2])

                def halves(a):
                    return a[0:r, 0:w].rearrange("p (a b) -> p a b", b=HD // 2)

                nc.vector.tensor_tensor(halves(rope_c), halves(ps), table(cos), ALU.mult)
                nc.vector.tensor_tensor(halves(rope_s), halves(ps), table(sin), ALU.mult).then_inc(release(item), 1)
                used(dve, item)
                if c == "qa":
                    out = dst.rearrange("p (i k d) -> p k i d", i=GRP, k=KV)
                    cv, sv = (a[0:r, 0:w].rearrange("p (k i d) -> p k i d", i=GRP, k=KV) for a in (rope_c, rope_s))
                    lo, hi = (slice(None), slice(None), slice(None), slice(0, HD // 2)), \
                        (slice(None), slice(None), slice(None), slice(HD // 2, HD))
                else:
                    out, cv, sv = (a[:, 0:w].rearrange("p (k d) -> p k d", k=KV)
                                   for a in (dst, rope_c[0:r, :], rope_s[0:r, :]))
                    lo, hi = (slice(None), slice(None), slice(0, HD // 2)), (slice(None), slice(None), slice(HD // 2, HD))
                nc.vector.tensor_tensor(out[lo], cv[lo], sv[hi], ALU.subtract)
                nc.vector.tensor_tensor(out[hi], cv[hi], sv[lo], ALU.add).then_inc(roped, 1)

            def attention(item):
                _, part, v = item
                us = units(part)
                if v < len(us):
                    t, br, h = us[v]
                    r = ROWS[t]
                    b = branch_number(t, br) % 2
                    n = sum(x[0] for x in key_span(t, br)[2])
                    job = ("scores", t, br, h)
                    ps = bank_of(job)
                    dst = negm[0:r, b, h:h + 1]
                    full(dve, job)
                    if br == "swa":
                        if t == 0:
                            behind(step(nc.vector.memset(ps[0:HD, HD:P], MASKED)))
                        elif t < 4:
                            step(nc.vector.memset(ps[0:HD, 3 * HD:4 * HD], MASKED))
                            behind(step(nc.vector.memset(ps[HD:P, 0:HD], MASKED)))
                        behind(step(nc.vector.tensor_reduce(dst, ps[0:r, 0:n], AX_X, ALU.max, negate=True)))
                        nc.vector.tensor_tensor(dst, dst, neg_sink[0:r, h:h + 1], ALU.min).then_inc(rowmax_ready, 1)
                    else:
                        last = ps[0:r, n - r:n]
                        behind(step(nc.vector.tensor_tensor(last, last, causal[0:r, 0:r], ALU.add)))
                        nc.vector.tensor_reduce(dst, ps[0:r, 0:n], AX_X, ALU.max, negate=True).then_inc(
                            rowmax_ready, 1)
                if 0 <= v - 2 < len(us):
                    t, br, h = us[v - 2]
                    r = ROWS[t]
                    job = ("values", t, br, h)
                    full(dve, job)
                    if h == 0 and v - 2 > 0:
                        full(dve, ("ytr",) + us[v - 3][0:2])
                    nc.vector.tensor_copy(y_rows[0:r, HD * h:HD * h + HD], bank_of(job)[0:r, 0:HD]).then_inc(
                        release(job), 1)

            def select(item):
                g = item[1]
                used(dve, item)
                if group_place(g)[0] == 4:
                    used(dve, ("even", (g - GROUPS_A - 2 * HEADS)))
                    s = s_pair
                else:
                    s = s_ring[:, plain.index(g) % 2, :]
                half = [s[:, NSUB * i:NSUB * i + NSUB] for i in range(2)]
                if chain[0]:
                    behind(chain[0])
                n = [step(nc.vector.max(top[:, i, 0:8], half[i])) for i in range(2)]
                for i in range(2):
                    behind(n[i])
                    n[i] = step(nc.vector.max_index(top_u[:, i, 0:8], top[:, i, 0:8], half[i]))
                for i in range(2):
                    behind(n[i])
                    n[i] = step(nc.vector.match_replace(half[i], top[:, i, 0:8], half[i], REPLACED))
                for i in range(2):
                    behind(n[i])
                    n[i] = step(nc.vector.max(top[:, i, 8:16], half[i]))
                for i in range(2):
                    behind(n[i])
                    n[i] = step(nc.vector.max_index(top_u[:, i, 8:16], top[:, i, 8:16], half[i]))
                a = step(nc.vector.tensor_tensor(cand[:], top[:, 0, :].unsqueeze(2).broadcast_to([P, TOPK, TOPK]),
                                                 top[:, 1, :].unsqueeze(1).broadcast_to([P, TOPK, TOPK]), ALU.add))
                behind(n[1])
                step(nc.vector.tensor_copy(top_f[:], top_u[:]))
                flat = cand[:].rearrange("p a b -> p (a b)")
                behind(a)
                behind(step(nc.vector.max(best[:, 0:8], flat)))
                behind(step(nc.vector.max_index(place_u[:, 0, 0:8], best[:, 0:8], flat)))
                behind(step(nc.vector.match_replace(flat, best[:, 0:8], flat, REPLACED)))
                b = step(nc.vector.max(best[:, 8:16], flat))
                behind(b)
                nc.vector.tensor_scalar(small[:, 0:1], best[:, 0:1], -1.0, None, ALU.mult).then_inc(best_ready, 1)
                behind(step(nc.vector.max_index(place_u[:, 0, 8:16], best[:, 8:16], flat)))
                step(nc.vector.tensor_scalar(place_u[:, 1, :], place_u[:, 0, :], 4, None, ALU.logical_shift_right))
                behind(step(nc.vector.tensor_scalar(place_u[:, 2, :], place_u[:, 0, :], TOPK - 1, None,
                                                    ALU.bitwise_and)))
                behind(step(nc.vector.tensor_copy(place_f[:], place_u[:, 1:3, :])))
                for i in range(2):
                    behind(step(nc.vector.tensor_tensor(
                        onehot[:], place_f[:, i, :].unsqueeze(2).broadcast_to([P, TOPK, TOPK]),
                        iota.unsqueeze(1).broadcast_to([P, TOPK, TOPK]), ALU.is_equal)))
                    behind(step(nc.vector.tensor_tensor(
                        onehot[:], onehot[:], top_f[:, i, :].unsqueeze(1).broadcast_to([P, TOPK, TOPK]), ALU.mult)))
                    behind(step(nc.vector.tensor_reduce(picked[:, i, :], onehot[:], AX_X, ALU.add)))
                cols = slice(g * GROUP, g * GROUP + GROUP)
                step(nc.vector.scalar_tensor_tensor(experts[:, cols], picked[:, 0, :], float(NSUB), picked[:, 1, :],
                                                    ALU.mult, ALU.add))
                dve.wait_ge(exp_ready, select_number[g] + 1)
                behind(step(nc.vector.reciprocal(small[:, 2:3], small[:, 1:2])))
                nc.vector.tensor_scalar(gates[:, cols], best_e[:], small[:, 2:3], None, ALU.mult).then_inc(selected, 1)

            def dot(g, par, j, h_rows):
                dve.wait_ge(u_landed[j % RING], g * (2 * 16) + 16 * (j // RING + 1))
                u = u_ring[:, j % RING, :]
                nc.vector.scalar_tensor_tensor(u, u, 1.0, h_rows, ALU.mult, ALU.mult,
                                               accum_out=dots_sb[:, par, j:j + 1]).then_inc(u_free, 1)

            def weigh(g, par):
                dve.wait_ge(gelu_ready, g + 1)
                nc.vector.tensor_tensor(weights_sb[:, par, :], gelu_sb[:, par, :],
                                        gates[:, bass.ds(g * GROUP, GROUP)], ALU.mult).then_inc(weights_ready, 1)

            def collect(g, par, rows):
                dve.wait_ge(v_free, g * GROUP + (RING + GROUP))
                dve.wait_ge(collected, g + 2)
                for c in range(2):
                    o = rows[:, 512 * c:512 * c + 512]
                    ins = nc.vector.tensor_tensor(o, o, summed[par][c][:], ALU.add)
                ins.then_inc(collected, 1)

            step(nc.vector.memset(q_odd[:], 0.0))
            step(nc.vector.memset(raw_f[:], 0.0))
            behind(chain[0])
            dve.sem_inc(u_free, RING)
            dve.sem_inc(v_free, RING)
            dve.sem_inc(collected, 2)
            dve.wait_ge(const_loaded, 16)
            for item in before:
                front(item)
            for s in range(UNROLLED):
                for j in range(GROUP):
                    dot(s, s % 2, j, group_h(s))
                    if j == 1 and s >= 1:
                        weigh(s - 1, (s - 1) % 2)
                    if j == 8 and s >= 2:
                        collect(s - 2, s % 2, group_x(s - 2))
                    for item in slots.get((s, j), ()):
                        front(item)
            with dve.Fori(0, (GROUPS - UNROLLED) // 2) as p:
                for par in range(2):
                    first = UNROLLED - GROUPS_A + par
                    for j in range(GROUP):
                        dot(p * 2 + (UNROLLED + par), par, j, group_h(None, (p * 2 + first) // HEADS))
                        if j == 1:
                            weigh(p * 2 + (UNROLLED + par - 1), 1 - par)
                        if j == 8:
                            collect(p * 2 + (UNROLLED + par - 2), par, group_x(None, (p * 2 + (first - 2)) // HEADS))
            weigh(GROUPS - 1, 1)
            collect(GROUPS - 2, 0, group_x(GROUPS - 2))
            collect(GROUPS - 1, 1, group_x(GROUPS - 1))
            for item in finals:
                front(item)


def constants():
    c = np.zeros((P, C_END), np.float32)
    c[:, C_IDENT:C_IDENT + P] = np.eye(P)
    row, col = np.arange(P)[:, None], np.arange(P)[None, :]
    c[:, C_CAUSAL:C_CAUSAL + P] = np.where(col <= row, 0.0, MASKED)
    c[:, C_FOLD:C_FOLD + P] = np.eye(P)
    c[:, C_FOLD + P:C_FOLD + 2 * P] = (row % DEC == col)
    half = HD // 2
    inv = (np.float32(10000.0) ** (-np.arange(half, dtype=np.float32) / np.float32(half))).astype(np.float32)
    for t in range(TILES):
        pos = (np.arange(P) + (P * t if t < 4 else PAST)).astype(np.float32)
        angle = (pos[:, None] * inv[None, :]).astype(np.float32)
        c[:, C_COS + half * t:C_COS + half * t + half] = np.cos(angle)
        c[:, C_SIN + half * t:C_SIN + half * t + half] = np.sin(angle)
    c[:, C_IOTA:C_IOTA + TOPK] = np.arange(TOPK)
    tri = (np.arange(TRI)[None, :] >= np.arange(P)[:, None] + 384).astype(np.float32)
    return c, tri


def kernel(x_prompt, x_sample, cache_swa_k, cache_swa_v, cache_fox_k, cache_fox_v, cache_fox_logf, g_mix, w_in,
           b_fgate, sinks, w_a_out, w_b_out, w_out, g_ffn, w_pq, peer_sub_keys, peer_u, peer_v, g_final):
    import concourse.bacc as bacc
    from concourse.bass_utils import run_bass_kernel_spmd

    def rows_in(w, k=KC):
        return np.asarray(w).reshape(k, P, -1).transpose(1, 0, 2)

    w = rows_in(w_in[0])
    a, b, c, d, e = 512, 768, 2304, 2312, 3336
    ga, gb = w[:, :, d:e], w[:, :, e:]
    wa, wb = rows_in(w_a_out[0], 4), rows_in(w_b_out[0], 4)

    def cut(arrays, n):
        s = np.stack(arrays, 1)
        s = s.reshape(P, s.shape[1], s.shape[2], -1, n).transpose(3, 0, 1, 2, 4)
        return s.reshape(s.shape[0], P, -1)

    const, tri = constants()
    kvf = np.concatenate([w[:, :, a:b], w[:, :, c:d]], -1)
    arrays = {
        "x_prompt": np.asarray(x_prompt)[0], "x_sample": np.asarray(x_sample)[0],
        "w_qa": w[:, :, 0:a].reshape(P, -1), "w_kvf": kvf.reshape(P, -1),
        "w_qb": w[:, :, b:b + 512].reshape(P, -1), "w_kb": w[:, :, b + 512:b + 1024].reshape(P, -1),
        "w_vb": w[:, :, b + 1024:b + 1536].reshape(P, -1),
        "w_gates": cut([ga, gb], P), "w_branches": cut([wa, wb], P),
        "w_out": cut([rows_in(w_out[0])], 256), "w_pq": cut([rows_in(w_pq[0])], 256),
        "sub_keys": np.asarray(peer_sub_keys)[0].transpose(3, 0, 1, 2).reshape(P, 2 * HEADS, NSUB),
        "g_mix": np.asarray(g_mix)[0], "g_ffn": np.asarray(g_ffn)[0], "g_final": np.asarray(g_final),
        "b_fgate": np.asarray(b_fgate)[0], "sinks": np.asarray(sinks)[0],
        "swa_kT": np.asarray(cache_swa_k)[0, 0].reshape(WINDOW, P).T,
        "swa_k": np.asarray(cache_swa_k)[0, 0].reshape(WINDOW, P),
        "swa_v": np.asarray(cache_swa_v)[0, 0].reshape(WINDOW, P),
        "fox_kT": np.asarray(cache_fox_k)[0, 0].reshape(PAST, 4, P).transpose(2, 1, 0),
        "fox_v": np.asarray(cache_fox_v)[0, 0].reshape(2, P, 512).transpose(1, 0, 2),
        "fox_logf": np.asarray(cache_fox_logf)[0, 0].reshape(2, P, HEADS).transpose(1, 0, 2),
        "consts": const, "tri": tri, "peer_u": np.asarray(peer_u)[0], "peer_v": np.asarray(peer_v)[0],
    }
    arrays = {f"in_{k}": np.ascontiguousarray(v) for k, v in arrays.items()}
    outs = [(SEQ, D), (DEC, D), (WINDOW, P), (WINDOW, P), (SEQ, 512), (SEQ, 512), (SEQ, HEADS),
            (WINDOW, P), (WINDOW, P), (DEC, 512), (DEC, 512), (DEC, HEADS)]
    nc = bacc.Bacc("TRN2", target_bir_lowering=False, num_devices=1, dynamic_dma_scratch_size=8192)
    args = [nc.dram_tensor(k, v.shape, mybir.dt.from_np(v.dtype), kind="ExternalInput").ap()
            for k, v in arrays.items()]
    args += [nc.dram_tensor(f"out_{i}", s, F32, kind="ExternalOutput").ap() for i, s in enumerate(outs)]
    layer(nc, *args)
    r = run_bass_kernel_spmd(nc, [arrays], core_ids=[0]).results[0]
    shapes = [(1, SEQ, D), (1, DEC, D), (1, 1, WINDOW, KV, HD), (1, 1, WINDOW, KV, HD), (1, 1, SEQ, HEADS, HD),
              (1, 1, SEQ, HEADS, HD), (1, 1, SEQ, HEADS), (1, 1, WINDOW, KV, HD), (1, 1, WINDOW, KV, HD),
              (1, 1, DEC, HEADS, HD), (1, 1, DEC, HEADS, HD), (1, 1, DEC, HEADS)]
    return tuple(r[f"out_{i}"].reshape(s) for i, s in enumerate(shapes))
```

```python
from contextlib import ExitStack

import numpy as np

import concourse.bass as bass
from concourse import mybir

ALU = mybir.AluOpType
ACT = mybir.ActivationFunctionType
AX_X = mybir.AxisListType.X
F32 = mybir.dt.float32
U32 = mybir.dt.uint32

P = 128
D = 1024
KC = D // P
SEQ, DEC, PAST = 512, 64, 256
HD = 64
HEADS = 8
KV = 2
GRP = HEADS // KV
WINDOW = 128
SCALE = HD ** -0.5
EPS = 1e-6
MASKED = -1e30
REPLACED = -3e38
TILES = 5
ROWS = [P, P, P, P, DEC]
PART = {"A": (0, 1), "B": (2, 3, 4)}
TOKENS = {"A": 256, "B": 320}
TOPK = 16
NSUB = 128
GROUP = TOPK
RING = 8
DIAGS = 4
GROUPS_A = 2 * HEADS
GROUPS = GROUPS_A + 2 * HEADS + HEADS // 2
UNROLLED = 24
RATE_A, RATE_B = 1.75, 1.26
ATTENTION_COST, SELECT_COST = 1.0, 0.75
PROJ = [("qa", 0), ("qa", 1), ("kv", 0), ("qb", 0), ("qb", 1), ("kb", 0), ("kb", 1), ("vb", 0), ("vb", 1)]
PC = 256
STAGED = ("qa", "kv", "qb", "kb")
VECTOR_SLOTS = (3, 7, 11, 15)
STAGES = 4
BANKS = 4
TRI = 896
C_IDENT, C_CAUSAL, C_FOLD, C_COS, C_SIN, C_IOTA, C_END = 0, 128, 256, 512, 672, 832, 848


def part_of(t):
    return "A" if t in PART["A"] else "B"


def column_of(t):
    return P * (t - PART[part_of(t)][0])


def group_place(g):
    if g < GROUPS_A:
        return g % 2, g // 2
    n = g - GROUPS_A
    return (2 + n // HEADS, n % HEADS) if n < 2 * HEADS else (4, 2 * (n - 2 * HEADS))


def slots_of_pe(g):
    return [j for j in range(GROUP) if g >= GROUPS_A or j not in VECTOR_SLOTS]


def pe_before(g):
    n = len(VECTOR_SLOTS)
    if isinstance(g, int) and g < GROUPS_A:
        return g * (GROUP - n)
    return g * GROUP - GROUPS_A * n


def branches(part):
    return [(t, br) for t in PART[part] for br in ("swa", "fox")]


def units(part):
    return [(t, br, h) for t, br in branches(part) for h in range(HEADS)]


def branch_number(t, br):
    return 2 * t + (br == "fox")


def unit_number(t, br, h):
    return branch_number(t, br) * HEADS + h


def attention_items(part):
    n = len(units(part))
    out = []
    for v in range(n + 2):
        out.append((("att", part, v), 1.0))
        if v >= 9 and (v - 9) % 8 == 0:
            out.append((("ytr",) + branches(part)[(v - 9) // 8], 1.0))
    return out


def merge_items(part):
    n = TOKENS[part]
    us = n * 4 / 2400
    out = [(("gate", part, m, w), us * (KC if w < 2 else KC // 2)) for m in range(KC) for w in (0, 2, 1, 3)]
    for q in range(4):
        for t in PART[part]:
            out.append((("wout", part, q, t), KC * 256 * 4 / 2400))
            if q == 3:
                out.append((("norm", 5 + t), 2.0))
    return out


def project_items(part):
    out, waiting = [], None
    for n, (c, half) in enumerate(PROJ):
        for t in PART[part]:
            out.append((("proj", n, t), KC * PC * 4 / 2400))
            if waiting:
                out.append((("tr",) + waiting, 0.5))
            last = half == 1 or c == "kv"
            waiting = (c, t) if last and c in STAGED else None
    return out


def select_items(g):
    return [("score", g), ("halves", g), ("sums", g), ("places", g), ("weights", g)]


def plan():
    before = [("norm", 0), ("norm", 1)]
    inserted = {4: [("norm", 2)], 8: [("norm", 3)], 11: [("norm", 4)], 14: [("forget", t) for t in range(TILES)],
                17: [("logf",)]}
    for n, (item, _) in enumerate(project_items("A")):
        before.append(item)
        before += inserted.get(n, [])
    before.append(("cumulate",))
    before += [i for i, _ in attention_items("A")]
    before += [i for i, _ in merge_items("A")]
    before += [("query", "A", 0, 0), ("query", "A", 0, 1)]
    before += select_items(0) + select_items(1)

    rest = project_items("B") + [(i, ATTENTION_COST) for i, _ in attention_items("B")] + merge_items("B")
    for h in range(HEADS):
        rest += [(("query", "B", h, p), KC * TOKENS["B"] * 4 / 2400) for p in range(2)]
        for g in (GROUPS_A + h, GROUPS_A + HEADS + h):
            rest += [(i, SELECT_COST) for i in select_items(g)]
        if h % 2 == 0:
            rest.append((("even", h // 2), 0.4))
        else:
            rest += [(i, SELECT_COST) for i in select_items(GROUPS_A + 2 * HEADS + h // 2)]
    slots = {}
    budget = 0.0
    for s in range(UNROLLED):
        for j in range(2, GROUP):
            here = slots.setdefault((s, j), [])
            if j < 4 and s % 2 == 0 and s // 2 + 1 < HEADS:
                here.append(("query", "A", s // 2 + 1, j - 2))
                budget -= KC * TOKENS["A"] * 4 / 2400
            if 5 <= j < 15 and j % 2 and s + 2 < GROUPS_A:
                here.append(select_items(s + 2)[(j - 5) // 2])
            if s in (18, 19) and j == 4:
                here.append(("norm", 10 + s - 18))
            budget = min(budget + (RATE_A if s <= GROUPS_A else RATE_B), 3.0)
            while budget > 0 and rest:
                if rest[0][0][0] == "score" and (s, j) <= (GROUPS_A - 3, 13):
                    break
                item, cost = rest.pop(0)
                here.append(item)
                budget -= cost
    slots.setdefault((UNROLLED - 1, GROUP - 1), []).extend(i for i, _ in rest)
    return before, slots


def jobs_of(item):
    kind = item[0]
    if kind == "norm" and item[1] < 10:
        return [("nt", item[1], 0), ("nt", item[1], 1)]
    if kind in ("proj", "forget", "tr", "gate", "wout", "query", "even", "score"):
        return [item]
    if kind == "cumulate":
        return [("cumulate", 0), ("cumulate", 1)]
    if kind == "ytr":
        return [item]
    if kind == "att":
        _, part, v = item
        us = units(part)
        out = []
        if v < len(us):
            out.append(("scores",) + us[v])
        if 0 <= v - 1 < len(us):
            out.append(("pt",) + us[v - 1])
        if 0 <= v - 2 < len(us):
            out.append(("values",) + us[v - 2])
        return out
    return []


def weight_piece(item):
    if item[0] == "gate":
        return ("merge", item[1], 2 * item[2] + item[3] % 2)
    if item[0] == "wout":
        return ("wout", item[1], item[2])
    if item[0] == "query":
        return ("query", item[1], item[2])
    if item[0] == "proj":
        return ("proj", part_of(item[2]), item[1])
    return None


def layer(nc, x_prompt, x_sample, w_proj, w_forget, w_merge, w_out, w_pq, sub_keys,
          g_mix, g_ffn, g_final, b_fgate, sinks, swa_kT, swa_k, swa_v, fox_kT, fox_v, fox_logf, consts, tri_d,
          peer_u, peer_v, y_prompt, y_sample, p_swa_k, p_swa_v, p_fox_k, p_fox_v, p_logf,
          s_swa_k, s_swa_v, s_fox_k, s_fox_v, s_logf):
    before, slots = plan()
    order = list(before)
    for s in range(UNROLLED):
        for j in range(GROUP):
            order += slots.get((s, j), [])
    finals = [("norm", 10 + t) for t in PART["B"]]
    jobs = {}
    for item in order:
        for job in jobs_of(item):
            jobs[job] = len(jobs)
    pieces, last_job = {}, {}
    for item in order:
        w = weight_piece(item)
        if w:
            pieces.setdefault(w, len(pieces))
            last_job[w] = jobs_of(item)[-1]
    selects = [i[1] for i in order if i[0] == "score"]
    select_number = {g: n for n, g in enumerate(selects)}
    plain = [g for g in selects if group_place(g)[0] != 4]
    paired = [g for g in selects if group_place(g)[0] == 4]
    staged = [(c, t) for part in "AB" for c in STAGED for t in PART[part]]
    staged_number = {key: n for n, key in enumerate(staged)}
    ropes = [i for i in order if i[0] == "proj" and PROJ[i[1]][0] in ("qa", "kv")]
    rope_number = {i: n for n, i in enumerate(ropes)}

    with ExitStack() as ctx:
        def sb(name, shape, dt=F32):
            return ctx.enter_context(nc.sbuf_tensor(name, shape, dt))

        def sem(name):
            return ctx.enter_context(nc.semaphore(name))

        qx = sb("qx", [P, 5120])
        qT = {"A": qx[:, 0:2048].rearrange("p (b n) -> p b n", b=8),
              "B": qx[:, 2048:4608].rearrange("p (b n) -> p b n", b=8)}
        x_part = {"A": qx[:, 0:2048].rearrange("p (t d) -> p t d", d=D),
                  "B": qx[:, 2048:5120].rearrange("p (t d) -> p t d", d=D)}
        hT = {"A": sb("hT_A", [P, KC, 256]), "B": sb("hT_B", [P, KC, 320])}
        kk = sb("kk", [P, 4032])
        kaT = kk[:, 0:512]
        kbT = kk[:, 512:2560].rearrange("p (b n) -> p b n", b=4)
        kaT_s = kk[:, 2560:2752]
        kbT_s = kk[:, 2752:4032].rearrange("p (b n) -> p b n", b=4)
        h2 = {"A": sb("h2_A", [P, 2, D]), "B": kk[:, 0:3072].rearrange("p (t d) -> p t d", d=D)}
        va = sb("va", [P, TILES, KV * HD])
        vb = sb("vb", [P, TILES, HEADS * HD])
        cache_va = sb("cache_va", [P, KV * HD])
        cache_vb = sb("cache_vb", [P, 2, HEADS * HD])
        shared = sb("shared", [P, KC * 384])
        mixed = shared[:].rearrange("p (k n) -> p k n", k=KC)
        stage = shared[:, 0:STAGES * 512].rearrange("p (t d) -> p t d", d=512)
        rope_c, rope_s = shared[:, 2048:2048 + PC], shared[:, 2560:2560 + PC]
        u_ring = sb("u_ring", [P, RING, D])
        v_ring = sb("v_ring", [P, RING, D])
        w_ring = sb("w_ring", [P, 2, 2048])
        keysT = sb("keysT", [P, 2 * HEADS, NSUB])
        qp = sb("qp", [P, 2, 2, 256])
        q_even = sb("q_even", [P, 2, DEC])
        q_odd = sb("q_odd", [P, 2, P])
        s_ring = sb("s_ring", [P, 2, 2 * NSUB])
        s_pair = sb("s_pair", [P, 2 * NSUB])
        cand = sb("cand", [P, TOPK, TOPK])
        onehot = sb("onehot", [P, TOPK, TOPK])
        top = sb("top", [P, 2, TOPK])
        top_u = sb("top_u", [P, 2, TOPK], U32)
        top_f = sb("top_f", [P, 2, TOPK])
        best = sb("best", [P, TOPK])
        best_e = sb("best_e", [P, TOPK])
        place_u = sb("place_u", [P, 3, TOPK], U32)
        place_f = sb("place_f", [P, 2, TOPK])
        picked = sb("picked", [P, 2, TOPK])
        small = sb("small", [P, 4])
        experts = sb("experts", [P, GROUPS * GROUP], U32)
        gates = sb("gates", [P, GROUPS * GROUP])
        work = sb("work", [P, 1536])
        probs, probsT, y_rows = work[:, 0:512], work[:, 512:1024], work[:, 1024:1536]
        gate_sig = work[:, 0:640].rearrange("p (w n) -> p w n", w=2)
        gate_tmp = work[:, 640:1280].rearrange("p (w n) -> p w n", w=2)
        const = sb("const", [P, C_END])
        ident = const[:, C_IDENT:C_IDENT + P]
        causal = const[:, C_CAUSAL:C_CAUSAL + P]
        fold = const[:, C_FOLD:C_FOLD + 2 * P].rearrange("p (w n) -> p w n", w=2)
        cos = const[:, C_COS:C_COS + 160].rearrange("p (t n) -> p t n", t=TILES)
        sin = const[:, C_SIN:C_SIN + 160].rearrange("p (t n) -> p t n", t=TILES)
        iota = const[:, C_IOTA:C_IOTA + TOPK]
        g_row = sb("g_row", [P, D])
        negF = sb("negF", [HEADS, SEQ])
        negF_s = sb("negF_s", [HEADS, PAST + DEC])
        bias_f = sb("bias_f", [P, HEADS])
        sink = sb("sink", [P, HEADS])
        neg_sink = sb("neg_sink", [P, HEADS])
        raw_f = sb("raw_f", [P, TILES, HEADS])
        f_tmp = sb("f_tmp", [P, 6, TILES * HEADS])
        logf = sb("logf", [P, TILES, HEADS])
        cache_f = sb("cache_f", [P, 2, HEADS])
        negm = sb("negm", [P, 2, HEADS])
        lsum = sb("lsum", [P, 2, HEADS])
        sink_e = sb("sink_e", [P, 2, HEADS])
        rinv = sb("rinv", [P, HEADS])
        stat = sb("stat", [P, 4, 15])
        diag = sb("diag", [P, DIAGS, P])
        dots_sb = sb("dots_sb", [P, 2, GROUP])
        gelu_sb = sb("gelu_sb", [P, 2, GROUP])
        weights_sb = sb("weights_sb", [P, 2, GROUP])
        idx_u = sb("idx_u", [P, 2, GROUP], U32)
        idx_v = sb("idx_v", [P, 2, GROUP], U32)
        scratch = v_ring[:].rearrange("p a d -> p (a d)")
        x_tmp = scratch[:, 0:2048].rearrange("p (t d) -> p t d", d=D)
        h_tmp = scratch[:, 2048:4096].rearrange("p (t d) -> p t d", d=D)
        tri = scratch[:, 4096:4096 + TRI]
        w_f = scratch[:, 4096 + TRI:4096 + TRI + KC * HEADS].rearrange("p (k n) -> p k n", k=KC)

        bank = [ctx.enter_context(nc.psum_tensor(f"bank{i}", [P, 512], F32)) for i in range(BANKS)]
        summed = [[ctx.enter_context(nc.psum_tensor(f"summed{a}{b}", [P, 512], F32)) for b in range(2)]
                  for a in range(2)]

        bank_full = [sem(f"bank_full{i}") for i in range(BANKS)]
        bank_used = [sem(f"bank_used{i}") for i in range(BANKS)]
        const_loaded = sem("const_loaded")
        x_tmp_loaded = [sem(f"x_tmp_loaded{i}") for i in range(2)]
        cache_loaded = sem("cache_loaded")
        keys_loaded = sem("keys_loaded")
        g_loaded = sem("g_loaded")
        w_loaded = [sem(f"w_loaded{i}") for i in range(2)]
        x_loaded = sem("x_loaded")
        squares_summed = sem("squares_summed")
        mean_ready = sem("mean_ready")
        root_ready = sem("root_ready")
        normed = sem("normed")
        roped = sem("roped")
        stage_stored = [sem(f"stage_stored{i}") for i in range(STAGES)]
        logf_step = sem("logf_step")
        rowmax_ready = sem("rowmax_ready")
        y_ready = sem("y_ready")
        mixed_ready = sem("mixed_ready")
        best_ready = sem("best_ready")
        exp_ready = sem("exp_ready")
        selected = sem("selected")
        vector_chain = sem("vector_chain")
        outputs_stored = sem("outputs_stored")
        y_stored = sem("y_stored")
        idx_copied = sem("idx_copied")
        paced = sem("paced")
        paced_scalar = sem("paced_scalar")
        u_landed = [sem(f"u_landed{i}") for i in range(RING)]
        v_landed = [sem(f"v_landed{i}") for i in range(RING)]
        u_free = sem("u_free")
        v_free = sem("v_free")
        v_taken = sem("v_taken")
        gelu_ready = sem("gelu_ready")
        weights_ready = sem("weights_ready")
        diag_ready = sem("diag_ready")
        collected = sem("collected")

        def bank_of(job):
            return bank[jobs[job] % BANKS]

        def full(eng, job):
            n = jobs[job]
            eng.wait_ge(bank_full[n % BANKS], n // BANKS + 1)

        def used(eng, job):
            n = jobs[job]
            eng.wait_ge(bank_used[n % BANKS], n // BANKS + 1)

        def release(job):
            return bank_used[jobs[job] % BANKS]

        def piece_ap(w):
            return w_ring[:, pieces[w] % 2, :]

        def x_of(t):
            return x_part[part_of(t)][:, t - PART[part_of(t)][0], :]

        def h2_of(t):
            return h2[part_of(t)][:, t - PART[part_of(t)][0], :]

        def key_span(t, br):
            if br == "swa":
                if t == 4:
                    return kaT_s, 0, [(P, cache_va[:, :]), (DEC, va[0:DEC, 4, :])]
                first = max(t - 1, 0)
                return kaT, P * first, [(P, va[:, i, :]) for i in range(first, t + 1)]
            if t == 4:
                return kbT_s, 0, [(P, cache_vb[:, 0, :]), (P, cache_vb[:, 1, :]), (DEC, vb[0:DEC, 4, :])]
            return kbT, 0, [(P, vb[:, i, :]) for i in range(t + 1)]

        def group_x(g, offset=None):
            return x_part["B"][:, offset, :] if offset is not None else x_of(group_place(g)[0])

        def group_h(g, offset=None):
            return h2["B"][:, offset, :] if offset is not None else h2_of(group_place(g)[0])

        def stage_stores(c, t):
            return int(c == "kb" or (c == "kv" and t >= 3))

        def stores_of_stage(b, upto=None):
            keys = [k for k, n in staged_number.items() if n % STAGES == b and (upto is None or n < upto)]
            return 16 * sum(stage_stores(*k) for k in keys)

        block = ctx.enter_context(nc.Block())

        @block.sync
        def _(sp):
            def load_x_tmp(t):
                if t >= 2:
                    sp.wait_ge(normed, t - 1)
                src = x_prompt[P * t:P * t + P, :] if t < 4 else x_sample
                sp.dma_start(x_tmp[0:ROWS[t], t % 2, :], src).then_inc(x_tmp_loaded[t % 2], 16)

            by_number = sorted(pieces, key=pieces.get)

            def load_piece(n):
                kind, part, i = by_number[n]
                if n >= 2:
                    full(sp, last_job[by_number[n - 2]])
                src = {"proj": w_proj, "merge": w_merge, "wout": w_out, "query": w_pq}[kind][i]
                sp.dma_start(w_ring[:, n % 2, 0:src.shape[1]], src).then_inc(w_loaded[n % 2], 16)

            load_x_tmp(0)
            sp.dma_start(g_row[:], g_mix.partition_broadcast(P)).then_inc(g_loaded, 16)
            sp.dma_start(const[:], consts).then_inc(const_loaded, 16)
            load_x_tmp(1)
            load_piece(0)
            load_piece(1)
            load_x_tmp(2)
            load_piece(2)
            load_x_tmp(3)
            load_piece(3)
            load_x_tmp(4)
            sp.dma_start(w_f, w_forget).then_inc(cache_loaded, 16)
            for dst, src in ((bias_f[:], b_fgate.partition_broadcast(P)), (sink[:], sinks.partition_broadcast(P)),
                             (tri, tri_d), (cache_f[:], fox_logf), (kaT_s[:, 0:WINDOW], swa_kT),
                             (kbT_s[:, :, 0:PAST], fox_kT), (cache_va[:], swa_v), (cache_vb[:], fox_v)):
                sp.dma_start(dst, src).then_inc(cache_loaded, 16)
            for dst, src in ((s_swa_k, swa_k), (s_swa_v, swa_v)):
                sp.dma_start(dst[0:WINDOW - DEC, :], src[DEC:WINDOW, :]).then_inc(outputs_stored, 16)
            for n, w in enumerate(by_number):
                kind, part, i = w
                if n < 4:
                    continue
                load_piece(n)
                if n == len(PROJ):
                    sp.dma_start(keysT[:], sub_keys).then_inc(keys_loaded, 16)
                    sp.wait_ge(normed, 5)
                    sp.dma_start(g_row[:], g_ffn.partition_broadcast(P)).then_inc(g_loaded, 16)
                former, part = by_number[n - 1][0:2]
                if former == "merge" and by_number[n - 1][2] == 2 * KC - 1:
                    full(sp, ("gate", part, KC - 1, 3))
                    for t in PART[part]:
                        if t < 4:
                            sp.dma_start(x_of(t), x_prompt[P * t:P * t + P, :]).then_inc(x_loaded, 16)
                        else:
                            for half in range(2):
                                sp.dma_start(x_of(t)[DEC * half:DEC * half + DEC, :], x_sample).then_inc(x_loaded, 16)
                if w == ("query", "B", 0):
                    sp.wait_ge(normed, 10)
                    sp.dma_start(g_row[:], g_final.partition_broadcast(P)).then_inc(g_loaded, 16)

            for t in range(TILES):
                sp.wait_ge(normed, 11 + t)
                dst = y_prompt[P * t:P * t + P, :] if t < 4 else y_sample
                sp.dma_start(dst, h2_of(t)[0:ROWS[t], :]).then_inc(y_stored, 16)
            sp.wait_ge(y_stored, 16 * TILES)

        @block.gpsimd
        def _(pool):
            def copy_indices(g, dst, number, looped=False):
                nc.gpsimd.tensor_copy(dst, experts[:, bass.ds(g * GROUP, GROUP)]).then_inc(idx_copied, 1)
                pool.wait_ge(idx_copied, number)
                if looped:
                    pool.sem_inc(paced, 1)

            def gather(table, ring, landed, idx, j, looped):
                if looped:
                    pool.sem_inc(paced, 1)
                nc.gpsimd.indirect_dma_start(
                    ring[:, j % RING, :], None, table,
                    bass.IndirectOffsetOnAxis(idx[:, j:j + 1], 0)).then_inc(landed[j % RING], 16)

            def gather_u(g, par, j, looped=False):
                pool.wait_ge(u_free, g * GROUP + (j + 1))
                gather(peer_u, u_ring, u_landed, idx_u[:, par, :], j, looped)

            def gather_v(g, par, j, looped=False):
                if looped:
                    pool.wait_ge(v_free, pe_before(g) + (j + 1 - RING))
                elif g * GROUP + j >= RING:
                    g0, j0 = divmod(g * GROUP + j - RING, GROUP)
                    if j0 in slots_of_pe(g0):
                        pool.wait_ge(v_free, pe_before(g0) + slots_of_pe(g0).index(j0) + 1)
                    else:
                        pool.wait_ge(v_taken, len(VECTOR_SLOTS) * g0 + VECTOR_SLOTS.index(j0) + 1)
                gather(peer_v, v_ring, v_landed, idx_v[:, par, :], j, looped)

            for g in range(UNROLLED):
                pool.wait_ge(selected, select_number[g] + 1)
                copy_indices(g, idx_u[:, g % 2, :], max(2 * g, 1))
                if g:
                    copy_indices(g - 1, idx_v[:, (g - 1) % 2, :], 2 * g + 1)
                for j in range(GROUP):
                    gather_u(g, g % 2, j)
                    if g:
                        gather_v(g - 1, (g - 1) % 2, j)
            pool.wait_ge(selected, GROUPS)
            with pool.Fori(0, (GROUPS - UNROLLED) // 2) as p:
                for par in range(2):
                    g = p * 2 + (UNROLLED + par)
                    copy_indices(g, idx_u[:, par, :], g * 2, True)
                    copy_indices(g - 1, idx_v[:, 1 - par, :], g * 2 + 1, True)
                    for j in range(GROUP):
                        gather_u(g, par, j, True)
                        gather_v(g - 1, 1 - par, j, True)
            g = GROUPS - 1
            copy_indices(g, idx_v[:, 1, :], 2 * GROUPS)
            for j in range(GROUP):
                gather_v(g, 1, j)

        @block.tensor
        def _(pe):
            def take_bank(job):
                n = jobs[job]
                if n >= BANKS:
                    pe.wait_ge(bank_used[n % BANKS], n // BANKS)
                return bank_of(job)

            def done(ins, job):
                ins.then_inc(bank_full[jobs[job] % BANKS], 1)

            def front(item):
                kind = item[0]
                w = weight_piece(item)
                if w:
                    pe.wait_ge(w_loaded[pieces[w] % 2], 16 * (pieces[w] // 2 + 1))
                if kind == "norm" and item[1] < 10:
                    n = item[1]
                    t = n % 5
                    src = h_tmp[:, t % 2, :] if n < 5 else h2_of(t)
                    pe.wait_ge(normed, n + 1)
                    for half in range(2):
                        job = ("nt", n, half)
                        ps = take_bank(job)
                        for b in range(4):
                            k = 4 * half + b
                            mm = nc.tensor.transpose(ps[:, P * b:P * b + ROWS[t]], src[0:ROWS[t], P * k:P * k + P],
                                                     ident[0:ROWS[t], 0:ROWS[t]])
                        done(mm, job)
                elif kind == "proj":
                    _, n, t = item
                    used(pe, ("nt", t, 1))
                    ps = take_bank(item)
                    wv = piece_ap(w).rearrange("p (k n) -> p k n", k=KC)
                    for k in range(KC):
                        mm = nc.tensor.matmul(ps[0:ROWS[t], 0:PC],
                                              hT[part_of(t)][:, k, column_of(t):column_of(t) + ROWS[t]],
                                              wv[:, k, :], start=(k == 0), stop=(k == KC - 1))
                    done(mm, item)
                elif kind == "forget":
                    t = item[1]
                    if t == 0:
                        pe.wait_ge(cache_loaded, 16 * 9)
                    used(pe, ("nt", t, 1))
                    ps = take_bank(item)
                    for k in range(KC):
                        mm = nc.tensor.matmul(ps[0:ROWS[t], 0:HEADS],
                                              hT[part_of(t)][:, k, column_of(t):column_of(t) + ROWS[t]],
                                              w_f[:, k, :], start=(k == 0), stop=(k == KC - 1))
                    done(mm, item)
                elif kind == "tr":
                    _, c, t = item
                    for n, (name, _half) in enumerate(PROJ):
                        if name == c and c in ("qa", "kv"):
                            pe.wait_ge(roped, rope_number[("proj", n, t)] + 1)
                        elif name == c:
                            used(pe, ("proj", n, t))
                    ps = take_bank(item)
                    src = stage[:, staged_number[(c, t)] % STAGES, :]
                    for b in range(1 if c == "kv" else 4):
                        mm = nc.tensor.transpose(ps[:, P * b:P * b + ROWS[t]], src[0:ROWS[t], P * b:P * b + P],
                                                 ident[0:ROWS[t], 0:ROWS[t]])
                    done(mm, item)
                elif kind == "cumulate":
                    pe.wait_ge(logf_step, 5)
                    ps = take_bank(("cumulate", 0))
                    for i in range(4):
                        mm = nc.tensor.matmul(ps[0:HEADS, 0:SEQ], logf[:, i, :], tri[:, 384 - P * i:384 - P * i + SEQ],
                                              start=(i == 0), stop=(i == 3))
                    done(mm, ("cumulate", 0))
                    ps = take_bank(("cumulate", 1))
                    n = PAST + DEC
                    for i in range(3):
                        r = P if i < 2 else DEC
                        src = cache_f[:, i, :] if i < 2 else logf[0:DEC, 4, :]
                        mm = nc.tensor.matmul(ps[0:HEADS, 0:n], src, tri[0:r, 384 - P * i:384 - P * i + n],
                                              start=(i == 0), stop=(i == 2))
                    done(mm, ("cumulate", 1))
                elif kind == "att":
                    attention(item)
                elif kind == "ytr":
                    _, t, br = item
                    pe.wait_ge(y_ready, branch_number(t, br) + 1)
                    ps = take_bank(item)
                    for b in range(4):
                        mm = nc.tensor.transpose(ps[:, P * b:P * b + ROWS[t]], y_rows[0:ROWS[t], P * b:P * b + P],
                                                 ident[0:ROWS[t], 0:ROWS[t]])
                    done(mm, item)
                elif kind == "gate":
                    _, part, m, w4 = item
                    n = TOKENS[part]
                    if m == 0 and w4 == 0:
                        for t, br in branches(part):
                            used(pe, ("ytr", t, br))
                    ps = take_bank(item)
                    piece = piece_ap(w)
                    if w4 < 2:
                        wv = piece[:, 0:KC * P].rearrange("p (k n) -> p k n", k=KC)
                        for k in range(KC):
                            mm = nc.tensor.matmul(ps[:, 0:n], wv[:, k, :], hT[part][:, k, :],
                                                  start=(k == 0), stop=(k == KC - 1))
                    else:
                        wv = piece[:, KC * P:(KC + 4) * P].rearrange("p (k n) -> p k n", k=4)
                        for k in range(4):
                            mm = nc.tensor.matmul(ps[:, 0:n], wv[:, k, :], qT[part][:, 4 * (w4 - 2) + k, :],
                                                  start=(k == 0), stop=(k == 3))
                    done(mm, item)
                elif kind == "wout":
                    _, part, q, t = item
                    pe.wait_ge(mixed_ready, KC if part == "A" else 3 * KC)
                    ps = take_bank(item)
                    wv = piece_ap(w).rearrange("p (k n) -> p k n", k=KC)
                    for k in range(KC):
                        mm = nc.tensor.matmul(ps[:, 0:256], mixed[:, k, column_of(t):column_of(t) + P], wv[:, k, :],
                                              start=(k == 0), stop=(k == KC - 1))
                    done(mm, item)
                elif kind == "query":
                    _, part, h, p2 = item
                    n = TOKENS[part]
                    if h == 0 and p2 == 0:
                        for t in PART[part]:
                            used(pe, ("nt", 5 + t, 1))
                    ps = take_bank(item)
                    wv = piece_ap(w).rearrange("p (k n) -> p k n", k=KC)
                    for k in range(KC):
                        mm = nc.tensor.matmul(ps[:, 0:n], wv[:, k, P * p2:P * p2 + P], hT[part][:, k, :],
                                              start=(k == 0), stop=(k == KC - 1))
                    done(mm, item)
                elif kind == "even":
                    h = 2 * item[1]
                    used(pe, ("query", "B", h, 1))
                    ps = take_bank(item)
                    for p2 in range(2):
                        mm = nc.tensor.matmul(ps[0:DEC, P * p2:P * p2 + P], q_even[:, p2, :], keysT[:, 2 * h + p2, :],
                                              start=True, stop=True)
                    done(mm, item)
                elif kind == "score":
                    t, h = group_place(item[1])
                    h += t == 4
                    if item[1] == 0:
                        pe.wait_ge(keys_loaded, 16)
                    used(pe, ("query", part_of(t), h, 1))
                    ps = take_bank(item)
                    for p2 in range(2):
                        q = q_odd[:, p2, :] if t == 4 else qp[:, h % 2, p2, column_of(t):column_of(t) + P]
                        mm = nc.tensor.matmul(ps[:, P * p2:P * p2 + P], q, keysT[:, 2 * h + p2, :],
                                              start=True, stop=True)
                    done(mm, item)

            def attention(item):
                _, part, v = item
                us = units(part)
                if v < len(us):
                    t, br, h = us[v]
                    r, c = ROWS[t], column_of(t)
                    kT, first, blocks = key_span(t, br)
                    n = sum(b[0] for b in blocks)
                    if v == 0:
                        for pt in PART[part]:
                            for cc in STAGED:
                                used(pe, ("tr", cc, pt))
                            for piece in (7, 8):
                                used(pe, ("proj", piece, pt))
                        used(pe, ("cumulate", 1))
                    job = ("scores", t, br, h)
                    ps = take_bank(job)
                    if br == "swa":
                        lo = HD * (h // GRP)
                        mm = nc.tensor.matmul(ps[0:r, 0:n], qT[part][lo:lo + HD, h % GRP, c:c + r],
                                              kT[lo:lo + HD, first:first + n], start=True, stop=True)
                    else:
                        lo = HD * (h % 2)
                        nc.tensor.matmul(ps[0:r, 0:n], qT[part][lo:lo + HD, 4 + h // 2, c:c + r],
                                         kT[lo:lo + HD, h // 2, 0:n], start=True, stop=False)
                        fs = negF_s if t == 4 else negF
                        mm = nc.tensor.matmul(ps[0:r, 0:n], ident[0:HEADS, h:h + 1].broadcast_to([HEADS, r]),
                                              fs[:, 0:n], start=False, stop=True)
                    done(mm, job)
                if 0 <= v - 1 < len(us):
                    t, br, h = us[v - 1]
                    r = ROWS[t]
                    job = ("pt", t, br, h)
                    used(pe, ("scores", t, br, h))
                    ps = take_bank(job)
                    for b, (kn, _v) in enumerate(key_span(t, br)[2]):
                        mm = nc.tensor.transpose(ps[0:kn, P * b:P * b + r], probs[0:r, P * b:P * b + kn],
                                                 ident[0:r, 0:r])
                    done(mm, job)
                if 0 <= v - 2 < len(us):
                    t, br, h = us[v - 2]
                    r = ROWS[t]
                    job = ("values", t, br, h)
                    used(pe, ("pt", t, br, h))
                    ps = take_bank(job)
                    blocks = key_span(t, br)[2]
                    col = HD * (h // GRP if br == "swa" else h)
                    for b, (kn, values) in enumerate(blocks):
                        mm = nc.tensor.matmul(ps[0:r, 0:HD], probsT[0:kn, P * b:P * b + r],
                                              values[:, col:col + HD], start=(b == 0), stop=(b == len(blocks) - 1))
                    done(mm, job)

            def expert_sum(g, par, j):
                mine = slots_of_pe(g) if isinstance(g, int) else range(GROUP)
                if j not in mine:
                    return
                n = mine.index(j)
                if n == 0:
                    pe.wait_ge(collected, g + 1)
                pe.wait_ge(diag_ready, pe_before(g) + (n + 1))
                pe.wait_ge(v_landed[j % RING], g * (2 * 16) + 16 * (j // RING + 1))
                for c in range(2):
                    mm = nc.tensor.matmul(summed[par][c][:], diag[:, n % DIAGS, :],
                                          v_ring[:, j % RING, 512 * c:512 * c + 512],
                                          start=(n == 0), stop=(j == mine[-1]))
                mm.then_inc(v_free, 1)

            pe.wait_ge(const_loaded, 16)
            for item in before:
                front(item)
            for s in range(UNROLLED):
                for j in range(GROUP):
                    if s:
                        expert_sum(s - 1, (s - 1) % 2, j)
                    for item in slots.get((s, j), ()):
                        front(item)
            with pe.Fori(0, (GROUPS - UNROLLED) // 2) as p:
                for par in range(2):
                    for j in range(GROUP):
                        expert_sum(p * 2 + (UNROLLED - 1 + par), 1 - par, j)
            for j in range(GROUP):
                expert_sum(GROUPS - 1, 1, j)

        @block.scalar
        def _(act):
            def copy_out(job, dst, src, scale=1.0):
                nc.scalar.activation(dst, src, ACT.Copy, scale=scale).then_inc(release(job), 1)

            def front(item):
                kind = item[0]
                if kind == "norm":
                    n = item[1]
                    t = n % 5
                    r = ROWS[t] if n < 5 else P
                    if n < 5:
                        act.wait_ge(x_tmp_loaded[t % 2], 16 * (t // 2 + 1))
                        if n >= 2:
                            full(act, ("nt", n - 2, 1))
                        src, dst = x_tmp[0:r, t % 2, :], h_tmp[0:r, t % 2, :]
                    else:
                        if n < 10:
                            used(act, ("wout", part_of(t), 3, t))
                        else:
                            last = [g for g in range(GROUPS) if group_place(g)[0] == t][-1]
                            act.wait_ge(collected, 2 + last + 1)
                            act.wait_ge(v_taken, len(VECTOR_SLOTS) * GROUPS_A)
                        src, dst = x_of(t), h2_of(t)
                    nc.scalar.activation(dst, src, ACT.Square, accum_out=stat[0:r, 0, n:n + 1]).then_inc(
                        squares_summed, 1)
                    act.wait_ge(mean_ready, n + 1)
                    nc.scalar.activation(stat[0:r, 2, n:n + 1], stat[0:r, 1, n:n + 1], ACT.Sqrt).then_inc(
                        root_ready, 1)
                    if n < 10:
                        c = column_of(t)
                        for half in range(2):
                            job = ("nt", n, half)
                            full(act, job)
                            src = bank_of(job)[:].rearrange("p (b n) -> p b n", b=4)[:, :, 0:ROWS[t]]
                            copy_out(job, hT[part_of(t)][:, 4 * half:4 * half + 4, c:c + ROWS[t]], src)
                elif kind == "proj":
                    _, n, t = item
                    c, half = PROJ[n]
                    r = ROWS[t]
                    if c == "vb":
                        full(act, item)
                        copy_out(item, vb[0:r, t, PC * half:PC * half + PC], bank_of(item)[0:r, 0:PC])
                        if half:
                            used(act, item)
                            dst = p_fox_v[P * t:P * t + P, :] if t < 4 else s_fox_v
                            act.dma_start(dst, vb[0:r, t, :]).then_inc(outputs_stored, 16)
                elif kind == "tr":
                    _, c, t = item
                    r = ROWS[t]
                    b = staged_number[(c, t)] % STAGES
                    full(act, item)
                    if c == "kb":
                        dst = p_fox_k[P * t:P * t + P, :] if t < 4 else s_fox_k
                        act.dma_start(dst, stage[0:r, b, :]).then_inc(stage_stored[b], 16)
                    if c == "kv" and t >= 3:
                        dst = p_swa_k if t == 3 else s_swa_k[WINDOW - DEC:WINDOW, :]
                        act.dma_start(dst, stage[0:r, b, 0:P]).then_inc(stage_stored[b], 16)
                        used(act, ("proj", 2, t))
                        dst = p_swa_v if t == 3 else s_swa_v[WINDOW - DEC:WINDOW, :]
                        act.dma_start(dst, va[0:r, t, :]).then_inc(outputs_stored, 16)
                    src = bank_of(item)[:].rearrange("p (b n) -> p b n", b=4)[:, :, 0:r]
                    if c in ("qa", "qb"):
                        first = 4 * (c == "qb")
                        copy_out(item, qT[part_of(t)][:, first:first + 4, column_of(t):column_of(t) + r], src, SCALE)
                    elif c == "kv":
                        dst = kaT[:, P * t:P * t + P] if t < 4 else kaT_s[:, WINDOW:WINDOW + DEC]
                        copy_out(item, dst, bank_of(item)[:, 0:r])
                    else:
                        dst = kbT[:, :, P * t:P * t + P] if t < 4 else kbT_s[:, :, PAST:PAST + DEC]
                        copy_out(item, dst, src)
                elif kind == "logf":
                    act.wait_ge(logf_step, 1)
                    nc.scalar.activation(f_tmp[:, 2, :], f_tmp[:, 1, :], ACT.Exp).then_inc(logf_step, 1)
                    act.wait_ge(logf_step, 3)
                    nc.scalar.activation(f_tmp[:, 4, :], f_tmp[:, 3, :], ACT.Ln).then_inc(logf_step, 1)
                    act.wait_ge(logf_step, 5)
                    act.dma_start(p_logf.rearrange("(t p) h -> p t h", p=P), logf[:, 0:4, :]).then_inc(
                        outputs_stored, 16)
                    act.dma_start(s_logf, logf[0:DEC, 4, :]).then_inc(outputs_stored, 16)
                elif kind == "att":
                    _, part, v = item
                    us = units(part)
                    if v < len(us):
                        t, br, h = us[v]
                        r = ROWS[t]
                        b = branch_number(t, br)
                        n = sum(x[0] for x in key_span(t, br)[2])
                        job = ("scores", t, br, h)
                        act.wait_ge(rowmax_ready, unit_number(t, br, h) + 1)
                        bias = negm[0:r, b % 2, h:h + 1]
                        if br == "swa":
                            nc.scalar.activation(sink_e[0:r, b % 2, h:h + 1], sink[0:r, h:h + 1], ACT.Exp, bias=bias)
                        if v > 0:
                            full(act, ("pt",) + us[v - 1])
                        nc.scalar.activation(probs[0:r, 0:n], bank_of(job)[0:r, 0:n], ACT.Exp, bias=bias,
                                             accum_out=lsum[0:r, b % 2, h:h + 1]).then_inc(release(job), 1)
                    if 0 <= v - 1 < len(us):
                        t, br, h = us[v - 1]
                        job = ("pt", t, br, h)
                        full(act, job)
                        if v - 2 >= 0:
                            full(act, ("values",) + us[v - 2])
                        blocks = key_span(t, br)[2]
                        whole = [b for b in blocks if b[0] == P]
                        src = bank_of(job)
                        if ROWS[t] == P:
                            copy_out(job, probsT[:, 0:P * len(blocks)], src[:, 0:P * len(blocks)])
                        else:
                            nw = len(whole)
                            nc.scalar.activation(
                                probsT[:, 0:P * nw].rearrange("p (b n) -> p b n", b=nw)[:, :, 0:DEC],
                                src[:, 0:P * nw].rearrange("p (b n) -> p b n", b=nw)[:, :, 0:DEC], ACT.Copy)
                            copy_out(job, probsT[0:DEC, P * nw:P * nw + DEC], src[0:DEC, P * nw:P * nw + DEC])
                elif kind == "ytr":
                    _, t, br = item
                    first = 4 * (br == "fox")
                    full(act, item)
                    src = bank_of(item)[:].rearrange("p (b n) -> p b n", b=4)[:, :, 0:ROWS[t]]
                    copy_out(item, qT[part_of(t)][:, first:first + 4, column_of(t):column_of(t) + ROWS[t]], src)
                elif kind == "gate" and item[3] < 2:
                    _, part, m, w4 = item
                    n = TOKENS[part]
                    full(act, item)
                    if m > 0:
                        used(act, ("gate", part, m - 1, w4 + 2))
                    nc.scalar.activation(gate_sig[:, w4, 0:n], bank_of(item)[:, 0:n], ACT.Sigmoid).then_inc(
                        release(item), 1)
                elif kind == "query":
                    _, part, h, p2 = item
                    full(act, item)
                    if part == "B":
                        dst = q_even[:, p2, :] if h % 2 == 0 else q_odd[:, p2, DEC:P]
                        nc.scalar.activation(dst, bank_of(item)[:, 256:320], ACT.Copy)
                    copy_out(item, qp[:, h % 2, p2, :], bank_of(item)[:, 0:256])
                elif kind == "even":
                    n = paired.index(GROUPS_A + 2 * HEADS + item[1])
                    if n:
                        act.wait_ge(selected, select_number[paired[n - 1]] + 1)
                    full(act, item)
                    copy_out(item, s_pair[0:DEC, :], bank_of(item)[0:DEC, 0:2 * NSUB])
                elif kind == "score":
                    g = item[1]
                    full(act, item)
                    if group_place(g)[0] == 4:
                        copy_out(item, s_pair[DEC:P, :], bank_of(item)[DEC:P, 0:2 * NSUB])
                    else:
                        i = plain.index(g)
                        if i >= 2:
                            act.wait_ge(selected, select_number[plain[i - 2]] + 1)
                        copy_out(item, s_ring[:, i % 2, :], bank_of(item)[:, 0:2 * NSUB])
                elif kind == "weights":
                    act.wait_ge(best_ready, select_number[item[1]] + 1)
                    nc.scalar.activation(best_e[:], best[:], ACT.Exp, bias=small[:, 0:1],
                                         accum_out=small[:, 1:2]).then_inc(exp_ready, 1)

            def gelu(g, par):
                act.wait_ge(u_free, g * GROUP + (RING + GROUP))
                nc.scalar.activation(gelu_sb[:, par, :], dots_sb[:, par, :], ACT.Gelu).then_inc(gelu_ready, 1)

            def diagonal(g, par, n, fold_of):
                if n == 0:
                    act.wait_ge(weights_ready, g + 1)
                if not isinstance(g, int) or pe_before(g) + n >= DIAGS:
                    act.wait_ge(v_free, pe_before(g) + (n + 1 - DIAGS))
                if not isinstance(g, int):
                    act.sem_inc(paced_scalar, 1)
                j = slots_of_pe(g)[n] if isinstance(g, int) else n
                nc.scalar.activation(diag[:, n % DIAGS, :], fold[:, fold_of, :], ACT.Copy,
                                     scale=weights_sb[:, par, j:j + 1]).then_inc(diag_ready, 1)

            act.wait_ge(const_loaded, 16)
            for item in before:
                front(item)
            for s in range(UNROLLED):
                made = 0
                if s:
                    gelu(s - 1, (s - 1) % 2)
                for j in range(GROUP):
                    while s and made < len(slots_of_pe(s - 1)) and slots_of_pe(s - 1)[made] < j + DIAGS - 1:
                        diagonal(s - 1, (s - 1) % 2, made, 0)
                        made += 1
                    for item in slots.get((s, j), ()):
                        front(item)
            with act.Fori(0, (GROUPS - UNROLLED) // 2) as p:
                for par in range(2):
                    g = p * 2 + (UNROLLED - 1 + par)
                    gelu(g, 1 - par)
                    for j in range(GROUP):
                        diagonal(g, 1 - par, j, g // 32)
            gelu(GROUPS - 1, 1)
            for j in range(GROUP):
                diagonal(GROUPS - 1, 1, j, 1)
            for item in finals:
                front(item)
            act.wait_ge(outputs_stored, 16 * (2 + 5 + 2 + 2))
            for b in range(STAGES):
                act.wait_ge(stage_stored[b], stores_of_stage(b))

        @block.vector
        def _(dve):
            chain = [0]

            def step(ins):
                chain[0] += 1
                ins.then_inc(vector_chain, 1)
                return chain[0]

            def behind(n):
                dve.wait_ge(vector_chain, n)

            def front(item):
                kind = item[0]
                if kind == "norm":
                    n = item[1]
                    t = n % 5
                    r = ROWS[t] if n < 5 else P
                    src, dst = (x_tmp[0:r, t % 2, :], h_tmp[0:r, t % 2, :]) if n < 5 else (x_of(t), h2_of(t))
                    dve.wait_ge(squares_summed, n + 1)
                    nc.vector.tensor_scalar(stat[0:r, 1, n:n + 1], stat[0:r, 0, n:n + 1], 1.0 / D, EPS,
                                            ALU.mult, ALU.add).then_inc(mean_ready, 1)
                    dve.wait_ge(root_ready, n + 1)
                    mean, inv, tmp = (stat[0:r, i, n:n + 1] for i in (1, 3, 2))
                    behind(step(nc.vector.reciprocal(inv, tmp)))
                    behind(step(nc.vector.scalar_tensor_tensor(tmp, inv, inv, mean, ALU.mult, ALU.mult)))
                    behind(step(nc.vector.tensor_scalar(tmp, tmp, -0.5, 1.5, ALU.mult, ALU.add)))
                    behind(step(nc.vector.tensor_tensor(inv, inv, tmp, ALU.mult)))
                    dve.wait_ge(g_loaded, 16 * (n // 5 + 1))
                    nc.vector.scalar_tensor_tensor(dst, src, stat[0:r, 3, n:n + 1], g_row[0:r, :],
                                                   ALU.mult, ALU.mult).then_inc(normed, 1)
                elif kind == "proj":
                    project(item)
                elif kind == "forget":
                    t = item[1]
                    full(dve, item)
                    nc.vector.tensor_copy(raw_f[0:ROWS[t], t, :], bank_of(item)[0:ROWS[t], 0:HEADS]).then_inc(
                        release(item), 1)
                elif kind == "logf":
                    z, na, e, u, ln, w = (f_tmp[:, i, :] for i in range(6))
                    z3 = z.rearrange("p (t h) -> p t h", t=TILES)
                    dve.wait_ge(cache_loaded, 16 * 9)
                    used(dve, ("forget", TILES - 1))
                    behind(step(nc.vector.tensor_tensor(z3, raw_f[:], bias_f[:].unsqueeze(1).broadcast_to(
                        [P, TILES, HEADS]), ALU.add)))
                    nc.vector.scalar_tensor_tensor(na, z, -1.0, z, ALU.mult, ALU.min).then_inc(logf_step, 1)
                    dve.wait_ge(logf_step, 2)
                    nc.vector.tensor_scalar(u, e, 1.0, None, ALU.add).then_inc(logf_step, 1)
                    dve.wait_ge(logf_step, 4)
                    behind(step(nc.vector.tensor_scalar(w, u, 1.0, None, ALU.is_equal)))
                    step(nc.vector.tensor_tensor(ln, ln, w, ALU.add))
                    behind(step(nc.vector.scalar_tensor_tensor(w, u, -1.0, w, ALU.add, ALU.add)))
                    behind(step(nc.vector.reciprocal(u, w)))
                    behind(step(nc.vector.tensor_tensor(ln, ln, u, ALU.mult)))
                    behind(step(nc.vector.tensor_tensor(ln, ln, e, ALU.mult)))
                    nc.vector.scalar_tensor_tensor(logf[:].rearrange("p t h -> p (t h)"), z, 0.0, ln,
                                                   ALU.min, ALU.subtract).then_inc(logf_step, 1)
                    behind(step(nc.vector.tensor_scalar(neg_sink[:], sink[:], -1.0, None, ALU.mult)))
                elif kind == "cumulate":
                    for i, dst in ((0, negF), (1, negF_s)):
                        job = ("cumulate", i)
                        full(dve, job)
                        nc.vector.tensor_scalar(dst[:], bank_of(job)[0:HEADS, 0:dst.shape[1]], -1.0, None,
                                                ALU.mult).then_inc(release(job), 1)
                elif kind == "att":
                    attention(item)
                elif kind == "ytr":
                    _, t, br = item
                    r = ROWS[t]
                    b = branch_number(t, br) % 2
                    used(dve, ("values", t, br, HEADS - 1))
                    if br == "swa":
                        behind(step(nc.vector.tensor_tensor(lsum[0:r, b, :], lsum[0:r, b, :], sink_e[0:r, b, :],
                                                            ALU.add)))
                    behind(step(nc.vector.reciprocal(rinv[0:r, :], lsum[0:r, b, :])))
                    yv = y_rows[0:r, :].rearrange("p (h d) -> p h d", h=HEADS)
                    nc.vector.tensor_tensor(yv, yv, rinv[0:r, :].unsqueeze(2).broadcast_to([r, HEADS, HD]),
                                            ALU.mult).then_inc(y_ready, 1)
                elif kind == "gate" and item[3] >= 2:
                    _, part, m, w4 = item
                    n = TOKENS[part]
                    ready = m if part == "A" else KC + 2 * m
                    full(dve, item)
                    if m == 0 and w4 == 2:
                        upto = len(STAGED) * (2 if part == "A" else TILES)
                        for b in range(STAGES):
                            if stores_of_stage(b, upto):
                                dve.wait_ge(stage_stored[b], stores_of_stage(b, upto))
                    used(dve, ("gate", part, m, w4 - 2))
                    if w4 == 2 and ready:
                        dve.wait_ge(mixed_ready, ready)
                    nc.vector.tensor_tensor(gate_tmp[:, w4 - 2, 0:n], bank_of(item)[:, 0:n],
                                            gate_sig[:, w4 - 2, 0:n], ALU.mult).then_inc(release(item), 1)
                    if w4 == 3:
                        used(dve, item)
                        nc.vector.tensor_tensor(mixed[:, m, 0:n], gate_tmp[:, 0, 0:n], gate_tmp[:, 1, 0:n],
                                                ALU.add).then_inc(mixed_ready, 1)
                        if part == "B":
                            nc.vector.tensor_tensor(mixed[:, m, 320:384], gate_tmp[:, 0, 256:320],
                                                    gate_tmp[:, 1, 256:320], ALU.add).then_inc(mixed_ready, 1)
                elif kind == "wout":
                    _, part, q, t = item
                    full(dve, item)
                    dve.wait_ge(x_loaded, 16 * (2 if part == "A" else 6))
                    xv = x_of(t)[:, 256 * q:256 * q + 256]
                    nc.vector.tensor_tensor(xv, xv, bank_of(item)[:, 0:256], ALU.add).then_inc(release(item), 1)
                elif kind in ("halves", "sums", "places", "weights"):
                    select(kind, item[1])

            def project(item):
                _, n, t = item
                c, half = PROJ[n]
                if c == "vb":
                    return
                r = ROWS[t]
                ps = bank_of(item)
                number = staged_number[(c, t)]
                full(dve, item)
                if half == 0 and number >= STAGES:
                    full(dve, ("tr",) + staged[number - STAGES])
                    stored = stores_of_stage(number % STAGES, number)
                    if stored:
                        dve.wait_ge(stage_stored[number % STAGES], stored)
                dst = stage[0:r, number % STAGES, :]
                if c in ("qb", "kb"):
                    nc.vector.tensor_copy(dst[:, PC * half:PC * half + PC], ps[0:r, 0:PC]).then_inc(release(item), 1)
                    return
                heads = GRP if c == "qa" else KV
                w = heads * HD
                if rope_number[item]:
                    dve.wait_ge(roped, rope_number[item])
                if c == "kv":
                    nc.vector.tensor_copy(va[0:r, t, :], ps[0:r, w:2 * w])

                def table(a):
                    return a[0:r, t, :].unsqueeze(1).broadcast_to([r, 2 * heads, HD // 2])

                def halves(a):
                    return a[0:r, 0:w].rearrange("p (a b) -> p a b", b=HD // 2)

                nc.vector.tensor_tensor(halves(rope_c), halves(ps), table(cos), ALU.mult)
                nc.vector.tensor_tensor(halves(rope_s), halves(ps), table(sin), ALU.mult).then_inc(release(item), 1)
                used(dve, item)
                cv, sv = (a[0:r, 0:w].rearrange("p (i d) -> p i d", d=HD) for a in (rope_c, rope_s))
                if c == "qa":
                    out = dst.rearrange("p (i k d) -> p i k d", i=GRP, k=KV)[:, :, half, :]
                else:
                    out = dst[:, 0:w].rearrange("p (i d) -> p i d", d=HD)
                lo, hi = slice(0, HD // 2), slice(HD // 2, HD)
                nc.vector.tensor_tensor(out[:, :, lo], cv[:, :, lo], sv[:, :, hi], ALU.subtract)
                nc.vector.tensor_tensor(out[:, :, hi], cv[:, :, hi], sv[:, :, lo], ALU.add).then_inc(roped, 1)

            def attention(item):
                _, part, v = item
                us = units(part)
                if v < len(us):
                    t, br, h = us[v]
                    r = ROWS[t]
                    b = branch_number(t, br) % 2
                    n = sum(x[0] for x in key_span(t, br)[2])
                    job = ("scores", t, br, h)
                    ps = bank_of(job)
                    dst = negm[0:r, b, h:h + 1]
                    full(dve, job)
                    if br == "swa":
                        if t == 0:
                            behind(step(nc.vector.memset(ps[0:HD, HD:P], MASKED)))
                        elif t < 4:
                            step(nc.vector.memset(ps[0:HD, 3 * HD:4 * HD], MASKED))
                            behind(step(nc.vector.memset(ps[HD:P, 0:HD], MASKED)))
                        behind(step(nc.vector.tensor_reduce(dst, ps[0:r, 0:n], AX_X, ALU.max, negate=True)))
                        nc.vector.tensor_tensor(dst, dst, neg_sink[0:r, h:h + 1], ALU.min).then_inc(rowmax_ready, 1)
                    else:
                        last = ps[0:r, n - r:n]
                        behind(step(nc.vector.tensor_tensor(last, last, causal[0:r, 0:r], ALU.add)))
                        nc.vector.tensor_reduce(dst, ps[0:r, 0:n], AX_X, ALU.max, negate=True).then_inc(
                            rowmax_ready, 1)
                if 0 <= v - 2 < len(us):
                    t, br, h = us[v - 2]
                    r = ROWS[t]
                    job = ("values", t, br, h)
                    full(dve, job)
                    if h == 0 and v - 2 > 0:
                        full(dve, ("ytr",) + us[v - 3][0:2])
                    nc.vector.tensor_copy(y_rows[0:r, HD * h:HD * h + HD], bank_of(job)[0:r, 0:HD]).then_inc(
                        release(job), 1)

            def select(part, g):
                pair = group_place(g)[0] == 4
                s = s_pair if pair else s_ring[:, plain.index(g) % 2, :]
                half = [s[:, NSUB * i:NSUB * i + NSUB] for i in range(2)]
                flat = cand[:].rearrange("p a b -> p (a b)")
                cols = slice(g * GROUP, g * GROUP + GROUP)
                behind(chain[0])
                if part == "halves":
                    used(dve, ("score", g))
                    if pair:
                        used(dve, ("even", (g - GROUPS_A - 2 * HEADS)))
                    n = [step(nc.vector.max(top[:, i, 0:8], half[i])) for i in range(2)]
                    for i in range(2):
                        behind(n[i])
                        n[i] = step(nc.vector.max_index(top_u[:, i, 0:8], top[:, i, 0:8], half[i]))
                    for i in range(2):
                        behind(n[i])
                        n[i] = step(nc.vector.match_replace(half[i], top[:, i, 0:8], half[i], REPLACED))
                    for i in range(2):
                        behind(n[i])
                        n[i] = step(nc.vector.max(top[:, i, 8:16], half[i]))
                    for i in range(2):
                        behind(n[i])
                        n[i] = step(nc.vector.max_index(top_u[:, i, 8:16], top[:, i, 8:16], half[i]))
                elif part == "sums":
                    a = step(nc.vector.tensor_tensor(
                        cand[:], top[:, 0, :].unsqueeze(2).broadcast_to([P, TOPK, TOPK]),
                        top[:, 1, :].unsqueeze(1).broadcast_to([P, TOPK, TOPK]), ALU.add))
                    step(nc.vector.tensor_copy(top_f[:], top_u[:]))
                    behind(a)
                    behind(step(nc.vector.max(best[:, 0:8], flat)))
                    behind(step(nc.vector.max_index(place_u[:, 0, 0:8], best[:, 0:8], flat)))
                    behind(step(nc.vector.match_replace(flat, best[:, 0:8], flat, REPLACED)))
                    behind(step(nc.vector.max(best[:, 8:16], flat)))
                    nc.vector.tensor_scalar(small[:, 0:1], best[:, 0:1], -1.0, None, ALU.mult).then_inc(best_ready, 1)
                    step(nc.vector.max_index(place_u[:, 0, 8:16], best[:, 8:16], flat))
                elif part == "places":
                    step(nc.vector.tensor_scalar(place_u[:, 1, :], place_u[:, 0, :], 4, None,
                                                 ALU.logical_shift_right))
                    behind(step(nc.vector.tensor_scalar(place_u[:, 2, :], place_u[:, 0, :], TOPK - 1, None,
                                                        ALU.bitwise_and)))
                    behind(step(nc.vector.tensor_copy(place_f[:], place_u[:, 1:3, :])))
                    for i in range(2):
                        behind(step(nc.vector.tensor_tensor(
                            onehot[:], place_f[:, i, :].unsqueeze(2).broadcast_to([P, TOPK, TOPK]),
                            iota.unsqueeze(1).broadcast_to([P, TOPK, TOPK]), ALU.is_equal)))
                        behind(step(nc.vector.tensor_tensor(
                            onehot[:], onehot[:], top_f[:, i, :].unsqueeze(1).broadcast_to([P, TOPK, TOPK]),
                            ALU.mult)))
                        behind(step(nc.vector.tensor_reduce(picked[:, i, :], onehot[:], AX_X, ALU.add)))
                    step(nc.vector.scalar_tensor_tensor(experts[:, cols], picked[:, 0, :], float(NSUB),
                                                        picked[:, 1, :], ALU.mult, ALU.add))
                else:
                    dve.wait_ge(exp_ready, select_number[g] + 1)
                    behind(step(nc.vector.reciprocal(small[:, 2:3], small[:, 1:2])))
                    nc.vector.tensor_scalar(gates[:, cols], best_e[:], small[:, 2:3], None, ALU.mult).then_inc(
                        selected, 1)

            def dot(g, par, j, h_rows):
                dve.wait_ge(u_landed[j % RING], g * (2 * 16) + 16 * (j // RING + 1))
                u = u_ring[:, j % RING, :]
                nc.vector.scalar_tensor_tensor(u, u, 1.0, h_rows, ALU.mult, ALU.mult,
                                               accum_out=dots_sb[:, par, j:j + 1]).then_inc(u_free, 1)

            def weigh(g, par):
                dve.wait_ge(gelu_ready, g + 1)
                nc.vector.tensor_tensor(weights_sb[:, par, :], gelu_sb[:, par, :],
                                        gates[:, bass.ds(g * GROUP, GROUP)], ALU.mult).then_inc(weights_ready, 1)

            def collect(g, par, rows):
                dve.wait_ge(v_free, pe_before(g + 1))
                dve.wait_ge(collected, g + 2)
                if isinstance(g, int) and g <= GROUPS_A:
                    early = len([j for j in VECTOR_SLOTS if j < 8]) if g + 1 < GROUPS_A else 0
                    dve.wait_ge(v_taken, len(VECTOR_SLOTS) * min(g + 1, GROUPS_A) + early)
                for c in range(2):
                    o = rows[:, 512 * c:512 * c + 512]
                    ins = nc.vector.tensor_tensor(o, o, summed[par][c][:], ALU.add)
                ins.then_inc(collected, 1)

            def add_rows(g, j, rows):
                n = len(VECTOR_SLOTS) * g + VECTOR_SLOTS.index(j)
                dve.wait_ge(weights_ready, g + 1)
                dve.wait_ge(v_landed[j % RING], g * (2 * 16) + 16 * (j // RING + 1))
                dve.wait_ge(collected, 2 + (g - 1 if j <= 8 and g else g))
                if n:
                    dve.wait_ge(v_taken, n)
                nc.vector.scalar_tensor_tensor(rows, v_ring[:, j % RING, :], weights_sb[:, g % 2, j:j + 1], rows,
                                               ALU.mult, ALU.add).then_inc(v_taken, 1)

            step(nc.vector.memset(q_odd[:], 0.0))
            step(nc.vector.memset(raw_f[:], 0.0))
            behind(chain[0])
            dve.sem_inc(u_free, RING)
            dve.sem_inc(collected, 2)
            dve.wait_ge(const_loaded, 16)
            for item in before:
                front(item)
            for s in range(UNROLLED):
                for j in range(GROUP):
                    dot(s, s % 2, j, group_h(s))
                    if j == 0 and s >= 1:
                        weigh(s - 1, (s - 1) % 2)
                    if j in VECTOR_SLOTS and 1 <= s <= GROUPS_A:
                        add_rows(s - 1, j, group_x(s - 1))
                    if j == 8 and s >= 2:
                        collect(s - 2, s % 2, group_x(s - 2))
                    for item in slots.get((s, j), ()):
                        front(item)
            with dve.Fori(0, (GROUPS - UNROLLED) // 2) as p:
                for par in range(2):
                    first = UNROLLED - GROUPS_A + par
                    for j in range(GROUP):
                        dot(p * 2 + (UNROLLED + par), par, j, group_h(None, (p * 2 + first) // HEADS))
                        if j == 0:
                            weigh(p * 2 + (UNROLLED + par - 1), 1 - par)
                        if j == 8:
                            collect(p * 2 + (UNROLLED + par - 2), par, group_x(None, (p * 2 + (first - 2)) // HEADS))
            weigh(GROUPS - 1, 1)
            collect(GROUPS - 2, 0, group_x(GROUPS - 2))
            collect(GROUPS - 1, 1, group_x(GROUPS - 1))
            for item in finals:
                front(item)


def constants():
    c = np.zeros((P, C_END), np.float32)
    c[:, C_IDENT:C_IDENT + P] = np.eye(P)
    row, col = np.arange(P)[:, None], np.arange(P)[None, :]
    c[:, C_CAUSAL:C_CAUSAL + P] = np.where(col <= row, 0.0, MASKED)
    c[:, C_FOLD:C_FOLD + P] = np.eye(P)
    c[:, C_FOLD + P:C_FOLD + 2 * P] = (row % DEC == col)
    half = HD // 2
    inv = (np.float32(10000.0) ** (-np.arange(half, dtype=np.float32) / np.float32(half))).astype(np.float32)
    for t in range(TILES):
        pos = (np.arange(P) + (P * t if t < 4 else PAST)).astype(np.float32)
        angle = (pos[:, None] * inv[None, :]).astype(np.float32)
        c[:, C_COS + half * t:C_COS + half * t + half] = np.cos(angle)
        c[:, C_SIN + half * t:C_SIN + half * t + half] = np.sin(angle)
    c[:, C_IOTA:C_IOTA + TOPK] = np.arange(TOPK)
    tri = (np.arange(TRI)[None, :] >= np.arange(P)[:, None] + 384).astype(np.float32)
    return c, tri


def kernel(x_prompt, x_sample, cache_swa_k, cache_swa_v, cache_fox_k, cache_fox_v, cache_fox_logf, g_mix, w_in,
           b_fgate, sinks, w_a_out, w_b_out, w_out, g_ffn, w_pq, peer_sub_keys, peer_u, peer_v, g_final):
    import concourse.bacc as bacc
    from concourse.bass_utils import run_bass_kernel_spmd

    def rows_in(w, k=KC):
        return np.asarray(w).reshape(k, P, -1).transpose(1, 0, 2)

    w = rows_in(w_in[0])
    c, d, e = 2304, 2312, 3336

    def cut(array, n):
        s = array.reshape(P, array.shape[1], -1, n).transpose(2, 0, 1, 3)
        return s.reshape(s.shape[0], P, -1)

    merge = [np.concatenate([cut(gate, P), cut(rows_in(out[0], 4), P)], 2)
             for gate, out in ((w[:, :, d:e], w_a_out), (w[:, :, e:], w_b_out))]

    const, tri = constants()
    arrays = {
        "x_prompt": np.asarray(x_prompt)[0], "x_sample": np.asarray(x_sample)[0],
        "w_proj": cut(w[:, :, 0:c], PC), "w_forget": w[:, :, c:d],
        "w_merge": np.stack(merge, 1).reshape(2 * KC, P, -1),
        "w_out": cut(rows_in(w_out[0]), 256), "w_pq": cut(rows_in(w_pq[0]), 256),
        "sub_keys": np.asarray(peer_sub_keys)[0].transpose(3, 0, 1, 2).reshape(P, 2 * HEADS, NSUB),
        "g_mix": np.asarray(g_mix)[0], "g_ffn": np.asarray(g_ffn)[0], "g_final": np.asarray(g_final),
        "b_fgate": np.asarray(b_fgate)[0], "sinks": np.asarray(sinks)[0],
        "swa_kT": np.asarray(cache_swa_k)[0, 0].reshape(WINDOW, P).T,
        "swa_k": np.asarray(cache_swa_k)[0, 0].reshape(WINDOW, P),
        "swa_v": np.asarray(cache_swa_v)[0, 0].reshape(WINDOW, P),
        "fox_kT": np.asarray(cache_fox_k)[0, 0].reshape(PAST, 4, P).transpose(2, 1, 0),
        "fox_v": np.asarray(cache_fox_v)[0, 0].reshape(2, P, 512).transpose(1, 0, 2),
        "fox_logf": np.asarray(cache_fox_logf)[0, 0].reshape(2, P, HEADS).transpose(1, 0, 2),
        "consts": const, "tri": tri, "peer_u": np.asarray(peer_u)[0], "peer_v": np.asarray(peer_v)[0],
    }
    arrays = {f"in_{k}": np.ascontiguousarray(v) for k, v in arrays.items()}
    outs = [(SEQ, D), (DEC, D), (WINDOW, P), (WINDOW, P), (SEQ, 512), (SEQ, 512), (SEQ, HEADS),
            (WINDOW, P), (WINDOW, P), (DEC, 512), (DEC, 512), (DEC, HEADS)]
    nc = bacc.Bacc("TRN2", target_bir_lowering=False, num_devices=1, dynamic_dma_scratch_size=8192)
    args = [nc.dram_tensor(k, v.shape, mybir.dt.from_np(v.dtype), kind="ExternalInput").ap()
            for k, v in arrays.items()]
    args += [nc.dram_tensor(f"out_{i}", s, F32, kind="ExternalOutput").ap() for i, s in enumerate(outs)]
    layer(nc, *args)
    r = run_bass_kernel_spmd(nc, [arrays], core_ids=[0]).results[0]
    shapes = [(1, SEQ, D), (1, DEC, D), (1, 1, WINDOW, KV, HD), (1, 1, WINDOW, KV, HD), (1, 1, SEQ, HEADS, HD),
              (1, 1, SEQ, HEADS, HD), (1, 1, SEQ, HEADS), (1, 1, WINDOW, KV, HD), (1, 1, WINDOW, KV, HD),
              (1, 1, DEC, HEADS, HD), (1, 1, DEC, HEADS, HD), (1, 1, DEC, HEADS)]
    return tuple(r[f"out_{i}"].reshape(s) for i, s in enumerate(shapes))
```

```python
from contextlib import ExitStack

import numpy as np

import concourse.bass as bass
from concourse import mybir

ALU = mybir.AluOpType
ACT = mybir.ActivationFunctionType
AX_X = mybir.AxisListType.X
F32 = mybir.dt.float32
U32 = mybir.dt.uint32

P = 128
D = 1024
KC = D // P
SEQ, DEC, PAST = 512, 64, 256
HD = 64
HEADS = 8
KV = 2
GRP = HEADS // KV
WINDOW = 128
SCALE = HD ** -0.5
EPS = 1e-6
MASKED = -1e30
REPLACED = -3e38
TILES = 5
ROWS = [P, P, P, P, DEC]
PART = {"A": (0, 1), "B": (2, 3, 4)}
TOKENS = {"A": 256, "B": 320}
TOPK = 16
NSUB = 128
GROUP = TOPK
RING = 8
DIAGS = 4
GROUPS_A = 2 * HEADS
GROUPS_SAMPLE = GROUPS_A + HEADS
GROUPS_LAST = GROUPS_SAMPLE + HEADS // 2
GROUPS = GROUPS_LAST + HEADS
UNROLLED, UNROLLED_SV = 24, GROUPS_LAST + 2
RATE_A, RATE_B = 1.75, 1.26
ATTENTION_COST, SELECT_COST = 1.2, 0.75
VECTOR_SLOTS, VECTOR_SLOTS_LATE, VECTOR_SLOTS_LAST = (2, 4, 7, 10, 12, 15), (7, 15), (1, 4, 7, 10, 12, 14)
NORM_TILES = (0, 1, 2, 3, 4, 0, 1, 2, 3, 4, 0, 1, 2, 4, 3)
PROJ = [("qa", 0), ("qa", 1), ("kv", 0), ("qb", 0), ("qb", 1), ("kb", 0), ("kb", 1), ("vb", 0), ("vb", 1)]
PC = 256
STAGED = ("qa", "kv", "qb", "kb")
STAGES = 4
OUTPUTS_STORED = 2 + 2 + TILES + 2
BANKS = 4
TRI = 896
C_IDENT, C_CAUSAL, C_FOLD, C_COS, C_SIN, C_IOTA, C_END = 0, 128, 256, 512, 672, 832, 848


def part_of(t):
    return "A" if t in PART["A"] else "B"


def column_of(t):
    return P * (t - PART[part_of(t)][0])


def group_place(g):
    if g < GROUPS_A:
        return g % 2, g // 2
    if g < GROUPS_SAMPLE:
        return 2, g - GROUPS_A
    return (4, 2 * (g - GROUPS_SAMPLE)) if g < GROUPS_LAST else (3, g - GROUPS_LAST)


def slots_of_dve(g):
    if g == GROUPS - 1:
        return VECTOR_SLOTS_LAST
    return () if g >= GROUPS_A else VECTOR_SLOTS if g < GROUPS_A - 3 else VECTOR_SLOTS_LATE


def slots_of_pe(g):
    return [j for j in range(GROUP) if j not in slots_of_dve(g)]


def dve_before(g):
    return sum(len(slots_of_dve(i)) for i in range(g))


def pe_before(g):
    return g * GROUP - (dve_before(g) if isinstance(g, int) else dve_before(GROUPS_A))


def diag_slot(g, n):
    return (n - dve_before(g if isinstance(g, int) else GROUPS_A)) % DIAGS


def branches(part):
    return [(t, br) for br in ("swa", "fox") for t in PART[part]]


def units(part):
    return [(t, br, h) for t, br in branches(part) for h in range(HEADS)]


def branch_number(t, br):
    return (branches("A") + branches("B")).index((t, br))


def unit_number(t, br, h):
    return branch_number(t, br) * HEADS + h


def attention_items(part):
    n = len(units(part))
    out = ([], [], [])
    for v in range(n + 2):
        here = out[0 if v < n // 2 else 1 if v < n // 2 + 2 else 2]
        here.append((("att", part, v), ATTENTION_COST))
        if v >= 9 and (v - 9) % 8 == 0:
            t_br = branches(part)[(v - 9) // 8]
            here += [(("divide",) + t_br, 0.0), (("ytr",) + t_br, 1.0)]
    return out


def gate_items(part, b):
    us = TOKENS[part] * 4 / 2400
    return [(("gate", part, m, w), us * (KC if w < 2 else KC // 2)) for m in range(KC) for w in (b, b + 2)]


def output_items(part):
    out, waiting = [], []
    for q in range(4):
        for t in PART[part]:
            out.append((("wout", part, q, t), KC * 256 * 4 / 2400))
            if q == 3:
                out.append((("norm", 5 + t), 0.0))
                out += waiting
                waiting = [(("nt", 5 + t), 2.0)]
    return out + waiting


def project_items(part):
    once = {0: [("nt", 1)], 1: [("norm", 2)], 3: [("nt", 2), ("norm", 3)], 5: [("nt", 3), ("norm", 4)],
            7: [("nt", 4)], 14: [("forget", t) for t in range(TILES)], 17: [("logf",)],
            20: [("cumulate",)]} if part == "A" else {}
    out, waiting = [], None
    for n, (c, half) in enumerate(PROJ):
        for t in PART[part]:
            out.append((("proj", n, t), KC * PC * 4 / 2400))
            if waiting:
                out.append((("tr",) + waiting, 0.5))
                if waiting == ("kv", PART[part][-1]):
                    first = len(out)
            last = half == 1 or c == "kv"
            waiting = (c, t) if last and c in STAGED else None
    early, late = out[:first], out[first:]
    for n, items in sorted(once.items(), reverse=True):
        where = early if n < first else late
        at = n + 1 if n < first else n + 1 - first
        where[at:at] = [(i, 0.5) for i in items]
    return early, late


def interleave(a, b):
    out, n = [], 0
    for k, item in enumerate(a):
        out.append(item)
        while n < len(b) * (k + 1) // len(a):
            out.append(b[n])
            n += 1
    return out


def front_items(part):
    early, late = project_items(part)
    window, change, forget = attention_items(part)
    first, second = gate_items(part, 0), gate_items(part, 1)
    return (early + interleave(late, window) + change[:-1] + first[:1] + change[-1:] +
            interleave(first[1:], forget[:-1]) + second[:1] + forget[-1:] + second[1:] + output_items(part))


def select_items(g):
    return [("score", g), ("halves", g), ("sums", g), ("places", g), ("weights", g)]


def selection_items_b():
    groups, ahead = [], {}
    for h in range(HEADS):
        new = [GROUPS_A + h, GROUPS_LAST + h] + ([GROUPS_SAMPLE + h // 2] if h % 2 else [])
        ahead[new[0]] = [(("query", "B", h, p), KC * TOKENS["B"] * 4 / 2400) for p in range(2)]
        groups += new
    cost = SELECT_COST
    out = ahead[groups[0]] + [(("score", groups[0]), cost)]
    for g, following in zip(groups, groups[1:] + [None]):
        out += [(("halves", g), cost)] + ahead.get(following, []) + [(("sums", g), cost)]
        if following:
            out.append((("score", following), cost))
        if group_place(g)[0] == 3 and group_place(g)[1] % 2 == 0:
            out.append((("even", group_place(g)[1] // 2), cost))
        out += [(("places", g), cost), (("weights", g), cost)]
    return out


def plan():
    before = [("norm", 0), ("norm", 1), ("nt", 0)] + [i for i, _ in front_items("A")]
    assert before[-2:] == [("nt", 5), ("nt", 6)]
    zero, one = select_items(0), select_items(1)
    before[-1:] = [("query0", 0, 0), ("query0", 0, 1), ("nt", 6), zero[0], ("query0", 1, 0), ("query0", 1, 1)]
    before += zero[1:3] + one[:1] + zero[3:] + one[1:]

    rest = front_items("B")
    rest += selection_items_b()
    slots = {}
    budget = 0.0
    for s in range(UNROLLED):
        for j in range(2, GROUP):
            here = slots.setdefault((s, j), [])
            if j < 4 and s % 2 == 0 and s // 2 + 1 < HEADS:
                here.append(("query", "A", s // 2 + 1, j - 2))
                budget -= KC * TOKENS["A"] * 4 / 2400
            if 5 <= j < 15 and j % 2 and s + 2 < GROUPS_A:
                here.append(select_items(s + 2)[(j - 5) // 2])
            if s in (18, 19) and j == 4:
                here.append(("norm", 10 + s - 18))
            budget = min(budget + (RATE_A if s <= GROUPS_A else RATE_B), 3.0)
            while budget > 0 and rest:
                if rest[0][0][0] == "score" and (s, j) <= (GROUPS_A - 3, 13):
                    break
                item, cost = rest.pop(0)
                here.append(item)
                budget -= cost
    slots.setdefault((UNROLLED - 1, GROUP - 1), []).extend(i for i, _ in rest)
    slots[(GROUPS_SAMPLE + 2, 4)] = [("norm", 12)]
    slots[(GROUPS_LAST + 1, 12)] = [("norm", 13)]
    return before, slots


def jobs_of(item):
    kind = item[0]
    if kind == "nt":
        return [item + (0,), item + (1,)]
    if kind in ("query0", "proj", "forget", "tr", "gate", "wout", "query", "even", "score"):
        return [item]
    if kind == "cumulate":
        return [("cumulate", 0), ("cumulate", 1)]
    if kind == "ytr":
        return [item]
    if kind == "att":
        _, part, v = item
        us = units(part)
        out = []
        if v < len(us):
            out.append(("scores",) + us[v])
        if 0 <= v - 1 < len(us):
            out.append(("pt",) + us[v - 1])
        if 0 <= v - 2 < len(us):
            out.append(("values",) + us[v - 2])
        return out
    return []


def weight_piece(item):
    if item[0] == "gate":
        return ("merge", item[1], KC * (item[3] % 2) + item[2])
    if item[0] == "wout":
        return ("wout", item[1], item[2])
    if item[0] == "query0":
        return ("query", "A", 0)
    if item[0] == "query":
        return ("query", item[1], item[2])
    if item[0] == "proj":
        return ("proj", part_of(item[2]), item[1])
    return None


def layer(nc, x_prompt, x_sample, w_proj, w_forget, w_merge, w_out, w_pq, sub_keys,
          g_mix, g_ffn, g_final, b_fgate, sinks, swa_kT, swa_k, swa_v, fox_kT, fox_v, fox_logf, consts, tri_d,
          peer_u, peer_v, y_prompt, y_sample, p_swa_k, p_swa_v, p_fox_k, p_fox_v, p_logf,
          s_swa_k, s_swa_v, s_fox_k, s_fox_v, s_logf):
    before, slots = plan()
    order = list(before)
    for s in range(UNROLLED):
        for j in range(GROUP):
            order += slots.get((s, j), [])
    jobs = {}
    for item in order:
        for job in jobs_of(item):
            jobs[job] = len(jobs)
    pieces, last_job = {}, {}
    for item in order:
        w = weight_piece(item)
        if w:
            pieces.setdefault(w, len(pieces))
            last_job[w] = jobs_of(item)[-1]
    first_of_three = pieces[("wout", "B", 0)]
    by_number = sorted(pieces, key=pieces.get)
    slot_of = [n % 2 if n < first_of_three else (n - first_of_three + 2) % 3 for n in range(len(pieces))]
    turn_of = [slot_of[:n + 1].count(slot_of[n]) for n in range(len(pieces))]
    selects = [i[1] for i in order if i[0] == "score"]
    select_number = {g: n for n, g in enumerate(selects)}
    plain = [g for g in selects if group_place(g)[0] != 4]
    paired = [g for g in selects if group_place(g)[0] == 4]
    staged = [(c, t) for part in "AB" for c in STAGED for t in PART[part]]
    staged_number = {key: n for n, key in enumerate(staged)}
    ropes = [i for i in order if i[0] == "proj" and PROJ[i[1]][0] in ("qa", "kv")]
    rope_number = {i: n for n, i in enumerate(ropes)}

    with ExitStack() as ctx:
        def sb(name, shape, dt=F32):
            return ctx.enter_context(nc.sbuf_tensor(name, shape, dt))

        def sem(name):
            return ctx.enter_context(nc.semaphore(name))

        qx = sb("qx", [P, 5120])
        qT = {"A": qx[:, 0:2048].rearrange("p (b n) -> p b n", b=8),
              "B": qx[:, 2048:4608].rearrange("p (b n) -> p b n", b=8)}
        x_part = {"A": qx[:, 0:2048].rearrange("p (t d) -> p t d", d=D),
                  "B": qx[:, 2048:5120].rearrange("p (t d) -> p t d", d=D)}
        hT = {"A": sb("hT_A", [P, KC, 256]), "B": sb("hT_B", [P, KC, 320])}
        kk = sb("kk", [P, 4032])
        kaT = kk[:, 0:512]
        kbT = kk[:, 512:2560].rearrange("p (b n) -> p b n", b=4)
        kaT_s = kk[:, 2560:2752]
        kbT_s = kk[:, 2752:4032].rearrange("p (b n) -> p b n", b=4)
        h2 = {"A": sb("h2_A", [P, 2, D]), "B": kk[:, 0:3072].rearrange("p (t d) -> p t d", d=D)}
        va = sb("va", [P, TILES, KV * HD])
        vb = sb("vb", [P, TILES, HEADS * HD])
        cache_va = sb("cache_va", [P, KV * HD])
        cache_vb = sb("cache_vb", [P, 2, HEADS * HD])
        shared = sb("shared", [P, KC * 384])
        mixed = shared[:].rearrange("p (k n) -> p k n", k=KC)
        stage = shared[:, 0:STAGES * 512].rearrange("p (t d) -> p t d", d=512)
        rope_c, rope_s = shared[:, 2048:2048 + PC], shared[:, 2560:2560 + PC]
        u_ring = sb("u_ring", [P, RING, D])
        v_ring = sb("v_ring", [P, RING, D])
        w_ring = sb("w_ring", [P, 2, 2048])
        keysT = sb("keysT", [P, 2 * HEADS, NSUB])
        qp = sb("qp", [P, 2, 2, 256])
        q_even = sb("q_even", [P, 2, DEC])
        q_odd = sb("q_odd", [P, 2, P])
        s_ring = sb("s_ring", [P, 2, 2 * NSUB])
        s_pair = sb("s_pair", [P, 2 * NSUB])
        cand = sb("cand", [P, TOPK, TOPK])
        onehot = sb("onehot", [P, TOPK, TOPK])
        top = sb("top", [P, 2, TOPK])
        top_u = sb("top_u", [P, 2, TOPK], U32)
        top_f = sb("top_f", [P, 2, TOPK])
        best = sb("best", [P, TOPK])
        best_e = sb("best_e", [P, TOPK])
        place_u = sb("place_u", [P, 3, TOPK], U32)
        place_f = sb("place_f", [P, 2, TOPK])
        picked = sb("picked", [P, 2, TOPK])
        small = sb("small", [P, 4])
        experts = sb("experts", [P, GROUPS * GROUP], U32)
        gates = sb("gates", [P, GROUPS * GROUP])
        work = sb("work", [P, 1536])
        probs, probsT, y_rows = work[:, 0:512], work[:, 512:1024], work[:, 1024:1536]
        gate_tmp = work[:, 0:TOKENS["B"]]
        gate_sig = qx[:, 4608:4608 + TOKENS["B"]]
        const = sb("const", [P, C_END])
        ident = const[:, C_IDENT:C_IDENT + P]
        causal = const[:, C_CAUSAL:C_CAUSAL + P]
        fold = const[:, C_FOLD:C_FOLD + 2 * P].rearrange("p (w n) -> p w n", w=2)
        cos = const[:, C_COS:C_COS + 160].rearrange("p (t n) -> p t n", t=TILES)
        sin = const[:, C_SIN:C_SIN + 160].rearrange("p (t n) -> p t n", t=TILES)
        iota = const[:, C_IOTA:C_IOTA + TOPK]
        g_row = sb("g_row", [P, D])
        negF = sb("negF", [HEADS, SEQ])
        negF_s = sb("negF_s", [HEADS, PAST + DEC])
        bias_f = sb("bias_f", [P, HEADS])
        sink = sb("sink", [P, HEADS])
        neg_sink = sb("neg_sink", [P, HEADS])
        raw_f = sb("raw_f", [P, TILES, HEADS])
        f_tmp = sb("f_tmp", [P, 6, TILES * HEADS])
        logf = sb("logf", [P, TILES, HEADS])
        cache_f = sb("cache_f", [P, 2, HEADS])
        negm = sb("negm", [P, 2, HEADS])
        lsum = sb("lsum", [P, 2, HEADS])
        sink_e = sb("sink_e", [P, 2, HEADS])
        rinv = sb("rinv", [P, HEADS])
        stat = sb("stat", [P, 4, 15])
        diag = sb("diag", [P, DIAGS, P])
        dots_sb = sb("dots_sb", [P, 2, GROUP])
        gelu_sb = sb("gelu_sb", [P, 2, GROUP])
        weights_sb = sb("weights_sb", [P, 2, GROUP])
        idx_u = sb("idx_u", [P, 2, GROUP], U32)
        idx_v = sb("idx_v", [P, 2, GROUP], U32)
        scratch = v_ring[:].rearrange("p a d -> p (a d)")
        x_tmp = scratch[:, 0:2048].rearrange("p (t d) -> p t d", d=D)
        h_tmp = scratch[:, 2048:4096].rearrange("p (t d) -> p t d", d=D)
        tri = scratch[:, 4096:4096 + TRI]
        w_f = scratch[:, 4096 + TRI:4096 + TRI + KC * HEADS].rearrange("p (k n) -> p k n", k=KC)

        bank = [ctx.enter_context(nc.psum_tensor(f"bank{i}", [P, 512], F32)) for i in range(BANKS)]
        summed = [[ctx.enter_context(nc.psum_tensor(f"summed{a}{b}", [P, 512], F32)) for b in range(2)]
                  for a in range(2)]

        bank_full = [sem(f"bank_full{i}") for i in range(BANKS)]
        bank_used = [sem(f"bank_used{i}") for i in range(BANKS)]
        const_loaded = sem("const_loaded")
        x_tmp_loaded = [sem(f"x_tmp_loaded{i}") for i in range(2)]
        cache_loaded = sem("cache_loaded")
        keys_loaded = sem("keys_loaded")
        g_loaded = sem("g_loaded")
        w_loaded = [sem(f"w_loaded{i}") for i in range(3)]
        x_loaded = sem("x_loaded")
        squares_summed = sem("squares_summed")
        mean_ready = sem("mean_ready")
        root_ready = sem("root_ready")
        normed = sem("normed")
        roped = sem("roped")
        stage_stored = [sem(f"stage_stored{i}") for i in range(STAGES)]
        logf_step = sem("logf_step")
        rowmax_ready = sem("rowmax_ready")
        y_ready = sem("y_ready")
        mixed_ready = sem("mixed_ready")
        best_ready = sem("best_ready")
        exp_ready = sem("exp_ready")
        selected = sem("selected")
        vector_chain = sem("vector_chain")
        outputs_stored = sem("outputs_stored")
        y_stored = sem("y_stored")
        idx_copied = sem("idx_copied")
        paced = sem("paced")
        paced_scalar = sem("paced_scalar")
        u_landed = [sem(f"u_landed{i}") for i in range(RING)]
        v_landed = [sem(f"v_landed{i}") for i in range(RING)]
        u_free = sem("u_free")
        v_free = sem("v_free")
        v_taken = sem("v_taken")
        gelu_ready = sem("gelu_ready")
        weights_ready = sem("weights_ready")
        diag_ready = sem("diag_ready")
        collected = sem("collected")

        def bank_of(job):
            return bank[jobs[job] % BANKS]

        def full(eng, job):
            n = jobs[job]
            eng.wait_ge(bank_full[n % BANKS], n // BANKS + 1)

        def used(eng, job):
            n = jobs[job]
            eng.wait_ge(bank_used[n % BANKS], n // BANKS + 1)

        def release(job):
            return bank_used[jobs[job] % BANKS]

        def piece_ap(w):
            n = slot_of[pieces[w]]
            return w_ring[:, n, :] if n < 2 else vb[:].rearrange("p t d -> p (t d)")[:, 0:2048]

        def x_of(t):
            return x_part[part_of(t)][:, t - PART[part_of(t)][0], :]

        def h2_of(t):
            return h2[part_of(t)][:, t - PART[part_of(t)][0], :]

        def key_span(t, br):
            if br == "swa":
                if t == 4:
                    return kaT_s, 0, [(P, cache_va[:, :]), (DEC, va[0:DEC, 4, :])]
                first = max(t - 1, 0)
                return kaT, P * first, [(P, va[:, i, :]) for i in range(first, t + 1)]
            if t == 4:
                return kbT_s, 0, [(P, cache_vb[:, 0, :]), (P, cache_vb[:, 1, :]), (DEC, vb[0:DEC, 4, :])]
            return kbT, 0, [(P, vb[:, i, :]) for i in range(t + 1)]

        def group_x(g):
            return x_of(group_place(g)[0])

        def group_h(g):
            return h2_of(group_place(g)[0])

        def stage_stores(c, t):
            return int(c == "kb" or (c == "kv" and t >= 3))

        def stores_of_stage(b, upto=None):
            keys = [k for k, n in staged_number.items() if n % STAGES == b and (upto is None or n < upto)]
            return 16 * sum(stage_stores(*k) for k in keys)

        block = ctx.enter_context(nc.Block())

        @block.sync
        def _(sp):
            def load_x_tmp(t):
                if t >= 2:
                    sp.wait_ge(normed, t - 1)
                src = x_prompt[P * t:P * t + P, :] if t < 4 else x_sample
                sp.dma_start(x_tmp[0:ROWS[t], t % 2, :], src).then_inc(x_tmp_loaded[t % 2], 16)

            def load_piece(n):
                kind, part, i = by_number[n]
                former = [m for m in range(n) if slot_of[m] == slot_of[n]]
                if former:
                    full(sp, last_job[by_number[former[-1]]])
                elif slot_of[n] == 2:
                    full(sp, ("values",) + units("B")[-1])
                    sp.wait_ge(outputs_stored, 16 * OUTPUTS_STORED)
                src = {"proj": w_proj, "merge": w_merge, "wout": w_out, "query": w_pq}[kind][i]
                sp.dma_start(piece_ap(by_number[n])[:, 0:src.shape[1]], src).then_inc(w_loaded[slot_of[n]], 16)

            load_x_tmp(0)
            sp.dma_start(g_row[:], g_mix.partition_broadcast(P)).then_inc(g_loaded, 16)
            sp.dma_start(const[:], consts).then_inc(const_loaded, 16)
            load_x_tmp(1)
            load_piece(0)
            load_piece(1)
            load_x_tmp(2)
            load_piece(2)
            load_x_tmp(3)
            load_piece(3)
            load_x_tmp(4)
            sp.dma_start(w_f, w_forget).then_inc(cache_loaded, 16)
            for dst, src in ((bias_f[:], b_fgate.partition_broadcast(P)), (sink[:], sinks.partition_broadcast(P)),
                             (tri, tri_d), (cache_f[:], fox_logf), (kaT_s[:, 0:WINDOW], swa_kT),
                             (kbT_s[:, :, 0:PAST], fox_kT), (cache_va[:], swa_v), (cache_vb[:], fox_v)):
                sp.dma_start(dst, src).then_inc(cache_loaded, 16)
            for dst, src in ((s_swa_k, swa_k), (s_swa_v, swa_v)):
                sp.dma_start(dst[0:WINDOW - DEC, :], src[DEC:WINDOW, :]).then_inc(outputs_stored, 16)
            for n, w in enumerate(by_number):
                kind, part, i = w
                if n < 4:
                    continue
                load_piece(n)
                if n == len(PROJ):
                    sp.dma_start(keysT[:], sub_keys).then_inc(keys_loaded, 16)
                    sp.wait_ge(normed, 5)
                    sp.dma_start(g_row[:], g_ffn.partition_broadcast(P)).then_inc(g_loaded, 16)
                if w[0] == "wout" and i == (0 if part == "A" else 1):
                    used(sp, ("gate", part, KC - 1, 3))
                    for t in PART[part]:
                        if t < 4:
                            sp.dma_start(x_of(t), x_prompt[P * t:P * t + P, :]).then_inc(x_loaded, 16)
                        else:
                            for half in range(2):
                                sp.dma_start(x_of(t)[DEC * half:DEC * half + DEC, :], x_sample).then_inc(x_loaded, 16)
                if w == ("query", "B", 0):
                    sp.wait_ge(normed, 10)
                    sp.dma_start(g_row[:], g_final.partition_broadcast(P)).then_inc(g_loaded, 16)

            for n in range(10, 15):
                t = NORM_TILES[n]
                sp.wait_ge(normed, n + 1)
                dst = y_prompt[P * t:P * t + P, :] if t < 4 else y_sample
                sp.dma_start(dst, h2_of(t)[0:ROWS[t], :]).then_inc(y_stored, 16)
            sp.wait_ge(y_stored, 16 * TILES)

        @block.gpsimd
        def _(pool):
            def copy_indices(g, dst, number, looped=False):
                nc.gpsimd.tensor_copy(dst, experts[:, bass.ds(g * GROUP, GROUP)]).then_inc(idx_copied, 1)
                pool.wait_ge(idx_copied, number)
                if looped:
                    pool.sem_inc(paced, 1)

            def gather(table, ring, landed, idx, j, looped):
                if looped:
                    pool.sem_inc(paced, 1)
                nc.gpsimd.indirect_dma_start(
                    ring[:, j % RING, :], None, table,
                    bass.IndirectOffsetOnAxis(idx[:, j:j + 1], 0)).then_inc(landed[j % RING], 16)

            def gather_u(g, par, j, looped=False):
                pool.wait_ge(u_free, g * GROUP + (j + 1))
                gather(peer_u, u_ring, u_landed, idx_u[:, par, :], j, looped)

            def gather_v(g, par, j, looped=False):
                if looped:
                    pool.wait_ge(v_free, pe_before(g) + (j + 1 - RING))
                elif g * GROUP + j >= RING:
                    g0, j0 = divmod(g * GROUP + j - RING, GROUP)
                    if j0 in slots_of_pe(g0):
                        pool.wait_ge(v_free, pe_before(g0) + slots_of_pe(g0).index(j0) + 1)
                    else:
                        pool.wait_ge(v_taken, dve_before(g0) + slots_of_dve(g0).index(j0) + 1)
                gather(peer_v, v_ring, v_landed, idx_v[:, par, :], j, looped)

            for g in range(UNROLLED):
                pool.wait_ge(selected, select_number[g] + 1)
                copy_indices(g, idx_u[:, g % 2, :], max(2 * g, 1))
                if g:
                    copy_indices(g - 1, idx_v[:, (g - 1) % 2, :], 2 * g + 1)
                for j in range(GROUP):
                    gather_u(g, g % 2, j)
                    if g:
                        gather_v(g - 1, (g - 1) % 2, j)
            pool.wait_ge(selected, GROUPS)
            with pool.Fori(0, (GROUPS - UNROLLED) // 2) as p:
                for par in range(2):
                    g = p * 2 + (UNROLLED + par)
                    copy_indices(g, idx_u[:, par, :], g * 2, True)
                    copy_indices(g - 1, idx_v[:, 1 - par, :], g * 2 + 1, True)
                    for j in range(GROUP):
                        gather_u(g, par, j, True)
                        gather_v(g - 1, 1 - par, j, True)
            g = GROUPS - 1
            copy_indices(g, idx_v[:, 1, :], 2 * GROUPS)
            for j in range(GROUP):
                gather_v(g, 1, j)

        @block.tensor
        def _(pe):
            def take_bank(job):
                n = jobs[job]
                if n >= BANKS:
                    pe.wait_ge(bank_used[n % BANKS], n // BANKS)
                return bank_of(job)

            def done(ins, job):
                ins.then_inc(bank_full[jobs[job] % BANKS], 1)

            def front(item):
                kind = item[0]
                w = weight_piece(item)
                if w:
                    pe.wait_ge(w_loaded[slot_of[pieces[w]]], 16 * turn_of[pieces[w]])
                if kind == "nt":
                    n = item[1]
                    t = n % 5
                    src = h_tmp[:, t % 2, :] if n < 5 else h2_of(t)
                    pe.wait_ge(normed, n + 1)
                    for half in range(2):
                        job = ("nt", n, half)
                        ps = take_bank(job)
                        for b in range(4):
                            k = 4 * half + b
                            mm = nc.tensor.transpose(ps[:, P * b:P * b + ROWS[t]], src[0:ROWS[t], P * k:P * k + P],
                                                     ident[0:ROWS[t], 0:ROWS[t]])
                        done(mm, job)
                elif kind == "proj":
                    _, n, t = item
                    used(pe, ("nt", t, 1))
                    ps = take_bank(item)
                    wv = piece_ap(w).rearrange("p (k n) -> p k n", k=KC)
                    for k in range(KC):
                        mm = nc.tensor.matmul(ps[0:ROWS[t], 0:PC],
                                              hT[part_of(t)][:, k, column_of(t):column_of(t) + ROWS[t]],
                                              wv[:, k, :], start=(k == 0), stop=(k == KC - 1))
                    done(mm, item)
                elif kind == "forget":
                    t = item[1]
                    if t == 0:
                        pe.wait_ge(cache_loaded, 16 * 9)
                    used(pe, ("nt", t, 1))
                    ps = take_bank(item)
                    for k in range(KC):
                        mm = nc.tensor.matmul(ps[0:ROWS[t], 0:HEADS],
                                              hT[part_of(t)][:, k, column_of(t):column_of(t) + ROWS[t]],
                                              w_f[:, k, :], start=(k == 0), stop=(k == KC - 1))
                    done(mm, item)
                elif kind == "tr":
                    _, c, t = item
                    for n, (name, _half) in enumerate(PROJ):
                        if name == c and c in ("qa", "kv"):
                            pe.wait_ge(roped, rope_number[("proj", n, t)] + 1)
                        elif name == c:
                            used(pe, ("proj", n, t))
                    ps = take_bank(item)
                    src = stage[:, staged_number[(c, t)] % STAGES, :]
                    for b in range(1 if c == "kv" else 4):
                        mm = nc.tensor.transpose(ps[:, P * b:P * b + ROWS[t]], src[0:ROWS[t], P * b:P * b + P],
                                                 ident[0:ROWS[t], 0:ROWS[t]])
                    done(mm, item)
                elif kind == "cumulate":
                    pe.wait_ge(logf_step, 5)
                    ps = take_bank(("cumulate", 0))
                    for i in range(4):
                        mm = nc.tensor.matmul(ps[0:HEADS, 0:SEQ], logf[:, i, :], tri[:, 384 - P * i:384 - P * i + SEQ],
                                              start=(i == 0), stop=(i == 3))
                    done(mm, ("cumulate", 0))
                    ps = take_bank(("cumulate", 1))
                    n = PAST + DEC
                    for i in range(3):
                        r = P if i < 2 else DEC
                        src = cache_f[:, i, :] if i < 2 else logf[0:DEC, 4, :]
                        mm = nc.tensor.matmul(ps[0:HEADS, 0:n], src, tri[0:r, 384 - P * i:384 - P * i + n],
                                              start=(i == 0), stop=(i == 2))
                    done(mm, ("cumulate", 1))
                elif kind == "att":
                    attention(item)
                elif kind == "ytr":
                    _, t, br = item
                    pe.wait_ge(y_ready, branch_number(t, br) + 1)
                    ps = take_bank(item)
                    for b in range(4):
                        mm = nc.tensor.transpose(ps[:, P * b:P * b + ROWS[t]], y_rows[0:ROWS[t], P * b:P * b + P],
                                                 ident[0:ROWS[t], 0:ROWS[t]])
                    done(mm, item)
                elif kind == "gate":
                    _, part, m, w4 = item
                    n = TOKENS[part]
                    if m == 0 and w4 >= 2:
                        for t in PART[part]:
                            used(pe, ("ytr", t, ("swa", "fox")[w4 - 2]))
                    ps = take_bank(item)
                    piece = piece_ap(w)
                    if w4 < 2:
                        wv = piece[:, 0:KC * P].rearrange("p (k n) -> p k n", k=KC)
                        for k in range(KC):
                            mm = nc.tensor.matmul(ps[:, 0:n], wv[:, k, :], hT[part][:, k, :],
                                                  start=(k == 0), stop=(k == KC - 1))
                    else:
                        wv = piece[:, KC * P:(KC + 4) * P].rearrange("p (k n) -> p k n", k=4)
                        for k in range(4):
                            mm = nc.tensor.matmul(ps[:, 0:n], wv[:, k, :], qT[part][:, 4 * (w4 - 2) + k, :],
                                                  start=(k == 0), stop=(k == 3))
                    done(mm, item)
                elif kind == "wout":
                    _, part, q, t = item
                    pe.wait_ge(mixed_ready, KC if part == "A" else 4 * KC)
                    ps = take_bank(item)
                    wv = piece_ap(w).rearrange("p (k n) -> p k n", k=KC)
                    for k in range(KC):
                        mm = nc.tensor.matmul(ps[:, 0:256], mixed[:, k, column_of(t):column_of(t) + P], wv[:, k, :],
                                              start=(k == 0), stop=(k == KC - 1))
                    done(mm, item)
                elif kind == "query":
                    _, part, h, p2 = item
                    n = TOKENS[part]
                    if h == 0 and p2 == 0:
                        for t in PART[part]:
                            used(pe, ("nt", 5 + t, 1))
                    ps = take_bank(item)
                    wv = piece_ap(w).rearrange("p (k n) -> p k n", k=KC)
                    for k in range(KC):
                        mm = nc.tensor.matmul(ps[:, 0:n], wv[:, k, P * p2:P * p2 + P], hT[part][:, k, :],
                                              start=(k == 0), stop=(k == KC - 1))
                    done(mm, item)
                elif kind == "query0":
                    _, t, p2 = item
                    used(pe, ("nt", 5 + t, 1))
                    ps = take_bank(item)
                    wv = piece_ap(w).rearrange("p (k n) -> p k n", k=KC)
                    for k in range(KC):
                        mm = nc.tensor.matmul(ps[:, 0:P], wv[:, k, P * p2:P * p2 + P],
                                              hT["A"][:, k, column_of(t):column_of(t) + P],
                                              start=(k == 0), stop=(k == KC - 1))
                    done(mm, item)
                elif kind == "even":
                    h = 2 * item[1]
                    used(pe, ("query", "B", h, 1))
                    ps = take_bank(item)
                    for p2 in range(2):
                        mm = nc.tensor.matmul(ps[0:DEC, P * p2:P * p2 + P], q_even[:, p2, :], keysT[:, 2 * h + p2, :],
                                              start=True, stop=True)
                    done(mm, item)
                elif kind == "score":
                    t, h = group_place(item[1])
                    h += t == 4
                    if item[1] == 0:
                        pe.wait_ge(keys_loaded, 16)
                    used(pe, ("query0", t, 1) if item[1] < 2 else ("query", part_of(t), h, 1))
                    ps = take_bank(item)
                    for p2 in range(2):
                        q = q_odd[:, p2, :] if t == 4 else qp[:, h % 2, p2, column_of(t):column_of(t) + P]
                        mm = nc.tensor.matmul(ps[:, P * p2:P * p2 + P], q, keysT[:, 2 * h + p2, :],
                                              start=True, stop=True)
                    done(mm, item)

            def attention(item):
                _, part, v = item
                us = units(part)
                if v < len(us):
                    t, br, h = us[v]
                    r, c = ROWS[t], column_of(t)
                    kT, first, blocks = key_span(t, br)
                    n = sum(b[0] for b in blocks)
                    if v == 0:
                        for pt in PART[part]:
                            for cc in ("qa", "kv"):
                                used(pe, ("tr", cc, pt))
                    if v == len(us) // 2:
                        for pt in PART[part]:
                            for cc in ("qb", "kb"):
                                used(pe, ("tr", cc, pt))
                            for piece in (7, 8):
                                used(pe, ("proj", piece, pt))
                        used(pe, ("cumulate", 1))
                    job = ("scores", t, br, h)
                    ps = take_bank(job)
                    if br == "swa":
                        lo = HD * (h // GRP)
                        mm = nc.tensor.matmul(ps[0:r, 0:n], qT[part][lo:lo + HD, h % GRP, c:c + r],
                                              kT[lo:lo + HD, first:first + n], start=True, stop=True)
                    else:
                        lo = HD * (h % 2)
                        nc.tensor.matmul(ps[0:r, 0:n], qT[part][lo:lo + HD, 4 + h // 2, c:c + r],
                                         kT[lo:lo + HD, h // 2, 0:n], start=True, stop=False)
                        fs = negF_s if t == 4 else negF
                        mm = nc.tensor.matmul(ps[0:r, 0:n], ident[0:HEADS, h:h + 1].broadcast_to([HEADS, r]),
                                              fs[:, 0:n], start=False, stop=True)
                    done(mm, job)
                if 0 <= v - 1 < len(us):
                    t, br, h = us[v - 1]
                    r = ROWS[t]
                    job = ("pt", t, br, h)
                    used(pe, ("scores", t, br, h))
                    ps = take_bank(job)
                    for b, (kn, _v) in enumerate(key_span(t, br)[2]):
                        mm = nc.tensor.transpose(ps[0:kn, P * b:P * b + r], probs[0:r, P * b:P * b + kn],
                                                 ident[0:r, 0:r])
                    done(mm, job)
                if 0 <= v - 2 < len(us):
                    t, br, h = us[v - 2]
                    r = ROWS[t]
                    job = ("values", t, br, h)
                    used(pe, ("pt", t, br, h))
                    ps = take_bank(job)
                    blocks = key_span(t, br)[2]
                    col = HD * (h // GRP if br == "swa" else h)
                    for b, (kn, values) in enumerate(blocks):
                        mm = nc.tensor.matmul(ps[0:r, 0:HD], probsT[0:kn, P * b:P * b + r],
                                              values[:, col:col + HD], start=(b == 0), stop=(b == len(blocks) - 1))
                    done(mm, job)

            def expert_sum(g, par, j):
                mine = slots_of_pe(g) if isinstance(g, int) else range(GROUP)
                if j not in mine:
                    return
                n = mine.index(j)
                if n == 0:
                    pe.wait_ge(collected, g + 1)
                pe.wait_ge(diag_ready, pe_before(g) + (n + 1))
                pe.wait_ge(v_landed[j % RING], g * (2 * 16) + 16 * (j // RING + 1))
                for c in range(2):
                    mm = nc.tensor.matmul(summed[par][c][:], diag[:, diag_slot(g, n), :],
                                          v_ring[:, j % RING, 512 * c:512 * c + 512],
                                          start=(n == 0), stop=(j == mine[-1]))
                mm.then_inc(v_free, 1)

            pe.wait_ge(const_loaded, 16)
            for item in before:
                front(item)
            for s in range(UNROLLED):
                for j in range(GROUP):
                    if s:
                        expert_sum(s - 1, (s - 1) % 2, j)
                    for item in slots.get((s, j), ()):
                        front(item)
            with pe.Fori(0, (GROUPS - UNROLLED) // 2) as p:
                for par in range(2):
                    for j in range(GROUP):
                        expert_sum(p * 2 + (UNROLLED - 1 + par), 1 - par, j)
            for j in range(GROUP):
                expert_sum(GROUPS - 1, 1, j)

        @block.scalar
        def _(act):
            def copy_out(job, dst, src, scale=1.0):
                nc.scalar.activation(dst, src, ACT.Copy, scale=scale).then_inc(release(job), 1)

            def front(item):
                kind = item[0]
                if kind == "norm":
                    n = item[1]
                    t = NORM_TILES[n]
                    r = ROWS[t] if n < 5 else P
                    if n < 5:
                        act.wait_ge(x_tmp_loaded[t % 2], 16 * (t // 2 + 1))
                        if n >= 2:
                            full(act, ("nt", n - 2, 1))
                        src, dst = x_tmp[0:r, t % 2, :], h_tmp[0:r, t % 2, :]
                    else:
                        if n < 10:
                            used(act, ("wout", part_of(t), 3, t))
                        else:
                            last = [g for g in range(GROUPS) if group_place(g)[0] == t][-1]
                            act.wait_ge(collected, 2 + last + 1)
                            act.wait_ge(v_taken, dve_before(last + 1))
                        src, dst = x_of(t), h2_of(t)
                    nc.scalar.activation(dst, src, ACT.Square, accum_out=stat[0:r, 0, n:n + 1]).then_inc(
                        squares_summed, 1)
                    act.wait_ge(mean_ready, n + 1)
                    nc.scalar.activation(stat[0:r, 2, n:n + 1], stat[0:r, 1, n:n + 1], ACT.Sqrt).then_inc(
                        root_ready, 1)
                elif kind == "nt":
                    n = item[1]
                    t = n % 5
                    c = column_of(t)
                    for half in range(2):
                        job = ("nt", n, half)
                        full(act, job)
                        src = bank_of(job)[:].rearrange("p (b n) -> p b n", b=4)[:, :, 0:ROWS[t]]
                        copy_out(job, hT[part_of(t)][:, 4 * half:4 * half + 4, c:c + ROWS[t]], src)
                elif kind == "proj":
                    _, n, t = item
                    c, half = PROJ[n]
                    r = ROWS[t]
                    if c == "vb":
                        full(act, item)
                        copy_out(item, vb[0:r, t, PC * half:PC * half + PC], bank_of(item)[0:r, 0:PC])
                        if half:
                            used(act, item)
                            dst = p_fox_v[P * t:P * t + P, :] if t < 4 else s_fox_v
                            act.dma_start(dst, vb[0:r, t, :]).then_inc(outputs_stored, 16)
                elif kind == "tr":
                    _, c, t = item
                    r = ROWS[t]
                    b = staged_number[(c, t)] % STAGES
                    full(act, item)
                    if c == "kb":
                        dst = p_fox_k[P * t:P * t + P, :] if t < 4 else s_fox_k
                        act.dma_start(dst, stage[0:r, b, :]).then_inc(stage_stored[b], 16)
                    if c == "kv" and t >= 3:
                        dst = p_swa_k if t == 3 else s_swa_k[WINDOW - DEC:WINDOW, :]
                        act.dma_start(dst, stage[0:r, b, 0:P]).then_inc(stage_stored[b], 16)
                        used(act, ("proj", 2, t))
                        dst = p_swa_v if t == 3 else s_swa_v[WINDOW - DEC:WINDOW, :]
                        act.dma_start(dst, va[0:r, t, :]).then_inc(outputs_stored, 16)
                    src = bank_of(item)[:].rearrange("p (b n) -> p b n", b=4)[:, :, 0:r]
                    if c in ("qa", "qb"):
                        first = 4 * (c == "qb")
                        copy_out(item, qT[part_of(t)][:, first:first + 4, column_of(t):column_of(t) + r], src, SCALE)
                    elif c == "kv":
                        dst = kaT[:, P * t:P * t + P] if t < 4 else kaT_s[:, WINDOW:WINDOW + DEC]
                        copy_out(item, dst, bank_of(item)[:, 0:r])
                    else:
                        dst = kbT[:, :, P * t:P * t + P] if t < 4 else kbT_s[:, :, PAST:PAST + DEC]
                        copy_out(item, dst, src)
                elif kind == "logf":
                    act.wait_ge(logf_step, 1)
                    nc.scalar.activation(f_tmp[:, 2, :], f_tmp[:, 1, :], ACT.Exp).then_inc(logf_step, 1)
                    act.wait_ge(logf_step, 3)
                    nc.scalar.activation(f_tmp[:, 4, :], f_tmp[:, 3, :], ACT.Ln).then_inc(logf_step, 1)
                    act.wait_ge(logf_step, 5)
                    act.dma_start(p_logf.rearrange("(t p) h -> p t h", p=P), logf[:, 0:4, :]).then_inc(
                        outputs_stored, 16)
                    act.dma_start(s_logf, logf[0:DEC, 4, :]).then_inc(outputs_stored, 16)
                elif kind == "att":
                    _, part, v = item
                    us = units(part)
                    if part == "A" and v == 0:
                        act.wait_ge(cache_loaded, 16 * 9)
                    if v < len(us):
                        t, br, h = us[v]
                        r = ROWS[t]
                        b = branch_number(t, br)
                        n = sum(x[0] for x in key_span(t, br)[2])
                        job = ("scores", t, br, h)
                        act.wait_ge(rowmax_ready, unit_number(t, br, h) + 1)
                        bias = negm[0:r, b % 2, h:h + 1]
                        if br == "swa":
                            nc.scalar.activation(sink_e[0:r, b % 2, h:h + 1], sink[0:r, h:h + 1], ACT.Exp, bias=bias)
                        if v > 0:
                            full(act, ("pt",) + us[v - 1])
                        nc.scalar.activation(probs[0:r, 0:n], bank_of(job)[0:r, 0:n], ACT.Exp, bias=bias,
                                             accum_out=lsum[0:r, b % 2, h:h + 1]).then_inc(release(job), 1)
                    if 0 <= v - 1 < len(us):
                        t, br, h = us[v - 1]
                        job = ("pt", t, br, h)
                        full(act, job)
                        if v - 2 >= 0:
                            full(act, ("values",) + us[v - 2])
                        blocks = key_span(t, br)[2]
                        whole = [b for b in blocks if b[0] == P]
                        src = bank_of(job)
                        if ROWS[t] == P:
                            copy_out(job, probsT[:, 0:P * len(blocks)], src[:, 0:P * len(blocks)])
                        else:
                            nw = len(whole)
                            nc.scalar.activation(
                                probsT[:, 0:P * nw].rearrange("p (b n) -> p b n", b=nw)[:, :, 0:DEC],
                                src[:, 0:P * nw].rearrange("p (b n) -> p b n", b=nw)[:, :, 0:DEC], ACT.Copy)
                            copy_out(job, probsT[0:DEC, P * nw:P * nw + DEC], src[0:DEC, P * nw:P * nw + DEC])
                elif kind == "ytr":
                    _, t, br = item
                    first = 4 * (br == "fox")
                    full(act, item)
                    src = bank_of(item)[:].rearrange("p (b n) -> p b n", b=4)[:, :, 0:ROWS[t]]
                    copy_out(item, qT[part_of(t)][:, first:first + 4, column_of(t):column_of(t) + ROWS[t]], src)
                elif kind == "gate" and item[3] < 2:
                    _, part, m, w4 = item
                    n = TOKENS[part]
                    full(act, item)
                    if m > 0 or w4 == 1:
                        former = (m - 1, w4 + 2) if m else (KC - 1, 2)
                        used(act, ("gate", part) + former)
                    nc.scalar.activation(gate_sig[:, 0:n], bank_of(item)[:, 0:n], ACT.Sigmoid).then_inc(
                        release(item), 1)
                elif kind == "query":
                    _, part, h, p2 = item
                    full(act, item)
                    if part == "B":
                        dst = q_even[:, p2, :] if h % 2 == 0 else q_odd[:, p2, DEC:P]
                        nc.scalar.activation(dst, bank_of(item)[:, 256:320], ACT.Copy)
                    copy_out(item, qp[:, h % 2, p2, :], bank_of(item)[:, 0:256])
                elif kind == "query0":
                    _, t, p2 = item
                    full(act, item)
                    copy_out(item, qp[:, 0, p2, column_of(t):column_of(t) + P], bank_of(item)[:, 0:P])
                elif kind == "even":
                    n = paired.index(GROUPS_SAMPLE + item[1])
                    if n:
                        act.wait_ge(selected, select_number[paired[n - 1]] + 1)
                    full(act, item)
                    copy_out(item, s_pair[0:DEC, :], bank_of(item)[0:DEC, 0:2 * NSUB])
                elif kind == "score":
                    g = item[1]
                    full(act, item)
                    if group_place(g)[0] == 4:
                        copy_out(item, s_pair[DEC:P, :], bank_of(item)[DEC:P, 0:2 * NSUB])
                    else:
                        i = plain.index(g)
                        if i >= 2:
                            act.wait_ge(selected, select_number[plain[i - 2]] + 1)
                        copy_out(item, s_ring[:, i % 2, :], bank_of(item)[:, 0:2 * NSUB])
                elif kind == "weights":
                    act.wait_ge(best_ready, select_number[item[1]] + 1)
                    nc.scalar.activation(best_e[:], best[:], ACT.Exp, bias=small[:, 0:1],
                                         accum_out=small[:, 1:2]).then_inc(exp_ready, 1)

            def gelu(g, par):
                act.wait_ge(u_free, g * GROUP + (RING + GROUP))
                nc.scalar.activation(gelu_sb[:, par, :], dots_sb[:, par, :], ACT.Gelu).then_inc(gelu_ready, 1)

            def diagonal(g, par, n):
                fold_of = int(isinstance(g, int) and group_place(g)[0] == 4)
                if n == 0:
                    act.wait_ge(weights_ready, g + 1)
                if not isinstance(g, int) or pe_before(g) + n >= DIAGS:
                    act.wait_ge(v_free, pe_before(g) + (n + 1 - DIAGS))
                if not isinstance(g, int):
                    act.sem_inc(paced_scalar, 1)
                j = slots_of_pe(g)[n] if isinstance(g, int) else n
                nc.scalar.activation(diag[:, diag_slot(g, n), :], fold[:, fold_of, :], ACT.Copy,
                                     scale=weights_sb[:, par, j:j + 1]).then_inc(diag_ready, 1)

            act.wait_ge(const_loaded, 16)
            for item in before:
                front(item)
            for s in range(UNROLLED_SV):
                made = 0
                if s:
                    gelu(s - 1, (s - 1) % 2)
                for j in range(GROUP):
                    while s and made < len(slots_of_pe(s - 1)) and slots_of_pe(s - 1)[made] < j + DIAGS - 1:
                        diagonal(s - 1, (s - 1) % 2, made)
                        made += 1
                    for item in slots.get((s, j), ()):
                        front(item)
            with act.Fori(0, (GROUPS - UNROLLED_SV) // 2) as p:
                for par in range(2):
                    g = p * 2 + (UNROLLED_SV - 1 + par)
                    gelu(g, 1 - par)
                    for n in range(GROUP):
                        diagonal(g, 1 - par, n)
            gelu(GROUPS - 1, 1)
            for n in range(len(slots_of_pe(GROUPS - 1))):
                diagonal(GROUPS - 1, 1, n)
            front(("norm", 14))
            act.wait_ge(outputs_stored, 16 * OUTPUTS_STORED)
            for b in range(STAGES):
                act.wait_ge(stage_stored[b], stores_of_stage(b))

        @block.vector
        def _(dve):
            chain = [0]

            def step(ins):
                chain[0] += 1
                ins.then_inc(vector_chain, 1)
                return chain[0]

            def behind(n):
                dve.wait_ge(vector_chain, n)

            def front(item):
                kind = item[0]
                if kind == "norm":
                    n = item[1]
                    t = NORM_TILES[n]
                    r = ROWS[t] if n < 5 else P
                    src, dst = (x_tmp[0:r, t % 2, :], h_tmp[0:r, t % 2, :]) if n < 5 else (x_of(t), h2_of(t))
                    dve.wait_ge(squares_summed, n + 1)
                    nc.vector.tensor_scalar(stat[0:r, 1, n:n + 1], stat[0:r, 0, n:n + 1], 1.0 / D, EPS,
                                            ALU.mult, ALU.add).then_inc(mean_ready, 1)
                    dve.wait_ge(root_ready, n + 1)
                    mean, inv, tmp = (stat[0:r, i, n:n + 1] for i in (1, 3, 2))
                    behind(step(nc.vector.reciprocal(inv, tmp)))
                    behind(step(nc.vector.scalar_tensor_tensor(tmp, inv, inv, mean, ALU.mult, ALU.mult)))
                    behind(step(nc.vector.tensor_scalar(tmp, tmp, -0.5, 1.5, ALU.mult, ALU.add)))
                    behind(step(nc.vector.tensor_tensor(inv, inv, tmp, ALU.mult)))
                    dve.wait_ge(g_loaded, 16 * (n // 5 + 1))
                    nc.vector.scalar_tensor_tensor(dst, src, stat[0:r, 3, n:n + 1], g_row[0:r, :],
                                                   ALU.mult, ALU.mult).then_inc(normed, 1)
                elif kind == "proj":
                    project(item)
                elif kind == "forget":
                    t = item[1]
                    full(dve, item)
                    nc.vector.tensor_copy(raw_f[0:ROWS[t], t, :], bank_of(item)[0:ROWS[t], 0:HEADS]).then_inc(
                        release(item), 1)
                elif kind == "logf":
                    z, na, e, u, ln, w = (f_tmp[:, i, :] for i in range(6))
                    z3 = z.rearrange("p (t h) -> p t h", t=TILES)
                    dve.wait_ge(cache_loaded, 16 * 9)
                    used(dve, ("forget", TILES - 1))
                    behind(step(nc.vector.tensor_tensor(z3, raw_f[:], bias_f[:].unsqueeze(1).broadcast_to(
                        [P, TILES, HEADS]), ALU.add)))
                    nc.vector.scalar_tensor_tensor(na, z, -1.0, z, ALU.mult, ALU.min).then_inc(logf_step, 1)
                    dve.wait_ge(logf_step, 2)
                    nc.vector.tensor_scalar(u, e, 1.0, None, ALU.add).then_inc(logf_step, 1)
                    dve.wait_ge(logf_step, 4)
                    behind(step(nc.vector.tensor_scalar(w, u, 1.0, None, ALU.is_equal)))
                    step(nc.vector.tensor_tensor(ln, ln, w, ALU.add))
                    behind(step(nc.vector.scalar_tensor_tensor(w, u, -1.0, w, ALU.add, ALU.add)))
                    behind(step(nc.vector.reciprocal(u, w)))
                    behind(step(nc.vector.tensor_tensor(ln, ln, u, ALU.mult)))
                    behind(step(nc.vector.tensor_tensor(ln, ln, e, ALU.mult)))
                    nc.vector.scalar_tensor_tensor(logf[:].rearrange("p t h -> p (t h)"), z, 0.0, ln,
                                                   ALU.min, ALU.subtract).then_inc(logf_step, 1)
                elif kind == "cumulate":
                    for i, dst in ((0, negF), (1, negF_s)):
                        job = ("cumulate", i)
                        full(dve, job)
                        nc.vector.tensor_scalar(dst[:], bank_of(job)[0:HEADS, 0:dst.shape[1]], -1.0, None,
                                                ALU.mult).then_inc(release(job), 1)
                elif kind == "att":
                    attention(item)
                elif kind == "divide":
                    _, t, br = item
                    r = ROWS[t]
                    b = branch_number(t, br) % 2
                    used(dve, ("values", t, br, HEADS - 1))
                    if br == "swa":
                        behind(step(nc.vector.tensor_tensor(lsum[0:r, b, :], lsum[0:r, b, :], sink_e[0:r, b, :],
                                                            ALU.add)))
                    behind(step(nc.vector.reciprocal(rinv[0:r, :], lsum[0:r, b, :])))
                    yv = y_rows[0:r, :].rearrange("p (h d) -> p h d", h=HEADS)
                    nc.vector.tensor_tensor(yv, yv, rinv[0:r, :].unsqueeze(2).broadcast_to([r, HEADS, HD]),
                                            ALU.mult).then_inc(y_ready, 1)
                elif kind == "gate" and item[3] >= 2:
                    _, part, m, w4 = item
                    n = TOKENS[part]
                    full(dve, item)
                    if m == 0 and w4 == 2:
                        upto = len(STAGED) * (2 if part == "A" else TILES)
                        for b in range(STAGES):
                            if stores_of_stage(b, upto):
                                dve.wait_ge(stage_stored[b], stores_of_stage(b, upto))
                    used(dve, ("gate", part, m, w4 - 2))
                    ps = bank_of(item)
                    if w4 == 2:
                        if part == "B":
                            nc.vector.tensor_tensor(mixed[:, m, 320:384], ps[:, 256:320], gate_sig[:, 256:320],
                                                    ALU.mult).then_inc(mixed_ready, 1)
                        nc.vector.tensor_tensor(mixed[:, m, 0:n], ps[:, 0:n], gate_sig[:, 0:n],
                                                ALU.mult).then_inc(release(item), 1)
                    else:
                        ready = m if part == "A" else 2 * KC + 2 * m
                        if ready:
                            dve.wait_ge(mixed_ready, ready)
                        nc.vector.tensor_tensor(gate_tmp[:, 0:n], ps[:, 0:n], gate_sig[:, 0:n],
                                                ALU.mult).then_inc(release(item), 1)
                        used(dve, item)
                        if part == "B":
                            nc.vector.tensor_tensor(mixed[:, m, 320:384], mixed[:, m, 320:384], gate_tmp[:, 256:320],
                                                    ALU.add).then_inc(mixed_ready, 1)
                        nc.vector.tensor_tensor(mixed[:, m, 0:n], mixed[:, m, 0:n], gate_tmp[:, 0:n],
                                                ALU.add).then_inc(mixed_ready, 1)
                elif kind == "wout":
                    _, part, q, t = item
                    full(dve, item)
                    dve.wait_ge(x_loaded, 16 * (2 if part == "A" else 6))
                    xv = x_of(t)[:, 256 * q:256 * q + 256]
                    nc.vector.tensor_tensor(xv, xv, bank_of(item)[:, 0:256], ALU.add).then_inc(release(item), 1)
                elif kind in ("halves", "sums", "places", "weights"):
                    select(kind, item[1])

            def project(item):
                _, n, t = item
                c, half = PROJ[n]
                if c == "vb":
                    return
                r = ROWS[t]
                ps = bank_of(item)
                number = staged_number[(c, t)]
                full(dve, item)
                if half == 0 and number >= STAGES:
                    full(dve, ("tr",) + staged[number - STAGES])
                    stored = stores_of_stage(number % STAGES, number)
                    if stored:
                        dve.wait_ge(stage_stored[number % STAGES], stored)
                dst = stage[0:r, number % STAGES, :]
                if c in ("qb", "kb"):
                    nc.vector.tensor_copy(dst[:, PC * half:PC * half + PC], ps[0:r, 0:PC]).then_inc(release(item), 1)
                    return
                heads = GRP if c == "qa" else KV
                w = heads * HD
                if rope_number[item]:
                    dve.wait_ge(roped, rope_number[item])
                if c == "kv":
                    nc.vector.tensor_copy(va[0:r, t, :], ps[0:r, w:2 * w])

                def table(a):
                    return a[0:r, t, :].unsqueeze(1).broadcast_to([r, 2 * heads, HD // 2])

                def halves(a):
                    return a[0:r, 0:w].rearrange("p (a b) -> p a b", b=HD // 2)

                nc.vector.tensor_tensor(halves(rope_c), halves(ps), table(cos), ALU.mult)
                nc.vector.tensor_tensor(halves(rope_s), halves(ps), table(sin), ALU.mult).then_inc(release(item), 1)
                used(dve, item)
                cv, sv = (a[0:r, 0:w].rearrange("p (i d) -> p i d", d=HD) for a in (rope_c, rope_s))
                if c == "qa":
                    out = dst.rearrange("p (i k d) -> p i k d", i=GRP, k=KV)[:, :, half, :]
                else:
                    out = dst[:, 0:w].rearrange("p (i d) -> p i d", d=HD)
                lo, hi = slice(0, HD // 2), slice(HD // 2, HD)
                nc.vector.tensor_tensor(out[:, :, lo], cv[:, :, lo], sv[:, :, hi], ALU.subtract)
                nc.vector.tensor_tensor(out[:, :, hi], cv[:, :, hi], sv[:, :, lo], ALU.add).then_inc(roped, 1)

            def attention(item):
                _, part, v = item
                us = units(part)
                if part == "A" and v == 0:
                    dve.wait_ge(cache_loaded, 16 * 9)
                    behind(step(nc.vector.tensor_scalar(neg_sink[:], sink[:], -1.0, None, ALU.mult)))
                if v < len(us):
                    t, br, h = us[v]
                    r = ROWS[t]
                    b = branch_number(t, br) % 2
                    n = sum(x[0] for x in key_span(t, br)[2])
                    job = ("scores", t, br, h)
                    ps = bank_of(job)
                    dst = negm[0:r, b, h:h + 1]
                    full(dve, job)
                    if br == "swa":
                        if t == 0:
                            behind(step(nc.vector.memset(ps[0:HD, HD:P], MASKED)))
                        elif t < 4:
                            step(nc.vector.memset(ps[0:HD, 3 * HD:4 * HD], MASKED))
                            behind(step(nc.vector.memset(ps[HD:P, 0:HD], MASKED)))
                        behind(step(nc.vector.tensor_reduce(dst, ps[0:r, 0:n], AX_X, ALU.max, negate=True)))
                        nc.vector.tensor_tensor(dst, dst, neg_sink[0:r, h:h + 1], ALU.min).then_inc(rowmax_ready, 1)
                    else:
                        last = ps[0:r, n - r:n]
                        behind(step(nc.vector.tensor_tensor(last, last, causal[0:r, 0:r], ALU.add)))
                        nc.vector.tensor_reduce(dst, ps[0:r, 0:n], AX_X, ALU.max, negate=True).then_inc(
                            rowmax_ready, 1)
                if 0 <= v - 2 < len(us):
                    t, br, h = us[v - 2]
                    r = ROWS[t]
                    job = ("values", t, br, h)
                    full(dve, job)
                    if h == 0 and v - 2 > 0:
                        full(dve, ("ytr",) + us[v - 3][0:2])
                    nc.vector.tensor_copy(y_rows[0:r, HD * h:HD * h + HD], bank_of(job)[0:r, 0:HD]).then_inc(
                        release(job), 1)

            def select(part, g):
                pair = group_place(g)[0] == 4
                s = s_pair if pair else s_ring[:, plain.index(g) % 2, :]
                half = [s[:, NSUB * i:NSUB * i + NSUB] for i in range(2)]
                flat = cand[:].rearrange("p a b -> p (a b)")
                cols = slice(g * GROUP, g * GROUP + GROUP)
                behind(chain[0])
                if part == "halves":
                    used(dve, ("score", g))
                    if pair:
                        used(dve, ("even", g - GROUPS_SAMPLE))
                    n = [step(nc.vector.max(top[:, i, 0:8], half[i])) for i in range(2)]
                    for i in range(2):
                        behind(n[i])
                        n[i] = step(nc.vector.max_index(top_u[:, i, 0:8], top[:, i, 0:8], half[i]))
                    for i in range(2):
                        behind(n[i])
                        n[i] = step(nc.vector.match_replace(half[i], top[:, i, 0:8], half[i], REPLACED))
                    for i in range(2):
                        behind(n[i])
                        n[i] = step(nc.vector.max(top[:, i, 8:16], half[i]))
                    for i in range(2):
                        behind(n[i])
                        n[i] = step(nc.vector.max_index(top_u[:, i, 8:16], top[:, i, 8:16], half[i]))
                elif part == "sums":
                    a = step(nc.vector.tensor_tensor(
                        cand[:], top[:, 0, :].unsqueeze(2).broadcast_to([P, TOPK, TOPK]),
                        top[:, 1, :].unsqueeze(1).broadcast_to([P, TOPK, TOPK]), ALU.add))
                    step(nc.vector.tensor_copy(top_f[:], top_u[:]))
                    behind(a)
                    behind(step(nc.vector.max(best[:, 0:8], flat)))
                    behind(step(nc.vector.max_index(place_u[:, 0, 0:8], best[:, 0:8], flat)))
                    behind(step(nc.vector.match_replace(flat, best[:, 0:8], flat, REPLACED)))
                    behind(step(nc.vector.max(best[:, 8:16], flat)))
                    nc.vector.tensor_scalar(small[:, 0:1], best[:, 0:1], -1.0, None, ALU.mult).then_inc(best_ready, 1)
                    step(nc.vector.max_index(place_u[:, 0, 8:16], best[:, 8:16], flat))
                elif part == "places":
                    step(nc.vector.tensor_scalar(place_u[:, 1, :], place_u[:, 0, :], 4, None,
                                                 ALU.logical_shift_right))
                    behind(step(nc.vector.tensor_scalar(place_u[:, 2, :], place_u[:, 0, :], TOPK - 1, None,
                                                        ALU.bitwise_and)))
                    behind(step(nc.vector.tensor_copy(place_f[:], place_u[:, 1:3, :])))
                    for i in range(2):
                        behind(step(nc.vector.tensor_tensor(
                            onehot[:], place_f[:, i, :].unsqueeze(2).broadcast_to([P, TOPK, TOPK]),
                            iota.unsqueeze(1).broadcast_to([P, TOPK, TOPK]), ALU.is_equal)))
                        behind(step(nc.vector.tensor_tensor(
                            onehot[:], onehot[:], top_f[:, i, :].unsqueeze(1).broadcast_to([P, TOPK, TOPK]),
                            ALU.mult)))
                        behind(step(nc.vector.tensor_reduce(picked[:, i, :], onehot[:], AX_X, ALU.add)))
                    step(nc.vector.scalar_tensor_tensor(experts[:, cols], picked[:, 0, :], float(NSUB),
                                                        picked[:, 1, :], ALU.mult, ALU.add))
                else:
                    dve.wait_ge(exp_ready, select_number[g] + 1)
                    behind(step(nc.vector.reciprocal(small[:, 2:3], small[:, 1:2])))
                    nc.vector.tensor_scalar(gates[:, cols], best_e[:], small[:, 2:3], None, ALU.mult).then_inc(
                        selected, 1)

            def dot(g, par, j, h_rows):
                dve.wait_ge(u_landed[j % RING], g * (2 * 16) + 16 * (j // RING + 1))
                u = u_ring[:, j % RING, :]
                nc.vector.scalar_tensor_tensor(u, u, 1.0, h_rows, ALU.mult, ALU.mult,
                                               accum_out=dots_sb[:, par, j:j + 1]).then_inc(u_free, 1)

            def weigh(g, par):
                dve.wait_ge(gelu_ready, g + 1)
                nc.vector.tensor_tensor(weights_sb[:, par, :], gelu_sb[:, par, :],
                                        gates[:, bass.ds(g * GROUP, GROUP)], ALU.mult).then_inc(weights_ready, 1)

            def collect(g, par, rows):
                dve.wait_ge(v_free, pe_before(g + 1))
                dve.wait_ge(collected, g + 2)
                if isinstance(g, int):
                    early = len([j for j in slots_of_dve(g + 1) if j <= 8]) if g + 1 < GROUPS_A else 0
                    dve.wait_ge(v_taken, dve_before(g + 1) + early)
                for c in range(2):
                    o = rows[:, 512 * c:512 * c + 512]
                    ins = nc.vector.tensor_tensor(o, o, summed[par][c][:], ALU.add)
                ins.then_inc(collected, 1)

            def add_rows(g, j, rows):
                n = dve_before(g) + slots_of_dve(g).index(j)
                dve.wait_ge(weights_ready, g + 1)
                dve.wait_ge(v_landed[j % RING], g * (2 * 16) + 16 * (j // RING + 1))
                before_collect = j <= 8 and 0 < g < GROUPS - 1
                dve.wait_ge(collected, 2 + g - before_collect)
                if n:
                    dve.wait_ge(v_taken, n)
                nc.vector.scalar_tensor_tensor(rows, v_ring[:, j % RING, :], weights_sb[:, g % 2, j:j + 1], rows,
                                               ALU.mult, ALU.add).then_inc(v_taken, 1)

            step(nc.vector.memset(q_odd[:], 0.0))
            step(nc.vector.memset(raw_f[:], 0.0))
            behind(chain[0])
            dve.sem_inc(u_free, RING)
            dve.sem_inc(collected, 2)
            dve.wait_ge(const_loaded, 16)
            for item in before:
                front(item)
            for s in range(UNROLLED_SV):
                for j in range(GROUP):
                    dot(s, s % 2, j, group_h(s))
                    if j == 0 and s >= 1:
                        weigh(s - 1, (s - 1) % 2)
                    if s and j in slots_of_dve(s - 1):
                        add_rows(s - 1, j, group_x(s - 1))
                    if j == 8 and s >= 2:
                        collect(s - 2, s % 2, group_x(s - 2))
                    for item in slots.get((s, j), ()):
                        front(item)
            last = group_place(GROUPS - 1)[0]
            with dve.Fori(0, (GROUPS - UNROLLED_SV) // 2) as p:
                for par in range(2):
                    for j in range(GROUP):
                        dot(p * 2 + (UNROLLED_SV + par), par, j, h2_of(last))
                        if j == 0:
                            weigh(p * 2 + (UNROLLED_SV + par - 1), 1 - par)
                        if j == 8:
                            collect(p * 2 + (UNROLLED_SV + par - 2), par, x_of(last))
            weigh(GROUPS - 1, 1)
            collect(GROUPS - 2, 0, x_of(last))
            for j in slots_of_dve(GROUPS - 1):
                add_rows(GROUPS - 1, j, x_of(last))
            collect(GROUPS - 1, 1, x_of(last))
            front(("norm", 14))


def constants():
    c = np.zeros((P, C_END), np.float32)
    c[:, C_IDENT:C_IDENT + P] = np.eye(P)
    row, col = np.arange(P)[:, None], np.arange(P)[None, :]
    c[:, C_CAUSAL:C_CAUSAL + P] = np.where(col <= row, 0.0, MASKED)
    c[:, C_FOLD:C_FOLD + P] = np.eye(P)
    c[:, C_FOLD + P:C_FOLD + 2 * P] = (row % DEC == col)
    half = HD // 2
    inv = (np.float32(10000.0) ** (-np.arange(half, dtype=np.float32) / np.float32(half))).astype(np.float32)
    for t in range(TILES):
        pos = (np.arange(P) + (P * t if t < 4 else PAST)).astype(np.float32)
        angle = (pos[:, None] * inv[None, :]).astype(np.float32)
        c[:, C_COS + half * t:C_COS + half * t + half] = np.cos(angle)
        c[:, C_SIN + half * t:C_SIN + half * t + half] = np.sin(angle)
    c[:, C_IOTA:C_IOTA + TOPK] = np.arange(TOPK)
    tri = (np.arange(TRI)[None, :] >= np.arange(P)[:, None] + 384).astype(np.float32)
    return c, tri


def kernel(x_prompt, x_sample, cache_swa_k, cache_swa_v, cache_fox_k, cache_fox_v, cache_fox_logf, g_mix, w_in,
           b_fgate, sinks, w_a_out, w_b_out, w_out, g_ffn, w_pq, peer_sub_keys, peer_u, peer_v, g_final):
    import concourse.bacc as bacc
    from concourse.bass_utils import run_bass_kernel_spmd

    def rows_in(w, k=KC):
        return np.asarray(w).reshape(k, P, -1).transpose(1, 0, 2)

    w = rows_in(w_in[0])
    c, d, e = 2304, 2312, 3336

    def cut(array, n):
        s = array.reshape(P, array.shape[1], -1, n).transpose(2, 0, 1, 3)
        return s.reshape(s.shape[0], P, -1)

    merge = [np.concatenate([cut(gate, P), cut(rows_in(out[0], 4), P)], 2)
             for gate, out in ((w[:, :, d:e], w_a_out), (w[:, :, e:], w_b_out))]

    const, tri = constants()
    arrays = {
        "x_prompt": np.asarray(x_prompt)[0], "x_sample": np.asarray(x_sample)[0],
        "w_proj": cut(w[:, :, 0:c], PC), "w_forget": w[:, :, c:d],
        "w_merge": np.concatenate(merge),
        "w_out": cut(rows_in(w_out[0]), 256), "w_pq": cut(rows_in(w_pq[0]), 256),
        "sub_keys": np.asarray(peer_sub_keys)[0].transpose(3, 0, 1, 2).reshape(P, 2 * HEADS, NSUB),
        "g_mix": np.asarray(g_mix)[0], "g_ffn": np.asarray(g_ffn)[0], "g_final": np.asarray(g_final),
        "b_fgate": np.asarray(b_fgate)[0], "sinks": np.asarray(sinks)[0],
        "swa_kT": np.asarray(cache_swa_k)[0, 0].reshape(WINDOW, P).T,
        "swa_k": np.asarray(cache_swa_k)[0, 0].reshape(WINDOW, P),
        "swa_v": np.asarray(cache_swa_v)[0, 0].reshape(WINDOW, P),
        "fox_kT": np.asarray(cache_fox_k)[0, 0].reshape(PAST, 4, P).transpose(2, 1, 0),
        "fox_v": np.asarray(cache_fox_v)[0, 0].reshape(2, P, 512).transpose(1, 0, 2),
        "fox_logf": np.asarray(cache_fox_logf)[0, 0].reshape(2, P, HEADS).transpose(1, 0, 2),
        "consts": const, "tri": tri, "peer_u": np.asarray(peer_u)[0], "peer_v": np.asarray(peer_v)[0],
    }
    arrays = {f"in_{k}": np.ascontiguousarray(v) for k, v in arrays.items()}
    outs = [(SEQ, D), (DEC, D), (WINDOW, P), (WINDOW, P), (SEQ, 512), (SEQ, 512), (SEQ, HEADS),
            (WINDOW, P), (WINDOW, P), (DEC, 512), (DEC, 512), (DEC, HEADS)]
    nc = bacc.Bacc("TRN2", target_bir_lowering=False, num_devices=1, dynamic_dma_scratch_size=8192)
    args = [nc.dram_tensor(k, v.shape, mybir.dt.from_np(v.dtype), kind="ExternalInput").ap()
            for k, v in arrays.items()]
    args += [nc.dram_tensor(f"out_{i}", s, F32, kind="ExternalOutput").ap() for i, s in enumerate(outs)]
    layer(nc, *args)
    r = run_bass_kernel_spmd(nc, [arrays], core_ids=[0]).results[0]
    shapes = [(1, SEQ, D), (1, DEC, D), (1, 1, WINDOW, KV, HD), (1, 1, WINDOW, KV, HD), (1, 1, SEQ, HEADS, HD),
              (1, 1, SEQ, HEADS, HD), (1, 1, SEQ, HEADS), (1, 1, WINDOW, KV, HD), (1, 1, WINDOW, KV, HD),
              (1, 1, DEC, HEADS, HD), (1, 1, DEC, HEADS, HD), (1, 1, DEC, HEADS)]
    return tuple(r[f"out_{i}"].reshape(s) for i, s in enumerate(shapes))
```
